# Optimizing a Trainium2 kernel written in Bass

```python
import math
import numpy as np
import jax
import jax.numpy as jnp
from jax import lax

D_MODEL = 1024
BATCH = 1
SEQ = 1024
DEPTH = 1

ATTN_PATTERNS = ((128, 1), (512, 4), (2048, 16))
N_GROUPS_A = 3
HEADS_PER_GROUP = 4
N_HEADS_A = N_GROUPS_A * HEADS_PER_GROUP
HEAD_DIM_A = 128
D_ATTN = N_HEADS_A * HEAD_DIM_A
D_ATTN_OUT = HEADS_PER_GROUP * HEAD_DIM_A
BLOCK_A = 128
N_HEADS_B = 8
HEAD_DIM_K = 128
HEAD_DIM_V = 128
D_KEY_B = N_HEADS_B * HEAD_DIM_K
D_VAL_B = N_HEADS_B * HEAD_DIM_V
CONV_WIDTH = 4
CHUNK = 64
N_BRANCHES = 2
D_FF = ((8 * D_MODEL // 3 + 255) // 256) * 256
EPS = 1e-6
IN_SPLITS = (D_ATTN, D_ATTN, D_ATTN, D_KEY_B, D_KEY_B, D_VAL_B, D_VAL_B, N_HEADS_B, N_HEADS_B, N_BRANCHES * D_MODEL)
D_IN = 3 * D_ATTN + 2 * D_KEY_B + 2 * D_VAL_B + 2 * N_HEADS_B + N_BRANCHES * D_MODEL

kernel_name = 'hybrid_dilated_swa_gated_deltanet'

def rmsnorm(x, w):
    xf = x.astype(jnp.float32)
    xf = xf * lax.rsqrt(jnp.mean(xf * xf, axis=-1, keepdims=True) + EPS)
    return xf.astype(x.dtype) * w

def l2norm(t):
    return t * lax.rsqrt(jnp.sum(t * t, axis=-1, keepdims=True) + EPS)

def alibi_slopes():
    return jnp.exp2(-8.0 * jnp.arange(1, N_HEADS_A + 1, dtype=jnp.float32) / N_HEADS_A)

def dilated_window_attention(q, k, v, slopes, window, dilation):
    b, s, h, dh = q.shape
    f32 = jnp.float32
    w_sub = window // dilation
    span = BLOCK_A * dilation
    s_pad = -(-s // span) * span
    nb = s_pad // span

    def to_blocks(t):
        t = jnp.pad(t, ((0, 0), (0, s_pad - s), (0, 0), (0, 0)))
        return t.reshape(b, nb, BLOCK_A, dilation, h, dh)

    qb, kb, vb = to_blocks(q), to_blocks(k), to_blocks(v)

    def with_prev(t):
        prev = jnp.pad(t[:, :-1], ((0, 0), (1, 0), (0, 0), (0, 0), (0, 0), (0, 0)))
        return jnp.concatenate([prev, t], axis=2)

    kc, vc = with_prev(kb), with_prev(vb)
    scores = jnp.einsum('bnirhd,bnjrhd->bnrhij', qb, kc).astype(f32) * (dh ** -0.5)
    i = jnp.arange(BLOCK_A)[:, None]
    j = jnp.arange(2 * BLOCK_A)[None, :]
    delta = BLOCK_A + i - j
    band = (delta >= 0) & (delta <= w_sub)
    has_prev = (jnp.arange(nb)[:, None, None] > 0) | (j >= BLOCK_A)[None]
    valid = band[None] & has_prev
    bias = -(slopes.astype(f32) * dilation)[:, None, None] * delta.astype(f32)
    scores = jnp.where(valid[None, :, None, None], scores + bias, -jnp.inf)
    m = jnp.max(scores, axis=-1, keepdims=True)
    p = jnp.exp(scores - m)
    den = jnp.sum(p, axis=-1)
    o = jnp.einsum('bnrhij,bnjrhd->bnirhd', p, vc.astype(f32))
    o = o / jnp.transpose(den, (0, 1, 4, 2, 3))[..., None]
    lse = jnp.transpose(m[..., 0] + jnp.log(den), (0, 1, 4, 2, 3))
    o = o.reshape(b, s_pad, h, dh)[:, :s]
    lse = lse.reshape(b, s_pad, h)[:, :s]
    return o, lse

def causal_depthwise_conv(x, w):
    c = x.shape[-1]
    return lax.conv_general_dilated(x, w[:, None, :].astype(x.dtype), window_strides=(1,),
                                    padding=((CONV_WIDTH - 1, 0),),
                                    dimension_numbers=('NWC', 'WIO', 'NWC'),
                                    feature_group_count=c)

def gated_delta_rule(q, k, v, g, beta):
    b, s, h, dk = q.shape
    dv = v.shape[-1]
    n = s // CHUNK

    def chunks(t):
        return jnp.moveaxis(t.reshape(b, n, CHUNK, h, -1), 3, 1)

    q, k, v = chunks(q), chunks(k), chunks(v)
    g = jnp.moveaxis(g.reshape(b, n, CHUNK, h), 3, 1)
    beta = jnp.moveaxis(beta.reshape(b, n, CHUNK, h), 3, 1)
    gc = jnp.cumsum(g, axis=-1)
    incl = jnp.tril(jnp.ones((CHUNK, CHUNK), dtype=bool))
    strict = jnp.tril(jnp.ones((CHUNK, CHUNK), dtype=bool), -1)
    decay = jnp.exp(jnp.where(incl, gc[..., :, None] - gc[..., None, :], -jnp.inf))
    kk = jnp.einsum('bhnid,bhnjd->bhnij', k, k)
    a = jnp.where(strict, beta[..., :, None] * kk * decay, 0.0)
    eye = jnp.eye(CHUNK, dtype=a.dtype)
    rhs = jnp.concatenate([beta[..., None] * v, (beta * jnp.exp(gc))[..., None] * k], axis=-1)
    sol = lax.linalg.triangular_solve(eye + a, rhs, left_side=True, lower=True, unit_diagonal=True)
    u_bar, w = sol[..., :dv], sol[..., dv:]
    qk = jnp.einsum('bhnid,bhnjd->bhnij', q, k) * decay
    q_dec = q * jnp.exp(gc)[..., None]
    k_dec = k * jnp.exp(gc[..., -1:] - gc)[..., None]
    g_last = jnp.exp(gc[..., -1])

    def step(state, xs):
        u_bar_c, w_c, qk_c, q_c, k_c, gl_c = xs
        u = u_bar_c - jnp.einsum('bhck,bhkv->bhcv', w_c, state)
        o = jnp.einsum('bhck,bhkv->bhcv', q_c, state) + jnp.einsum('bhcj,bhjv->bhcv', qk_c, u)
        state = gl_c[..., None, None] * state + jnp.einsum('bhck,bhcv->bhkv', k_c, u)
        return state, o

    xs = tuple(jnp.moveaxis(t, 2, 0) for t in (u_bar, w, qk, q_dec, k_dec, g_last))
    state0 = jnp.zeros((b, h, dk, dv), jnp.float32)
    _, o = lax.scan(step, state0, xs)
    return jnp.transpose(o, (1, 0, 3, 2, 4)).reshape(b, s, h, dv)

def setup_inputs(seed: int = 0) -> dict:
    key = jax.random.key(seed)
    ks = jax.random.split(key, 16)
    f32 = jnp.float32

    def nrm(k, shape, fan_in):
        return jax.random.normal(k, shape, f32) * (fan_in ** -0.5)

    def gain(k, shape):
        return 1.0 + 0.02 * jax.random.normal(k, shape, f32)

    x = jax.random.normal(ks[0], (BATCH, SEQ, D_MODEL), f32)
    a_log = jnp.log(jax.random.uniform(ks[4], (DEPTH, N_HEADS_B), f32, minval=1.0, maxval=16.0))
    dt = jnp.exp(jax.random.uniform(ks[5], (DEPTH, N_HEADS_B), f32, minval=math.log(1e-3), maxval=math.log(1e-1)))
    dt_bias = dt + jnp.log(-jnp.expm1(-dt))
    return {
        'x': x,
        'norm_mix': gain(ks[1], (DEPTH, D_MODEL)),
        'w_in': nrm(ks[2], (DEPTH, D_MODEL, D_IN), D_MODEL),
        'conv_w': nrm(ks[3], (DEPTH, CONV_WIDTH, 2 * D_KEY_B + D_VAL_B), CONV_WIDTH),
        'a_log': a_log,
        'dt_bias': dt_bias,
        'dn_norm': gain(ks[6], (DEPTH, HEAD_DIM_V)),
        'w_proj_attn': nrm(ks[7], (DEPTH, D_ATTN_OUT, D_MODEL), D_ATTN_OUT),
        'w_proj_delta': nrm(ks[8], (DEPTH, D_VAL_B, D_MODEL), D_VAL_B),
        'w_out': nrm(ks[9], (DEPTH, D_MODEL, D_MODEL), D_MODEL),
        'norm_ffn': gain(ks[10], (DEPTH, D_MODEL)),
        'w_gate': nrm(ks[11], (DEPTH, D_MODEL, D_FF), D_MODEL),
        'w_up': nrm(ks[12], (DEPTH, D_MODEL, D_FF), D_MODEL),
        'w_down': nrm(ks[13], (DEPTH, D_FF, D_MODEL), D_FF),
        'norm_final': gain(ks[14], (D_MODEL,)),
    }

def reference(x, norm_mix, w_in, conv_w, a_log, dt_bias, dn_norm, w_proj_attn, w_proj_delta,
              w_out, norm_ffn, w_gate, w_up, w_down, norm_final):
    b, s, _ = x.shape
    f32 = jnp.float32
    slopes = alibi_slopes()
    split_at = np.cumsum(IN_SPLITS)[:-1].tolist()
    h = x
    for layer in range(DEPTH):
        u = rmsnorm(h, norm_mix[layer])
        proj = u @ w_in[layer]
        qa, ka, va, qd, kd, vd, z, beta_raw, a_raw, gate_raw = jnp.split(proj, split_at, axis=-1)

        qa = qa.reshape(b, s, N_HEADS_A, HEAD_DIM_A)
        ka = ka.reshape(b, s, N_HEADS_A, HEAD_DIM_A)
        va = va.reshape(b, s, N_HEADS_A, HEAD_DIM_A)
        outs, lses = [], []
        for gi, (window, dilation) in enumerate(ATTN_PATTERNS):
            hs = slice(gi * HEADS_PER_GROUP, (gi + 1) * HEADS_PER_GROUP)
            o, lse = dilated_window_attention(qa[:, :, hs], ka[:, :, hs], va[:, :, hs], slopes[hs], window, dilation)
            outs.append(o)
            lses.append(lse)
        mix_w = jax.nn.softmax(jnp.stack(lses), axis=0)
        y_a = jnp.einsum('gbsh,gbshd->bshd', mix_w, jnp.stack(outs)).reshape(b, s, D_ATTN_OUT).astype(x.dtype)
        y_a = y_a @ w_proj_attn[layer]

        qkv = jax.nn.silu(causal_depthwise_conv(jnp.concatenate([qd, kd, vd], axis=-1), conv_w[layer]))
        qd, kd, vd = jnp.split(qkv, [D_KEY_B, 2 * D_KEY_B], axis=-1)
        qd = l2norm(qd.reshape(b, s, N_HEADS_B, HEAD_DIM_K).astype(f32)) * (HEAD_DIM_K ** -0.5)
        kd = l2norm(kd.reshape(b, s, N_HEADS_B, HEAD_DIM_K).astype(f32))
        vd = vd.reshape(b, s, N_HEADS_B, HEAD_DIM_V).astype(f32)
        beta = jax.nn.sigmoid(beta_raw.astype(f32))
        g = -jnp.exp(a_log[layer].astype(f32)) * jax.nn.softplus(a_raw.astype(f32) + dt_bias[layer].astype(f32))
        o_d = gated_delta_rule(qd, kd, vd, g, beta)
        o_d = rmsnorm(o_d, dn_norm[layer].astype(f32)) * jax.nn.silu(z.reshape(b, s, N_HEADS_B, HEAD_DIM_V).astype(f32))
        y_b = o_d.reshape(b, s, D_VAL_B).astype(x.dtype) @ w_proj_delta[layer]

        gate_a, gate_b = jnp.split(jax.nn.sigmoid(gate_raw), N_BRANCHES, axis=-1)
        h = h + (gate_a * y_a + gate_b * y_b) @ w_out[layer]

        hn = rmsnorm(h, norm_ffn[layer])
        h = h + (jax.nn.silu(hn @ w_gate[layer]) * (hn @ w_up[layer])) @ w_down[layer]
    return rmsnorm(h, norm_final)


_drawn_inputs = setup_inputs


def setup_inputs(seed=0):
    import zlib

    import numpy as np

    out = dict(_drawn_inputs(seed))
    spreads = {}
    factors = {'norm_mix': 4.163, 'dn_norm': 8.0, 'norm_ffn': 13.329, 'norm_final': 8.234}
    for name, (base, spread) in spreads.items():
        noise = np.random.default_rng([zlib.crc32(name.encode()), seed]).standard_normal(out[name].shape)
        drawn = base * np.exp(spread * noise) if base else spread * noise
        out[name] = jnp.asarray(drawn.astype(out[name].dtype))
    for name, factor in factors.items():
        out[name] = (out[name] * factor).astype(out[name].dtype)
    return out
```

```python
import math
from contextlib import ExitStack

import numpy as np

import concourse.bass as bass
from concourse import mybir

F32 = mybir.dt.float32
F32R = mybir.dt.float32r
I32 = mybir.dt.int32
U8 = mybir.dt.uint8
ALU = mybir.AluOpType
ACT = mybir.ActivationFunctionType
AXX = mybir.AxisListType.X
ds = bass.ds

P = 128
S = 1024
D = 1024
KT = D // P
HALF = 512
NSLOT = 4
DILATION = (1, 4, 16)
NHA = 12
NHB = 8
NCH = S // P
DFF = ((8 * D // 3 + 255) // 256) * 256
FF_CHUNKS = (8, 8, DFF // P - 16)
EPS = 1e-6
NEG = -1e30
D_ATTN = NHA * P
COL_QA, COL_KA, COL_VA = 0, D_ATTN, 2 * D_ATTN
COL_QD = 3 * D_ATTN
COL_KD, COL_VD, COL_Z = COL_QD + NHB * P, COL_QD + 2 * NHB * P, COL_QD + 3 * NHB * P
COL_BETA = COL_QD + 4 * NHB * P
COL_GATE = COL_BETA + 2 * NHB
FREE = 3
PASSES = ((0, 0), (0, 1), (1, 0))


def wait(eng, sem, value):
    if isinstance(value, int) and value <= 0:
        return
    eng.wait_ge(sem, value)


def build(nc, x, norm_mix, w_in, conv_w, a_log, dt_bias, dn_norm, w_proj_attn, w_proj_delta,
          w_out, norm_ffn, w_gate, w_up, w_down, norm_final, out):
    ctx = ExitStack()
    with ctx:
        place = [nc.sbuf_base + (-nc.sbuf_base) % 64]

        def at(name, shape, dt, offset):
            return nc.alloc_sbuf_tensor_at(name, shape, dt, offset=offset)

        passed = {}

        def wait_alone(eng, s_, value):
            if isinstance(value, int) and value <= 0:
                return
            eng.wait_ge(s_, value)
            if not isinstance(value, int):
                if eng not in passed:
                    passed[eng] = sem(f"passed{len(passed)}")
                eng.sem_inc(passed[eng], 1)

        def size_of(shape, dt):
            n = (1 if dt == U8 else 4) * int(np.prod(shape[1:]))
            return n + (-n) % 32

        def keep(name, shape, dt=F32):
            t = at(name, shape, dt, place[0])
            place[0] += size_of(shape, dt)
            return t

        def sem(name):
            return ctx.enter_context(nc.semaphore(name))

        ident = keep("ident", [P, P])
        ones = keep("ones", [P, P])
        band = keep("band", [P, 2, 256])
        band_pair = keep("band_pair", [P, P])
        neg_upper = keep("neg_upper", [P, P])
        strict_up = keep("strict_up", [P, P])
        merge_mask = keep("merge_mask", [P, 7, P], U8)
        slopes = keep("slopes", [P, NHA])
        norm_mix_c = keep("norm_mix_c", [P, KT])
        norm_ffn_c = keep("norm_ffn_c", [P, KT])
        norm_final_c = keep("norm_final_c", [P, KT])
        dn_norm_c = keep("dn_norm_c", [P, 1])
        conv_c = keep("conv_c", [P, 4, 3 * NHB])
        rate = keep("rate", [40, 4])
        per_token = keep("per_token", [P, NCH, 4, 32])

        raw, wpart = [], []
        for slot in range(2):
            raw.append(keep(f"raw{slot}", [P, KT, P]))
            wpart.append([keep(f"w_hi{slot}", [P, KT, P], F32R), keep(f"w_lo{slot}", [P, KT, P], F32R)])
        slot2 = place[0]
        raw.append(keep("raw2", [P, KT, P]))
        wpart.append([keep("w_hi2", [P, KT, P], F32R), keep("w_lo2", [P, KT, P], F32R)])
        tmp = [at(f"tmp{i}", [P, S], F32, slot2 + 4096 * i) for i in range(3)]

        act_in = [keep("u_hi", [P, KT, S], F32R), keep("u_lo", [P, KT, S], F32R)]
        work = place[0]
        v_region = [at("v_hi", [P, KT, S], F32R, work), at("v_lo", [P, KT, S], F32R, work + 32768)]
        x_rows = at("x_rows", [P, KT, D], F32, work)
        h_t = at("h_t", [P, KT, S], F32, work + 65536)
        assert work + 98304 <= nc.sbuf_usable_end, (work, nc.sbuf_usable_end)

        bank = [ctx.enter_context(nc.psum_tensor(f"bank{i}", [P, HALF], F32)) for i in range(8)]
        D0, D1, X0, X1, Y0, Y1, Z0, Z1 = range(8)

        scr_stat = nc.dram_tensor("scr_stat", [3, 2 * S], F32).ap()
        scr_rows = nc.dram_tensor("scr_rows", [3, NHB, S], F32).ap()
        scr_attn = nc.dram_tensor("scr_attn", [NSLOT * P, S], F32).ap()
        scr_delta = nc.dram_tensor("scr_delta", [NHB * P, S], F32).ap()
        scr_part = nc.dram_tensor("scr_part", [D, S], F32).ap()

        raw_loaded = [sem(f"raw_loaded{i}") for i in range(3)]
        weights_split = sem("weights_split")
        projected = sem("projected")
        phase_end = sem("phase_end")
        consts = sem("consts")
        const_step = sem("const_step")
        params = sem("params")
        conv_loaded = sem("conv_loaded")

        class Phase:
            def __init__(self, base, per, period, used):
                self.base, self.per, self.period, self.used = base, per, period, used

            def tile(self, it, i):
                return self.per * it + (self.base + i)

            def use(self, it, i):
                return (self.per // self.period) * it + (self.used + i // self.period + 1)

        order = [("attn", 9, NSLOT, 3), ("gate_a", 2, KT, 2), ("delta", 4, NHB, 2), ("gate_b", 2, KT, 2), ("out", 2, KT // 2, 2)]
        for c, n in enumerate(FF_CHUNKS):
            order += [(f"up{c}", 2, n, 2), (f"down{c}", 2, KT // 2, 2)]
        ph, base, used = {}, 0, 0
        for name, per, iters, period in order:
            ph[name] = Phase(base, per, period, used)
            base += per * iters
            used += per * iters // period

        def load_weights(sp, phase, it, i, src):
            n = phase.tile(it, i)
            wait_alone(sp, weights_split, n + (FREE - phase.period + 1))
            slot = i % phase.period
            sp.dma_start(raw[slot][:, 0:src.shape[1], :], src).then_inc(raw_loaded[slot], 16)

        def split_weights(pool, phase, it, i, kt=KT):
            n, slot = phase.tile(it, i), i % phase.period
            hi, lo = wpart[slot]
            pool.wait_ge(raw_loaded[slot], phase.use(it, i) * 16)
            wait_alone(pool, projected, n * 2 + 2 * (FREE - phase.period + 1))
            nc.gpsimd.tensor_copy(hi[:, 0:kt, :], raw[slot][:, 0:kt, :])
            pool.drain()
            nc.gpsimd.tensor_tensor(lo[:, 0:kt, :], raw[slot][:, 0:kt, :], hi[:, 0:kt, :].bitcast(F32),
                                    ALU.subtract).then_inc(weights_split, 1)

        def dense_k(pe, phase, it, i, half, k, kt, dst, rhs, free=None, closed=True):
            n, slot = phase.tile(it, i), i % phase.period
            if k == 0:
                if half == 0:
                    pe.wait_ge(weights_split, n + (FREE + 1))
                if free is not None:
                    wait(pe, *free)
            for wp, ap in PASSES:
                last = nc.tensor.matmul(bank[dst][:, :], wpart[slot][wp][:, k, :],
                                        rhs[ap][:, k, half * HALF:(half + 1) * HALF],
                                        start=k == 0 and (wp, ap) == PASSES[0],
                                        stop=closed and k == kt - 1 and (wp, ap) == PASSES[-1])
            if k == kt - 1 and closed:
                last.then_inc(projected, 1)

        def done(phase, it, i, half):
            return phase.tile(it, i) * 2 + (2 * FREE + half + 1)

        def barrier(eng, number):
            eng.drain().then_inc(phase_end, 1)
            eng.wait_ge(phase_end, 4 * number)

        def w_cols(w, col, kt=KT):
            return w.rearrange("(k p) n -> p k n", p=P)[:, 0:kt, ds(col, P)]

        def flat(t):
            return t[:, :, :].rearrange("p a b -> p (a b)")

        w_in2, conv2 = w_in[0], conv_w[0]
        cst = {}

        w_ba = at("w_ba", [P, KT, 40], F32, work + 32768)
        w_ba_part = [at("w_ba_hi", [P, KT, 40], F32R, work + 34304), at("w_ba_lo", [P, KT, 40], F32R, work + 35840)]
        iota_i = at("iota_i", [P, P], I32, work + 37376)
        u_tmp = at("u_tmp", [P, 2, HALF], F32, work + 38912)
        sq_scr = at("sq_scr", [P, D], F32, work + 43008)
        xn = at("xn", [P, 2, D], F32, work + 47104)
        rstd = at("rstd", [P, KT], F32, work + 55296)
        ssum = at("ssum", [P, KT], F32, work + 55328)
        blocks = at("blocks", [P, 8, P], F32, work + 55360)
        lvl_tmp = at("lvl_tmp", [P, P], F32, work + 59456)
        rows = at("rows", [P, S], F32, work + 59968)
        row_t = [at(f"row_t{i}", [40, S], F32, work + 64064 + 4096 * i) for i in range(5)]
        reset = at("reset", [8, S], F32, work + 84544)

        x_loaded = sem("x_loaded")
        x_sq, x_rstd, x_ln = sem("x_sq"), sem("x_rstd"), sem("x_ln")
        x_scaled = sem("x_scaled")
        x_turned = sem("x_turned")
        x_weighted, x_high, x_low = sem("x_weighted"), sem("x_high"), sem("x_low")
        ba_split, ba_done, ba_act, ba_vec, ba_turned, rows_stored = (
            sem("ba_split"), sem("ba_done"), sem("ba_act"), sem("ba_vec"), sem("ba_turned"), sem("rows_stored"))
        ba_loaded = sem("ba_loaded")
        x_load = [sem(f"x_load{i}") for i in range(KT)]

        def setup_sp(sp):
            for c in range(KT):
                sp.dma_start(x_rows[:, c, :], x[0, c * P:(c + 1) * P, :]).then_inc(x_load[c], 16)
                if c == 1:
                    for t, src in ((norm_mix_c, norm_mix[0]), (norm_ffn_c, norm_ffn[0]), (norm_final_c, norm_final)):
                        sp.dma_start(t[:, :], src.rearrange("(f p) -> p f", p=P),
                                     allow_slow_non_contiguous=True).then_inc(params, 16)
                    sp.dma_start(dn_norm_c[:, :], dn_norm[0].rearrange("(p a) -> p a", a=1),
                                 allow_slow_non_contiguous=True).then_inc(params, 16)
            sp.wait_ge(consts, 1)
            for j in range(2):
                sp.dma_start(w_ba[:, :, 32 * j:32 * j + 8],
                             w_in2.rearrange("(k p) n -> p k n", p=P)[:, :, COL_BETA + 8 * j:COL_BETA + 8 * j + 8],
                             allow_slow_non_contiguous=True).then_inc(ba_loaded, 16)
            sp.dma_start(rate[32:40, 0:1], a_log[0].rearrange("(p a) -> p a", a=1),
                         allow_slow_non_contiguous=True).then_inc(ba_loaded, 16)
            sp.dma_start(rate[32:40, 2:3], dt_bias[0].rearrange("(p a) -> p a", a=1),
                         allow_slow_non_contiguous=True).then_inc(ba_loaded, 16)
            for j in range(4):
                sp.dma_start(conv_c[:, j, :], conv2[j].rearrange("(t p) -> p t", p=P),
                             allow_slow_non_contiguous=True).then_inc(conv_loaded, 16)

        def setup_store_sp(sp):
            sp.wait_ge(ba_vec, 7)
            for j, src in enumerate((rows[0:8, :], row_t[3][0:8, :], row_t[4][0:8, :])):
                sp.dma_start(scr_rows[j], src).then_inc(rows_stored, 16)
            sp.wait_ge(rows_stored, 48)

        def setup_pool(pool):
            step = [0]

            def then(ins):
                step[0] += 1
                ins.then_inc(const_step, 1)
                pool.wait_ge(const_step, step[0])

            g = nc.gpsimd
            then(g.memset(flat(w_ba), 0.0))
            g.memset(reset[:, :], 1.0).then_inc(consts, 1)
            then(g.memset(ones[:, :], 1.0))
            then(g.memset(ident[:, :], 0.0))
            then(g.affine_select(out=ident[:, :], in_=ident[:, :], compare_op=ALU.not_equal, fill=1.0, base=0,
                                 pattern=[[-1, P]], channel_multiplier=1))
            g.memset(neg_upper[:, :], 0.0).then_inc(consts, 1)
            for c in range(KT):
                for q in range(2):
                    pool.wait_ge(x_high, 2 * c + q + 1)
                    g.tensor_tensor(act_in[1][:, 4 * q:4 * q + 4, c * P:(c + 1) * P],
                                    u_tmp[:, q, :].rearrange("p (f t) -> p f t", t=P),
                                    act_in[0][:, 4 * q:4 * q + 4, c * P:(c + 1) * P].bitcast(F32),
                                    ALU.subtract).then_inc(x_low, 1)
            then(g.iota(iota_i[:, :], pattern=[[1, P]], base=0, channel_multiplier=-1))
            then(g.tensor_copy(band[:, 1, P:256], iota_i[:, :]))
            then(g.affine_select(out=band[:, 1, P:256], in_=band[:, 1, P:256], compare_op=ALU.is_ge, fill=NEG,
                                 base=0, pattern=[[-1, P]], channel_multiplier=1))
            then(g.iota(iota_i[:, :], pattern=[[1, P]], base=-P, channel_multiplier=-1))
            then(g.tensor_copy(band[:, 1, 0:P], iota_i[:, :]))
            then(g.affine_select(out=band[:, 1, 0:P], in_=band[:, 1, 0:P], compare_op=ALU.is_ge, fill=NEG,
                                 base=0, pattern=[[1, P]], channel_multiplier=-1))
            then(g.memset(band[:, 0, 0:P], NEG))
            then(g.tensor_copy(band[:, 0, P:256], band[:, 1, P:256]))
            then(g.tensor_copy(band_pair[:, :], band[:, 1, P:256]))
            pair = band_pair[:, :].rearrange("p (b i) -> p b i", b=2)
            then(g.affine_select(out=pair, in_=pair, compare_op=ALU.is_ge, fill=NEG, base=63,
                                 pattern=[[64, 2], [0, 64]], channel_multiplier=-1))
            then(g.affine_select(out=neg_upper[:, :], in_=neg_upper[:, :], compare_op=ALU.is_ge, fill=NEG, base=0,
                                 pattern=[[1, P]], channel_multiplier=-1))
            then(g.affine_select(out=strict_up[:, :], in_=ones[:, :], compare_op=ALU.is_ge, fill=0.0, base=-1,
                                 pattern=[[1, P]], channel_multiplier=-1))
            for h in range(NHA):
                g.memset(slopes[:, h:h + 1], float(2.0 ** (-8.0 * (h + 1) / NHA)) * DILATION[h // NSLOT])
            for l in range(8):
                b = 1 << l
                v = blocks[:, l, :].rearrange("p (n b) -> p n b", b=b)
                then(g.memset(blocks[:, l, :], 1.0))
                then(g.affine_select(out=v, in_=v, compare_op=ALU.is_ge, fill=0.0, base=0,
                                     pattern=[[-b, P // b], [0, b]], channel_multiplier=1))
                then(g.affine_select(out=v, in_=v, compare_op=ALU.is_ge, fill=0.0, base=b - 1,
                                     pattern=[[b, P // b], [0, b]], channel_multiplier=-1))
            for l in range(7):
                then(g.tensor_tensor(lvl_tmp[:, :], blocks[:, l + 1, :], blocks[:, l, :], ALU.subtract))
                up = l == 0
                then(g.affine_select(out=lvl_tmp[:, :], in_=lvl_tmp[:, :], compare_op=ALU.is_ge, fill=0.0, base=0,
                                     pattern=[[1 if up else -1, P]], channel_multiplier=-1 if up else 1))
                then(g.tensor_copy(merge_mask[:, l, :], lvl_tmp[:, :]))
            pool.sem_inc(consts, 1)

        def setup_act(act):
            act.wait_ge(consts, 1)
            for c in range(KT):
                act.wait_ge(x_load[c], 16)
                nc.scalar.activation(sq_scr[:, :], x_rows[:, c, :], ACT.Square,
                                     accum_out=ssum[:, c:c + 1]).then_inc(x_sq, 1)
                act.wait_ge(x_sq, c + 1)
                nc.scalar.activation(rstd[:, c:c + 1], ssum[:, c:c + 1], ACT.Ln, scale=1.0 / D, bias=EPS)
                act.drain()
                nc.scalar.activation(rstd[:, c:c + 1], rstd[:, c:c + 1], ACT.Exp, scale=-0.5).then_inc(x_rstd, 1)
                for q in range(2):
                    act.wait_ge(x_weighted, 2 * c + q + 1)
                    nc.scalar.activation(act_in[0][:, 4 * q:4 * q + 4, c * P:(c + 1) * P],
                                         u_tmp[:, q, :].rearrange("p (f t) -> p f t", t=P),
                                         ACT.Copy).then_inc(x_high, 1)
            act.wait_ge(ba_loaded, 64)
            nc.scalar.activation(rate[32:40, 1:2], rate[32:40, 0:1], ACT.Exp).then_inc(ba_act, 1)
            act.wait_ge(ba_done, 2)
            for q in range(2):
                nc.scalar.activation(row_t[0][:, q * HALF:(q + 1) * HALF], bank[Z0 + q][0:40, :],
                                     ACT.Copy).then_inc(ba_act, 1)
            act.wait_ge(ba_vec, 1)
            nc.scalar.activation(row_t[1][0:8, :], row_t[0][0:8, :], ACT.Exp, scale=-1.0)
            nc.scalar.activation(row_t[1][32:40, :], row_t[2][32:40, :], ACT.Exp)
            act.drain()
            nc.scalar.activation(row_t[1][32:40, :], row_t[1][32:40, :], ACT.Ln, bias=1.0).then_inc(ba_act, 1)
            act.wait_ge(ba_vec, 3)
            nc.scalar.activation(row_t[3][0:8, :], rows[0:8, :], ACT.Exp)
            nc.scalar.activation(rows[96:104, :], row_t[2][0:8, :], ACT.Exp).then_inc(ba_act, 1)
            for c in range(NCH):
                act.wait_ge(ba_turned, c + 1)
                nc.scalar.activation(per_token[:, c, :, 0:8],
                                     bank[X0 + c % 2][:, 0:P].rearrange("p (k e) -> p k e", e=32)[:, :, 0:8],
                                     ACT.Copy).then_inc(ba_act, 1)

        def setup_vec(dve):
            v = nc.vector
            dve.wait_ge(params, 16 * 4)
            for c in range(KT):
                dve.wait_ge(x_rstd, c + 1)
                if c >= 2:
                    dve.wait_ge(x_turned, 2 * (c - 1))
                v.tensor_scalar(xn[:, c % 2, :], x_rows[:, c, :], rstd[:, c:c + 1], None,
                                ALU.mult).then_inc(x_scaled, 1)
                for q in range(2):
                    dve.wait_ge(x_turned, 2 * c + q + 1)
                    if c:
                        dve.wait_ge(x_low, 2 * (c - 1) + q + 1)
                    v.tensor_tensor(u_tmp[:, q, :].rearrange("p (f t) -> p f t", t=P),
                                    bank[X0 + q][:, :].rearrange("p (f t) -> p f t", t=P),
                                    norm_mix_c[:, 4 * q:4 * q + 4].unsqueeze(2).broadcast_to([P, 4, P]),
                                    ALU.mult).then_inc(x_weighted, 1)
            dve.wait_ge(ba_loaded, 64)
            dve.wait_ge(consts, 1)
            v.tensor_copy(flat(w_ba_part[0]), flat(w_ba))
            dve.drain()
            v.tensor_tensor(flat(w_ba_part[1]), flat(w_ba), flat(w_ba_part[0]).bitcast(F32),
                            ALU.subtract).then_inc(ba_split, 1)
            b8, a8 = slice(0, 8), slice(32, 40)
            dve.wait_ge(ba_act, 3)
            v.tensor_scalar(row_t[0][a8, :], row_t[0][a8, :], rate[a8, 2:3], None, ALU.add)
            v.memset(reset[:, 0:S:P], 0.0)
            dve.drain()
            v.tensor_scalar(row_t[3][a8, :], row_t[0][a8, :], -1.0, None, ALU.mult)
            dve.drain()
            v.tensor_tensor(row_t[2][a8, :], row_t[0][a8, :], row_t[3][a8, :], ALU.min).then_inc(ba_vec, 1)
            dve.wait_ge(ba_act, 4)
            v.tensor_scalar(row_t[1][b8, :], row_t[1][b8, :], 1.0, None, ALU.add)
            v.scalar_tensor_tensor(row_t[1][a8, :], row_t[0][a8, :], 0.0, row_t[1][a8, :], ALU.max, ALU.add)
            dve.drain()
            v.reciprocal(rows[32:40, :], row_t[1][b8, :])
            v.tensor_scalar(row_t[2][b8, :], row_t[1][a8, :], rate[a8, 1:2], -1.0, ALU.mult,
                            ALU.mult).then_inc(ba_vec, 1)
            dve.drain()
            v.tensor_tensor_scan(rows[0:8, :], reset[:, :], row_t[2][b8, :], 0.0, ALU.mult, ALU.add)
            v.tensor_scalar(row_t[4][b8, :], rows[32:40, :], -1.0, None, ALU.mult)
            dve.drain()
            gc3 = rows[0:8, :].rearrange("p (c t) -> p c t", t=P)
            v.tensor_tensor(row_t[2][b8, :].rearrange("p (c t) -> p c t", t=P),
                            gc3[:, :, P - 1:P].broadcast_to([8, NCH, P]), gc3, ALU.subtract).then_inc(ba_vec, 1)
            dve.wait_ge(ba_act, 5)
            v.tensor_copy(row_t[1][b8, :], rows[32:40, :])
            dve.drain()
            v.tensor_tensor(rows[64:72, :], row_t[3][b8, :], row_t[1][b8, :], ALU.mult).then_inc(ba_vec, 4)

        def setup_pe(pe):
            pe.sem_inc(projected, 2 * FREE)
            pe.wait_ge(consts, 2)
            for c in range(KT):
                pe.wait_ge(x_scaled, c + 1)
                for q in range(2):
                    if c:
                        pe.wait_ge(x_weighted, 2 * (c - 1) + q + 1)
                    for f in range(4):
                        last = nc.tensor.transpose(bank[X0 + q][:, f * P:(f + 1) * P],
                                                   xn[:, c % 2, (4 * q + f) * P:(4 * q + f + 1) * P], ident[:, :])
                    last.then_inc(x_turned, 1)
            pe.wait_ge(ba_split, 1)
            pe.wait_ge(x_low, 2 * KT)
            for q in range(2):
                for k in range(KT):
                    for wp, ap in PASSES:
                        last = nc.tensor.matmul(bank[Z0 + q][0:40, :], w_ba_part[wp][:, k, :].bitcast(F32),
                                                act_in[ap][:, k, q * HALF:(q + 1) * HALF].bitcast(F32),
                                                start=k == 0 and (wp, ap) == PASSES[0],
                                                stop=k == KT - 1 and (wp, ap) == PASSES[-1])
                last.then_inc(ba_done, 1)

        def setup_turn_pe(pe):
            pe.wait_ge(ba_vec, 7)
            for c in range(NCH):
                if c >= 2:
                    pe.wait_ge(ba_act, 5 + c - 1)
                nc.tensor.transpose(bank[X0 + c % 2][:, 0:P], rows[:, c * P:(c + 1) * P],
                                    ident[:, :]).then_inc(ba_turned, 1)

        a0 = work
        qk_t = []
        for g in range(3):
            qk_t.append((at(f"qa{g}", [P, S], F32, a0), at(f"ka{g}", [P, S], F32, a0 + 4096)))
            a0 += 8192
        va_t = at("va_t", [P, S], F32, a0)
        va = at("va", [P, KT, P], F32, a0 + 4096)
        a0 += 8192
        score, prob, prob_t = [], [], []
        for b in range(2):
            score.append(at(f"score{b}", [P, HALF], F32, a0))
            prob.append(at(f"prob{b}", [P, HALF], F32, a0 + 2048))
            prob_t.append(at(f"prob_t{b}", [P, HALF], F32, a0 + 4096))
            a0 += 6144
        o_t = [at(f"o_t{g}", [P, S], F32, a0 + 4096 * g) for g in range(3)]
        a0 += 12288
        stat_b = [at(f"stat_b{g}", [P, 2 * S], F32, a0 + 8192 * g) for g in range(3)]
        a0 += 24576
        joint = at("joint", [P, S], F32, a0)
        stat = at("stat", [P, 16], F32, a0 + 4096)
        neg_max = at("neg_max", [P, 8], F32, a0 + 4160)
        stat_t = at("stat_t", [16, P], F32, a0 + 4192)
        assert a0 + 4800 <= work + 98304

        dense_read = sem("dense_read")
        v_turned, v_copied = sem("v_turned"), sem("v_copied")
        scored, scaled, maxed, exped = sem("scored"), sem("scaled"), sem("maxed"), sem("exped")
        p_turned, p_copied = sem("p_turned"), sem("p_copied")
        o_ready, o_taken = sem("o_ready"), sem("o_taken")
        st_turned, st_copied, st_stored, st_loaded = sem("st_turned"), sem("st_copied"), sem("st_stored"), [sem(f"st_loaded{g}") for g in range(3)]
        mix_vec, mix_act, mixed_sem, y_stored = sem("mix_vec"), sem("mix_act"), sem("mixed_a"), sem("y_stored")

        PAIRS = (4, 4, 2)
        NP_SLOT = sum(PAIRS)
        FIRST_PAIR = {2: 0, 0: 0, 1: 4}

        def pair_no(s, g, p):
            return NP_SLOT * s + ((0, 4, 8)[g] + p)

        def att_steps(g):
            if g == 2:
                return ["v0", "v1", "s0", "s1", "t0", "t1", "o0", "o1", "st"]
            return ["v0", "v1", "s0", "s1", "t0", "s2", "t1", "o0", "s3", "t2", "o1", "t3", "o2", "o3", "st"]

        def block_keys(g, b):
            if g == 0:
                return (b - 1 if b else None), b
            if g == 1:
                return (b - 4 if b >= 4 else None), b
            return None, b

        def token_order(g, ap, half=None, bankwise=False):
            return ap

        def att_pe(pe, s, g, step):
            q, k = qk_t[g]
            kind, p = step[0], step[1:]
            if kind == "v":
                h = int(p)
                wait(pe, dense_read, 18 * s + (6 * g + 6))
                for i in range(4):
                    last = nc.tensor.transpose(bank[Y0 + h][:, i * P:(i + 1) * P],
                                               va_t[:, (4 * h + i) * P:(4 * h + i + 1) * P], ident[:, :])
                last.then_inc(v_turned, 1)
            elif step == "st":
                wait(pe, exped, pair_no(s, g, PAIRS[g] - 1) + 1)
                nc.tensor.transpose(bank[X0][0:16, 0:P], stat[:, :], ident[:, :]).then_inc(st_turned, 1)
            elif kind == "s":
                p = int(p)
                n = pair_no(s, g, p)
                if p >= 2:
                    wait(pe, scaled, n - 1)
                elif p == 0:
                    wait(pe, st_copied, 3 * s + g)
                for i in range(4 if g == 2 else 2):
                    b = (4 if g == 2 else 2) * p + i
                    lhs = q[:, b * P:(b + 1) * P]
                    if g == 2:
                        last = nc.tensor.matmul(bank[X0 + p % 2][:, i * P:(i + 1) * P], lhs, k[:, b * P:(b + 1) * P],
                                                start=True, stop=True)
                    else:
                        before, own = block_keys(g, b)
                        blocks_k = k[:, :].rearrange("p (b i) -> p b i", i=P)
                        if before is None:
                            rhs = blocks_k[:, own:own + 1, :].broadcast_to([P, 2, P])
                        else:
                            rhs = blocks_k[:, before:own + 1:own - before, :]
                        last = nc.tensor.matmul(bank[X0 + p % 2][:, i * 256:(i + 1) * 256].rearrange("p (a j) -> p a j", a=2),
                                                lhs, rhs, start=True, stop=True)
                last.then_inc(scored, 1)
            elif kind == "t":
                p = int(p)
                n = pair_no(s, g, p)
                wait(pe, exped, n + 1)
                wait(pe, p_copied, n - 1)
                if p < 2:
                    wait(pe, v_copied, 6 * s + (2 * g + 2))
                for i in range(4):
                    last = nc.tensor.transpose(bank[Y0 + p % 2][:, i * P:(i + 1) * P],
                                               prob[p % 2][:, i * P:(i + 1) * P], ident[:, :])
                last.then_inc(p_turned, 1)
            else:
                p = int(p)
                n = pair_no(s, g, p)
                wait(pe, p_copied, n + 1)
                ob = Z0 + (p if g == 2 else p // 2)
                if g == 2:
                    wait(pe, o_taken, 6 * s + 2 * g + (p - 1))
                elif p % 2 == 0:
                    wait(pe, o_taken, 6 * s + (2 * g + p // 2 - 1))
                for i in range(4 if g == 2 else 2):
                    b = (4 if g == 2 else 2) * p + i
                    o = bank[ob][:, (b % 4) * P:(b % 4 + 1) * P]
                    before, own = block_keys(g, b)
                    pt = prob_t[p % 2]
                    if g == 2:
                        last = nc.tensor.matmul(o, va[:, own, :], pt[:, i * P:(i + 1) * P], start=True, stop=True)
                    else:
                        if before is not None:
                            nc.tensor.matmul(o, va[:, before, :], pt[:, 2 * i * P:(2 * i + 1) * P], start=True, stop=False)
                        last = nc.tensor.matmul(o, va[:, own, :], pt[:, (2 * i + 1) * P:(2 * i + 2) * P],
                                                start=before is None, stop=True)
                last.then_inc(o_ready, 1)

        def att_act(act, s, g, step):
            kind, p = step[0], step[1:]
            if kind == "v":
                h = int(p)
                act.wait_ge(v_turned, 6 * s + (2 * g + h + 1))
                if h == 0:
                    wait(act, o_ready, pair_no(s, g, 0))
                nc.scalar.activation(va[:, 4 * h:4 * h + 4, :],
                                     bank[Y0 + h][:, :].rearrange("p (b d) -> p b d", d=P), ACT.Copy).then_inc(v_copied, 1)
            elif step == "st":
                act.wait_ge(st_copied, 3 * s + (g + 1))
                act.dma_start(scr_stat[g].rearrange("(a b) -> a b", b=P), stat_t[:, :]).then_inc(st_stored, 16)
            elif kind == "s":
                p = int(p)
                n = pair_no(s, g, p)
                act.wait_ge(maxed, n + 1)
                wait(act, p_turned, n - 1)
                m = 4 if g == 2 else 2
                w = HALF // m
                for i in range(m):
                    b = m * p + i
                    last = nc.scalar.activation(prob[p % 2][:, i * w:(i + 1) * w], score[p % 2][:, i * w:(i + 1) * w],
                                                ACT.Exp, bias=neg_max[:, b:b + 1], accum_out=stat[:, 8 + b:9 + b])
                last.then_inc(exped, 1)
            elif kind == "t":
                p = int(p)
                n = pair_no(s, g, p)
                act.wait_ge(p_turned, n + 1)
                wait(act, o_ready, n - 1)
                nc.scalar.activation(prob_t[p % 2][:, :], bank[Y0 + p % 2][:, :], ACT.Copy).then_inc(p_copied, 1)
            else:
                p = int(p)
                if g != 2 and p % 2 == 0:
                    return
                h = p if g == 2 else p // 2
                act.wait_ge(o_ready, pair_no(s, g, p) + 1)
                if h == 0:
                    wait(act, mixed_sem, s)
                src, o = bank[Z0 + h], o_t[g]
                if g == 0:
                    dst, src = o[:, h * HALF:(h + 1) * HALF], src[:, :]
                elif g == 1:
                    dst = o[:, h * HALF:(h + 1) * HALF].rearrange("p (i r) -> p r i", r=4)
                    src = src[:, :].rearrange("p (r i) -> p r i", r=4)
                else:
                    dst = o[:, :].rearrange("p (i r) -> p r i", r=16)[:, 8 * h:8 * h + 8, :]
                    src = src[:, :].rearrange("p (r i) -> p r i", r=8)
                nc.scalar.activation(dst, src, ACT.Copy).then_inc(o_taken, 1)

        def att_vec(dve, s, g, step):
            kind, p = step[0], step[1:]
            v = nc.vector
            if step == "st":
                dve.wait_ge(st_turned, 3 * s + (g + 1))
                wait(dve, st_stored, 16 * (3 * s + g))
                v.tensor_copy(stat_t[:, :], bank[X0][0:16, 0:P]).then_inc(st_copied, 1)
            elif kind == "s":
                p = int(p)
                n = pair_no(s, g, p)
                dve.wait_ge(scored, n + 1)
                wait(dve, exped, n - 1)
                if p == 0:
                    wait(dve, st_turned, 3 * s + g)
                slope = slopes[:, ds(s + 4 * g, 1)]
                if g == 2:
                    dist = band_pair[:, :].unsqueeze(1).broadcast_to([P, 4, P])
                    m, w = 4, P
                else:
                    first = block_keys(g, 2 * p)[0] is None
                    both = block_keys(g, 2 * p + 1)[0] is None
                    m, w = 2, 256
                    if first and both:
                        dist = band[:, 0:1, :].broadcast_to([P, 2, 256])
                    elif first:
                        dist = band[:, :, :]
                    else:
                        dist = band[:, 1:2, :].broadcast_to([P, 2, 256])
                sc = score[p % 2][:, :].rearrange("p (a j) -> p a j", a=m)
                v.scalar_tensor_tensor(sc, dist, slope, bank[X0 + p % 2][:, :].rearrange("p (a j) -> p a j", a=m),
                                       ALU.mult, ALU.add).then_inc(scaled, 1)
                dve.drain()
                v.reduce_max(stat[:, m * p:m * p + m], sc, AXX)
                dve.drain()
                v.tensor_scalar(neg_max[:, m * p:m * p + m], stat[:, m * p:m * p + m], -1.0, None,
                                ALU.mult).then_inc(maxed, 1)

        def token_view(g, ap):
            if g == 0:
                return ap
            if g == 1:
                return ap.rearrange("p (n r i) -> p n i r", n=2, r=4)
            return ap.rearrange("p (r i) -> p i r", r=16)

        def like(g, ap):
            if g == 0:
                return ap
            if g == 1:
                return ap.rearrange("p (n i r) -> p n i r", n=2, r=4)
            return ap.rearrange("p (i r) -> p i r", r=16)

        def mix_vec_engine(dve, s, piece):
            v = nc.vector
            mx = [stat_b[g][:, 0:S] for g in range(3)]
            den = [stat_b[g][:, S:2 * S] for g in range(3)]
            if piece == "max":
                for g in range(2):
                    dve.wait_ge(st_loaded[g], 16 * s + 16)
                wait(dve, y_stored, 16 * s)
                v.tensor_tensor(like(1, joint[:, :]), like(1, mx[0]), token_view(1, mx[1]), ALU.max)
                dve.drain()
                dve.wait_ge(st_loaded[2], 16 * s + 16)
                v.tensor_tensor(like(2, joint[:, :]), like(2, joint[:, :]), token_view(2, mx[2]), ALU.max)
                dve.drain()
            elif piece[:3] == "sub":
                g = int(piece[3])
                v.tensor_tensor(token_view(g, mx[g]), token_view(g, mx[g]), like(g, joint[:, :]),
                                ALU.subtract).then_inc(mix_vec, 1)
            elif piece[:3] == "mul":
                g = int(piece[3])
                dve.wait_ge(o_taken, 6 * s + 6)
                dve.wait_ge(mix_act, 3 * s + (g + 1))
                v.tensor_tensor(den[g], den[g], mx[g], ALU.mult)
                v.tensor_tensor(like(g, o_t[g][:, :]), like(g, o_t[g][:, :]), token_view(g, mx[g]), ALU.mult)
                dve.drain()
            elif piece[:3] == "add":
                g = int(piece[3])
                first = den[0] if g == 1 else joint[:, :]
                v.tensor_tensor(like(g, joint[:, :]), like(g, first), token_view(g, den[g]), ALU.add)
                v.tensor_tensor(o_t[0][:, :], o_t[0][:, :], o_t[g][:, :], ALU.add)
                dve.drain()
            elif piece[:3] == "rec":
                q = slice(256 * int(piece[3]), 256 * int(piece[3]) + 256)
                v.reciprocal(joint[:, q], joint[:, q])
                dve.drain()
            elif piece == "end":
                v.tensor_tensor(joint[:, :], o_t[0][:, :], joint[:, :], ALU.mult).then_inc(mixed_sem, 1)

        def mix_act_engine(act, s, piece):
            if piece == "load":
                for g in range(3):
                    act.wait_ge(st_stored, 16 * (3 * s + 3))
                    act.dma_start(stat_b[g][:, :], scr_stat[g].partition_broadcast(P)).then_inc(st_loaded[g], 16)
            elif piece[:3] == "sub":
                g = int(piece[3])
                act.wait_ge(mix_vec, 3 * s + (g + 1))
                nc.scalar.activation(stat_b[g][:, 0:S], stat_b[g][:, 0:S], ACT.Exp).then_inc(mix_act, 1)
            elif piece == "end":
                act.wait_ge(mixed_sem, s + 1)
                act.dma_start(scr_attn[ds(s * P, P), :], joint[:, :]).then_inc(y_stored, 16)

        MIX = {0: {32: ["load"], 38: ["max"], 41: ["sub0", "sub1"], 44: ["sub2"], 47: ["mul0"]},
               1: {1: ["mul1"], 4: ["mul2"], 6: ["add1"], 9: ["add2"], 12: ["rec0"], 14: ["rec1"], 19: ["rec2"],
                   21: ["rec3"], 23: ["end"]}}

        def mix_pieces(eng, mix, s, g, j):
            for piece in MIX.get(g, {}).get(j, ()):
                mix(eng, s, piece)

        def dense_att_pe(pe, s, g, j):
            i, half, k = j // 16, j // 8 % 2, j % 8
            m = 9 * s + (3 * g + i)
            dense_k(pe, ph["attn"], s, 3 * g + i, half, k, KT, D0 + half, act_in,
                    (dense_read, m * 2 + (half - 1)))

        def dense_att_act(act, s, g, j):
            if j % 8 != 7:
                return
            i, half = j // 16, j // 8 % 2
            act.wait_ge(projected, done(ph["attn"], s, 3 * g + i, half))
            t = (*qk_t[g], va_t)[i]
            src = bank[D0 + half]
            if i == 2 and half == 0:
                wait(act, v_turned, 6 * s + 2 * g)
            if g == 0:
                dst, src = t[:, half * HALF:(half + 1) * HALF], src[:, :]
            elif g == 1:
                dst = t[:, half * HALF:(half + 1) * HALF].rearrange("p (r i) -> p r i", r=4)
                src = src[:, :].rearrange("p (i r) -> p r i", r=4)
            else:
                dst = t[:, :].rearrange("p (r i) -> p r i", r=16)[:, :, 32 * half:32 * half + 32]
                src = src[:, :].rearrange("p (i r) -> p r i", r=16)
            nc.scalar.activation(dst, src, ACT.Copy, scale=float(P) ** -0.5 if i == 0 else 1.0).then_inc(dense_read, 1)

        def segment(eng, s, g, dense, side, side_s, mix=None):
            before = (g + 2) % 3
            steps = att_steps(before) if side is not None else []
            for j in range(48):
                if dense is not None:
                    dense(eng, s, g, j)
                if j % 3 == 2 and j // 3 < len(steps):
                    side(eng, side_s, before, steps[j // 3])
                if mix is not None:
                    mix_pieces(eng, mix, s - 1, g, j)

        def nothing(*_):
            pass

        def attention(eng, dense, side, mix):
            segment(eng, 0, 0, dense, None, 0)
            segment(eng, 0, 1, dense, side, 0)
            segment(eng, 0, 2, dense, side, 0)
            with eng.Fori(1, NSLOT) as s:
                segment(eng, s, 0, dense, side, s - 1, mix)
                segment(eng, s, 1, dense, side, s, mix)
                segment(eng, s, 2, dense, side, s)
            segment(eng, NSLOT, 0, None, side, NSLOT - 1, mix)
            segment(eng, NSLOT, 1, None, None, 0, mix)

        def attention_sp(sp):
            with sp.Fori(0, NSLOT) as s:
                for i in range(9):
                    first = (COL_QA, COL_KA, COL_VA)[i % 3] + NSLOT * P * (i // 3)
                    load_weights(sp, ph["attn"], s, i, w_cols(w_in2, s * P + first))
            sp.wait_ge(y_stored, 16 * NSLOT)

        class Gates:
            def __init__(self, name, number, kt, scr, gate_col, w_proj):
                self.phase, self.number, self.kt, self.scr = ph[name], number, kt, scr
                self.gate_col, self.w_proj, self.second = gate_col, w_proj, name == "gate_b"
                self.loaded, self.high, self.low = sem(f"{name}_loaded"), sem(f"{name}_high"), sem(f"{name}_low")
                self.sigmoid, self.product = sem(f"{name}_sigmoid"), sem(f"{name}_product")
                self.stored, self.part, self.merged = sem(f"{name}_stored"), sem(f"{name}_part"), sem(f"{name}_merged")

        def gates_sp(sp, G):
            sp.wait_ge(phase_end, 4 * G.number)
            sp.dma_start(h_t[:, 0:G.kt, :], G.scr.rearrange("(k p) t -> p k t", p=P)).then_inc(G.loaded, 16)

            def step(f):
                load_weights(sp, G.phase, f, 0, w_cols(w_in2, f * P + G.gate_col))
                load_weights(sp, G.phase, f, 1, w_cols(G.w_proj, f * P, G.kt))

            with sp.Fori(0, KT) as f:
                step(f)
            if not G.second:
                sp.wait_ge(G.stored, 16 * KT)
            sp.sem_inc(phase_end, 1)

        def gates_pool(pool, G):
            with pool.Fori(0, KT) as f:
                split_weights(pool, G.phase, f, 0)
                split_weights(pool, G.phase, f, 1, G.kt)

        def gates_pe(pe, G):
            def step(f):
                for half in range(2):
                    for k in range(KT):
                        dense_k(pe, G.phase, f, 0, half, k, KT, D0 + half, act_in, (G.sigmoid, f * 2 + (half - 1)))
                for half in range(2):
                    for k in range(G.kt):
                        if isinstance(f, int) and half == 0:
                            pe.wait_ge(G.low, k + 1)
                        dense_k(pe, G.phase, f, 1, half, k, G.kt, Y0 + half, v_region,
                                (G.product, f * 2 + (half - 1)))

            step(0)
            with pe.Fori(1, KT) as f:
                step(f)

        def gates_act(act, G):
            act.wait_ge(G.loaded, 16)
            for k in range(G.kt):
                nc.scalar.activation(v_region[0][:, k, :], h_t[:, k, :], ACT.Copy).then_inc(G.high, 1)

            def step(f):
                for half in range(2):
                    act.wait_ge(projected, done(G.phase, f, 0, half))
                    wait(act, G.product, f * 2 + (half - 1))
                    nc.scalar.activation(tmp[0][:, half * HALF:(half + 1) * HALF], bank[D0 + half][:, :],
                                         ACT.Sigmoid).then_inc(G.sigmoid, 1)
                if G.second:
                    wait(act, G.merged, f)
                    act.dma_start(tmp[2][:, :], scr_part[ds(f * P, P), :]).then_inc(G.part, 16)

            def store(f):
                act.wait_ge(G.product, f * 2 + 2)
                act.dma_start(scr_part[ds(f * P, P), :], tmp[1][:, :]).then_inc(G.stored, 16)

            step(0)
            if not G.second:
                store(0)
            with act.Fori(1, KT) as f:
                step(f)
                if not G.second:
                    store(f)

        def gates_vec(dve, G):
            v = nc.vector
            dve.wait_ge(G.loaded, 16)
            for k in range(G.kt):
                dve.wait_ge(G.high, k + 1)
                v.tensor_tensor(v_region[1][:, k, :], h_t[:, k, :], v_region[0][:, k, :].bitcast(F32),
                                ALU.subtract).then_inc(G.low, 1)
            if G.second:
                dve.drain()

            def step(f):
                for half in range(2):
                    c = slice(half * HALF, (half + 1) * HALF)
                    dve.wait_ge(G.sigmoid, f * 2 + (half + 1))
                    dve.wait_ge(projected, done(G.phase, f, 1, half))
                    if not G.second and half == 0:
                        wait(dve, G.stored, f * 16)
                    v.tensor_tensor(tmp[1][:, c], tmp[0][:, c], bank[Y0 + half][:, :], ALU.mult).then_inc(G.product, 1)
                if G.second:
                    dve.drain()
                    dve.wait_ge(G.part, f * 16 + 16)
                    v.tensor_tensor(h_t[:, ds(f, 1), :].rearrange("p a t -> p (a t)"), tmp[1][:, :], tmp[2][:, :],
                                    ALU.add).then_inc(G.merged, 1)
                    dve.drain()

            step(0)
            with dve.Fori(1, KT) as f:
                step(f)

        gates_a = Gates("gate_a", 2, NSLOT, scr_attn, COL_GATE, w_proj_attn[0])
        gates_b = Gates("gate_b", 4, NHB, scr_delta, COL_GATE + D, w_proj_delta[0])

        d0 = [work]

        def dt_(name, shape):
            t = at(name, shape, F32, d0[0])
            d0[0] += size_of(shape, F32)
            return t

        conv_in = [dt_(f"conv_in{i}", [P, 3 + S + 5]) for i in range(2)]
        conv_out = dt_("conv_out", [P, S])
        qkv = [dt_(f"qkv{i}", [P, S]) for i in range(3)]
        z_next, z_now = dt_("z_next", [P, S]), dt_("z_now", [P, S])
        sq = [dt_(f"sq{i}", [P, S]) for i in range(2)]
        qn, kn = dt_("qn", [P, S]), dt_("kn", [P, S])
        row = [dt_(f"row{i}", [P, S]) for i in range(3)]
        decay, neg_a = row[0], row[2]
        inv, inv_t, half_way = dt_("inv", [P, S]), dt_("inv_t", [P, S]), dt_("half_way", [P, S])
        beta_v, beta_k, k_dec = dt_("beta_v", [P, S]), dt_("beta_k", [P, S]), dt_("k_dec", [P, S])
        col = dt_("col", [P, NCH, 4])
        decay_all = dt_("decay_all", [P, NCH])
        state, u_now = dt_("state", [P, P]), dt_("u_now", [P, P])
        assert d0[0] <= work + 98304, d0[0] - work
        u_bar, w_t = inv, half_way
        o_raw, o_sq = beta_v, beta_k

        dl = {x_: sem("dl_" + x_) for x_ in (
            "read", "conv", "silu", "sq", "ss", "ln", "normed", "vt", "bv", "kt", "kdec", "kk", "qk", "rows",
            "diff", "dec", "a", "pt", "t0t", "t0", "t0c", "y", "yc", "dt", "dtm", "tt", "ttc", "ub", "ubc", "wt", "wtc",
            "qdec", "ws", "u", "o", "s", "sup", "z", "os", "osq", "oss", "oln", "out", "stored", "zero")}

        def c4(t, half):
            return t[:, half * HALF:(half + 1) * HALF].rearrange("p (c t) -> p c t", t=P)

        def chunk(t, c):
            return t[:, c * P:(c + 1) * P]

        def delta_steps():
            steps = ["sq", "ss", "vt0", "vt1", "kt0", "kt1", "kk0", "kk1", "qk0", "qk1", "t00", "t01"]
            for level in range(1, 7):
                steps += [f"{x_}{level}{h_}" for x_ in ("y", "d", "t") for h_ in range(2)]
            steps += ["ub0", "ub1", "wt0", "wt1"]
            steps += [f"c{c}" for c in range(NCH)]
            steps += ["on", "end"]
            return steps

        DSTEPS = delta_steps()

        def delta_pe(pe, h, step):
            mm, tr = nc.tensor.matmul, nc.tensor.transpose
            two = h * 2
            if step == "ss":
                wait(pe, dl["sup"], h * NCH)
                wait(pe, dl["osq"], two)
                for i in range(2):
                    pe.wait_ge(dl["sq"], two + (i + 1))
                    for half in range(2):
                        last = mm(bank[(X0, Y0)[i] + half][:, :], ones[:, :], sq[i][:, half * HALF:(half + 1) * HALF],
                                  start=True, stop=True)
                    last.then_inc(dl["ss"], 1)
            elif step[:2] == "vt":
                half = int(step[2])
                pe.wait_ge(dl["silu"], h * 3 + 3)
                wait(pe, dl["oln"], two)
                for c in range(4 * half, 4 * half + 4):
                    last = tr(bank[Z0 + half][:, (c % 4) * P:(c % 4 + 1) * P], chunk(qkv[2], c), ident[:, :])
                last.then_inc(dl["vt"], 1)
            elif step[:2] == "kt":
                half = int(step[2])
                pe.wait_ge(dl["normed"], two + 2)
                for c in range(4 * half, 4 * half + 4):
                    last = tr(bank[X0 + half][:, (c % 4) * P:(c % 4 + 1) * P], chunk(kn, c), ident[:, :])
                last.then_inc(dl["kt"], 1)
            elif step[:2] == "kk":
                half = int(step[2])
                for c in range(4 * half, 4 * half + 4):
                    last = mm(bank[Y0 + half][:, (c % 4) * P:(c % 4 + 1) * P], chunk(kn, c), chunk(kn, c), start=True, stop=True)
                last.then_inc(dl["kk"], 1)
            elif step[:2] == "qk":
                half = int(step[2])
                pe.wait_ge(dl["bv"], two + (half + 1))
                for c in range(4 * half, 4 * half + 4):
                    last = mm(bank[Z0 + half][:, (c % 4) * P:(c % 4 + 1) * P], chunk(kn, c), chunk(qn, c), start=True, stop=True)
                last.then_inc(dl["qk"], 1)
            elif step[:2] == "t0":
                half = int(step[2])
                pe.wait_ge(dl["t0t"], h + 1)
                pe.wait_ge(dl["kdec"], two + (half + 1))
                for c in range(4 * half, 4 * half + 4):
                    last = tr(bank[X0 + half][:, (c % 4) * P:(c % 4 + 1) * P], chunk(inv_t, c), ident[:, :])
                last.then_inc(dl["t0"], 1)
            elif step[0] in "ydt" and step[1] in "123456":
                level, half = int(step[1]), int(step[2])
                n = h * 12 + (2 * (level - 1) + half)
                if step[0] == "y":
                    if level == 1:
                        pe.wait_ge(dl["t0c"], two + (half + 1))
                        pe.wait_ge(dl["a"], two + 2)
                    for c in range(4 * half, 4 * half + 4):
                        last = mm(bank[Y0 + half][:, (c % 4) * P:(c % 4 + 1) * P], chunk(neg_a, c), chunk(inv, c),
                                  start=True, stop=True)
                    last.then_inc(dl["y"], 1)
                elif step[0] == "d":
                    pe.wait_ge(dl["yc"], n + 1)
                    if level > 1:
                        pe.wait_ge(dl["ttc"], n - 1)
                    else:
                        pe.wait_ge(dl["pt"], two + (half + 1))
                    for c in range(4 * half, 4 * half + 4):
                        last = mm(bank[Z0 + half][:, (c % 4) * P:(c % 4 + 1) * P], chunk(inv_t, c), chunk(half_way, c),
                                  start=True, stop=True)
                    last.then_inc(dl["dt"], 1)
                else:
                    pe.wait_ge(dl["dtm"], n + 1)
                    for c in range(4 * half, 4 * half + 4):
                        last = tr(bank[X0 + half][:, (c % 4) * P:(c % 4 + 1) * P], chunk(inv, c), ident[:, :])
                    last.then_inc(dl["tt"], 1)
            elif step[:2] == "ub":
                half = int(step[2])
                pe.wait_ge(dl["ttc"], h * 12 + (11 + half))
                for c in range(4 * half, 4 * half + 4):
                    last = mm(bank[Y0 + half][:, (c % 4) * P:(c % 4 + 1) * P], chunk(inv_t, c), chunk(beta_v, c),
                              start=True, stop=True)
                last.then_inc(dl["ub"], 1)
            elif step[:2] == "wt":
                half = int(step[2])
                for c in range(4 * half, 4 * half + 4):
                    last = mm(bank[Z0 + half][:, (c % 4) * P:(c % 4 + 1) * P], chunk(beta_k, c), chunk(inv_t, c),
                              start=True, stop=True)
                last.then_inc(dl["wt"], 1)
            elif step[0] == "c":
                c = int(step[1])
                n = h * NCH + c
                if c == 0:
                    pe.wait_ge(dl["ubc"], two + 2)
                    pe.wait_ge(dl["wtc"], two + 2)
                    pe.wait_ge(dl["qdec"], h + 1)
                    pe.wait_ge(dl["zero"], h + 1)
                else:
                    pe.wait_ge(dl["sup"], n)
                mm(bank[X0][:, 0:P], chunk(w_t, c), state[:, :], start=True, stop=True).then_inc(dl["ws"], 1)
                o = bank[Y0 + c // 4][:, (c % 4) * P:(c % 4 + 1) * P]
                mm(o, state[:, :], chunk(row[1], c), start=True, stop=False)
                pe.wait_ge(dl["u"], n + 1)
                mm(bank[X1][:, 0:P], chunk(k_dec, c), u_now[:, :], start=True, stop=True).then_inc(dl["s"], 1)
                mm(o, u_now[:, :], chunk(decay, c), start=False, stop=True).then_inc(dl["o"], 1)
            elif step == "on":
                for half in range(2):
                    pe.wait_ge(dl["osq"], two + (half + 1))
                    mm(bank[Z0 + half][:, :], ones[:, :], o_sq[:, half * HALF:(half + 1) * HALF],
                       start=True, stop=True).then_inc(dl["oss"], 1)

        def delta_act(act, h, step):
            f = nc.scalar.activation
            two = h * 2
            if step == "sq":
                for i in range(2):
                    act.wait_ge(dl["silu"], h * 3 + (i + 1))
                    wait(act, dl["normed"], two)
                    f(sq[i][:, :], qkv[i][:, :], ACT.Square).then_inc(dl["sq"], 1)
                wait(act, dl["stored"], h * 16)
                act.wait_ge(dl["read"], h * 8 + 8)
                f(z_now[:, :], z_next[:, :], ACT.Copy).then_inc(dl["z"], 1)
            elif step == "ss":
                for i in range(2):
                    act.wait_ge(dl["ss"], two + (i + 1))
                    for half in range(2):
                        f(sq[i][:, half * HALF:(half + 1) * HALF], bank[(X0, Y0)[i] + half][:, :], ACT.Ln, bias=EPS)
                    act.drain()
                    f(sq[i][:, :], sq[i][:, :], ACT.Exp, scale=-0.5).then_inc(dl["ln"], 1)
                act.wait_ge(dl["diff"], h + 1)
                f(decay[:, :], decay[:, :], ACT.Exp).then_inc(dl["dec"], 1)
            elif step[:2] == "t0":
                half = int(step[2])
                act.wait_ge(dl["t0"], two + (half + 1))
                f(c4(inv, half), bank[X0 + half][:, :].rearrange("p (c t) -> p c t", t=P), ACT.Copy).then_inc(dl["t0c"], 1)
            elif step[0] in "yt" and step[1] in "123456":
                level, half = int(step[1]), int(step[2])
                n = h * 12 + (2 * (level - 1) + half)
                if step[0] == "y":
                    act.wait_ge(dl["y"], n + 1)
                    f(half_way[:, half * HALF:(half + 1) * HALF], bank[Y0 + half][:, :], ACT.Copy).then_inc(dl["yc"], 1)
                else:
                    act.wait_ge(dl["tt"], n + 1)
                    f(inv_t[:, half * HALF:(half + 1) * HALF], bank[X0 + half][:, :], ACT.Copy).then_inc(dl["ttc"], 1)
            elif step[:2] == "ub":
                half = int(step[2])
                act.wait_ge(dl["ub"], two + (half + 1))
                f(u_bar[:, half * HALF:(half + 1) * HALF], bank[Y0 + half][:, :], ACT.Copy).then_inc(dl["ubc"], 1)
            elif step[0] == "c" and step[1] in "37":
                half = int(step[1]) // 4
                act.wait_ge(dl["o"], h * NCH + (4 * half + 4))
                f(o_raw[:, half * HALF:(half + 1) * HALF], bank[Y0 + half][:, :], ACT.Copy)
                f(o_sq[:, half * HALF:(half + 1) * HALF], bank[Y0 + half][:, :], ACT.Square).then_inc(dl["osq"], 1)
            elif step == "on":
                for half in range(2):
                    act.wait_ge(dl["oss"], two + (half + 1))
                    f(o_sq[:, half * HALF:(half + 1) * HALF], bank[Z0 + half][:, :], ACT.Ln, scale=1.0 / P, bias=EPS)
                    act.drain()
                    f(o_sq[:, half * HALF:(half + 1) * HALF], o_sq[:, half * HALF:(half + 1) * HALF], ACT.Exp,
                      scale=-0.5).then_inc(dl["oln"], 1)
            elif step == "end":
                act.wait_ge(dl["out"], h + 1)
                act.dma_start(scr_delta[ds(h * P, P), :], z_now[:, :]).then_inc(dl["stored"], 16)
                if not isinstance(h, int):
                    load_rows(act, h + 1)

        def delta_vec(dve, h, step):
            v = nc.vector
            two = h * 2

            def b4(kind, half):
                return col[:, 4 * half:4 * half + 4, kind:kind + 1].broadcast_to([P, 4, P])

            if step == "sq":
                v.tensor_copy(col[:, :, :], per_token[:, :, :, ds(h, 1)].rearrange("p c k a -> p c (k a)"))
                dve.wait_ge(dl["rows"], h * 48 + 48)
                v.tensor_copy(decay_all[:, :], row[1][:, P - 1:S:P])
                dve.drain()
                c8 = decay[:, :].rearrange("p (c t) -> p c t", t=P)
                v.tensor_tensor(c8, c8, col[:, :, 0:1].broadcast_to([P, NCH, P]), ALU.subtract)
                dve.drain()
                v.scalar_tensor_tensor(c8, c8, 0.0, neg_upper[:, :].unsqueeze(1).broadcast_to([P, NCH, P]),
                                       ALU.min, ALU.add).then_inc(dl["diff"], 1)
            elif step == "ss":
                dve.wait_ge(dl["ln"], two + 1)
                v.scalar_tensor_tensor(qn[:, :], qkv[0][:, :], float(P) ** -0.5, sq[0][:, :], ALU.mult,
                                       ALU.mult).then_inc(dl["normed"], 1)
                dve.wait_ge(dl["ln"], two + 2)
                v.tensor_tensor(kn[:, :], qkv[1][:, :], sq[1][:, :], ALU.mult).then_inc(dl["normed"], 1)
                dve.wait_ge(dl["dec"], h + 1)
                v.tensor_tensor(neg_a[:, :], neg_a[:, :], decay[:, :], ALU.mult)
                dve.drain()
                a8 = neg_a[:, :].rearrange("p (c t) -> p c t", t=P)
                v.tensor_tensor(a8, a8, strict_up[:, :].unsqueeze(1).broadcast_to([P, NCH, P]), ALU.mult)
                v.tensor_tensor(row[1][:, :], row[1][:, :], qn[:, :], ALU.mult).then_inc(dl["qdec"], 1)
                wait(dve, dl["s"], h * NCH)
                v.memset(state[:, :], 0.0).then_inc(dl["zero"], 1)
                v.tensor_copy(inv_t[:, :].rearrange("p (c t) -> p c t", t=P),
                              ident[:, :].unsqueeze(1).broadcast_to([P, NCH, P]))
                dve.drain()
            elif step[:2] == "vt":
                half = int(step[2])
                dve.wait_ge(dl["vt"], two + (half + 1))
                if half == 0:
                    wait(dve, dl["out"], h)
                v.tensor_tensor(c4(beta_v, half), bank[Z0 + half][:, :].rearrange("p (c t) -> p c t", t=P),
                                b4(1, half), ALU.mult).then_inc(dl["bv"], 1)
            elif step[:2] == "kt":
                half = int(step[2])
                dve.wait_ge(dl["kt"], two + (half + 1))
                src = bank[X0 + half][:, :].rearrange("p (c t) -> p c t", t=P)
                v.tensor_tensor(c4(beta_k, half), src, b4(2, half), ALU.mult)
                v.tensor_tensor(c4(k_dec, half), src, b4(3, half), ALU.mult).then_inc(dl["kdec"], 1)
            elif step[:2] == "kk":
                half = int(step[2])
                hs = slice(half * HALF, (half + 1) * HALF)
                dve.wait_ge(dl["kk"], two + (half + 1))
                v.tensor_tensor(neg_a[:, hs], bank[Y0 + half][:, :], neg_a[:, hs], ALU.mult).then_inc(dl["a"], 1)
            elif step[:2] == "qk":
                half = int(step[2])
                hs = slice(half * HALF, (half + 1) * HALF)
                dve.wait_ge(dl["qk"], two + (half + 1))
                v.tensor_tensor(decay[:, hs], bank[Z0 + half][:, :], decay[:, hs], ALU.mult).then_inc(dl["pt"], 1)
                if half == 0:
                    dve.drain()
                    v.copy_predicated(inv_t[:, :].rearrange("p (c t) -> p c t", t=P),
                                      merge_mask[:, 0:1, :].broadcast_to([P, NCH, P]),
                                      neg_a[:, :].rearrange("p (c t) -> p c t", t=P)).then_inc(dl["t0t"], 1)
            elif step[0] == "d" and step[1] in "123456":
                level, half = int(step[1]), int(step[2])
                n = h * 12 + (2 * (level - 1) + half)
                wait_alone(dve, dl["dt"], n + 1)
                v.copy_predicated(c4(inv, half), merge_mask[:, level:level + 1, :].broadcast_to([P, 4, P]),
                                  bank[Z0 + half][:, :].rearrange("p (c t) -> p c t", t=P)).then_inc(dl["dtm"], 1)
            elif step[:2] == "wt":
                half = int(step[2])
                dve.wait_ge(dl["wt"], two + (half + 1))
                v.tensor_copy(w_t[:, half * HALF:(half + 1) * HALF], bank[Z0 + half][:, :]).then_inc(dl["wtc"], 1)
            elif step[0] == "c":
                c = int(step[1])
                n = h * NCH + c
                dve.wait_ge(dl["ws"], n + 1)
                if c == 0:
                    dve.wait_ge(dl["ubc"], two + 2)
                v.tensor_tensor(u_now[:, :], chunk(u_bar, c), bank[X0][:, 0:P], ALU.subtract).then_inc(dl["u"], 1)
                dve.wait_ge(dl["s"], n + 1)
                v.scalar_tensor_tensor(state[:, :], state[:, :], decay_all[:, c:c + 1], bank[X1][:, 0:P],
                                       ALU.mult, ALU.add).then_inc(dl["sup"], 1)
            elif step == "on":
                for half in range(2):
                    hs = slice(half * HALF, (half + 1) * HALF)
                    dve.wait_ge(dl["oln"], two + (half + 1))
                    v.scalar_tensor_tensor(o_raw[:, hs], o_raw[:, hs], dn_norm_c[:, 0:1], o_sq[:, hs], ALU.mult, ALU.mult)
                dve.drain()
                dve.wait_ge(dl["z"], h + 1)
                v.tensor_tensor(z_now[:, :], o_raw[:, :], z_now[:, :], ALU.mult).then_inc(dl["out"], 1)

        def dense_delta_pe(pe, h, j):
            i, half, k = j // 16, j // 8 % 2, j % 8
            m = 4 * h + i
            dense_k(pe, ph["delta"], h, i, half, k, KT, D0 + half, act_in, (dl["read"], m * 2 + (half - 1)))

        def dense_delta_act(act, h, j):
            if j % 8 != 7:
                return
            i, half = j // 16, j // 8 % 2
            f = nc.scalar.activation
            act.wait_ge(projected, done(ph["delta"], h, i, half))
            if i == 3:
                if half == 0:
                    wait(act, dl["z"], h)
                f(z_next[:, half * HALF:(half + 1) * HALF], bank[D0 + half][:, :], ACT.Silu).then_inc(dl["read"], 1)
                return
            if half == 0:
                wait(act, dl["conv"], h * 3 + (i - 1))
            f(conv_in[i % 2][:, 3 + half * HALF:3 + (half + 1) * HALF], bank[D0 + half][:, :],
              ACT.Copy).then_inc(dl["read"], 1)

        def silu_delta_act(act, h, i):
            act.wait_ge(dl["conv"], h * 3 + (i + 1))
            if i < 2:
                wait(act, dl["normed"], h * 2 - 2 + (i + 1) if isinstance(h, int) else h * 2 + (i - 1))
            else:
                wait(act, dl["vt"], h * 2)
            nc.scalar.activation(qkv[i][:, :], conv_out[:, :], ACT.Silu).then_inc(dl["silu"], 1)

        def conv_vec(dve, h, i):
            v = nc.vector
            dve.wait_ge(dl["read"], h * 8 + (2 * i + 2))
            wait(dve, dl["silu"], h * 3 + i)
            tile_ = i * NHB
            for j in range(4):
                tap = conv_c[:, j, ds(h + tile_, 1)]
                if j == 0:
                    v.tensor_scalar(conv_out[:, :], conv_in[i % 2][:, 0:S], tap, None, ALU.mult)
                else:
                    last = v.scalar_tensor_tensor(conv_out[:, :], conv_in[i % 2][:, j:j + S], tap, conv_out[:, :],
                                                  ALU.mult, ALU.add)
                if j < 3:
                    dve.drain()
            last.then_inc(dl["conv"], 1)

        def delta_slots():
            at_ = {}
            weight = [1.0 if s_[0] != "c" else 2.2 for s_ in DSTEPS]
            total, run = sum(weight), 0.0
            for s_, w_ in zip(DSTEPS, weight):
                run += w_
                at_.setdefault(min(63, int(run / total * 64)), []).append(s_)
            return at_

        SLOTS = delta_slots()

        def delta_iteration(eng, h, dense, conv, silu, side, side_h):
            for j in range(64):
                if h is not None:
                    dense(eng, h, j)
                    if j % 16 == 15 and j < 48:
                        conv(eng, h, j // 16)
                        silu(eng, h, j // 16)
                if side_h is not None:
                    for s_ in SLOTS.get(j, ()):
                        side(eng, side_h, s_)

        def delta(eng, dense, conv, silu, side):
            delta_iteration(eng, 0, dense, conv, silu, side, None)
            with eng.Fori(1, NHB) as h:
                delta_iteration(eng, h, dense, conv, silu, side, h - 1)
            delta_iteration(eng, None, dense, conv, silu, side, NHB - 1)

        def load_rows(act, h):
            wait(act, dl["o"], h * NCH)
            for j in range(3):
                src = scr_rows[j][ds(h, 1), :] if not isinstance(h, int) else scr_rows[j][h:h + 1, :]
                act.dma_start(row[j][:, :], src.rearrange("a t -> (a t)").partition_broadcast(P)).then_inc(dl["rows"], 16)

        def delta_sp(sp):
            with sp.Fori(0, NHB) as h:
                for i, c in enumerate((COL_QD, COL_KD, COL_VD, COL_Z)):
                    load_weights(sp, ph["delta"], h, i, w_cols(w_in2, h * P + c))
            sp.wait_ge(dl["stored"], 16 * NHB)
            sp.sem_inc(phase_end, 1)

        x_tile = [at(f"x_tile{i}", [P, KT, P], F32, work + 4096 * i) for i in range(2)]
        sq_sum = at("sq_sum", [P, S], F32, work + 8192)
        sq_now = at("sq_now", [P, S], F32, work + 12288)
        rms = at("rms", [P, S], F32, work + 16384)
        scaled_h = [at(f"scaled_h{i}", [P, S], F32, work + 20480 + 4096 * i) for i in range(2)]
        o_high, o_low, x_here = sem("o_high"), sem("o_low"), [sem(f"x_here{i}") for i in range(2)]
        h_squared, h_summed = sem("h_squared"), sem("h_summed")
        n_sum, n_rms, n_scaled, n_high, n_low = sem("n_sum"), sem("n_rms"), sem("n_scaled"), sem("n_high"), sem("n_low")
        OB = ((D0, D1), (Y0, Y1))

        def out_sp(sp):
            sp.wait_ge(phase_end, 4 * 5)

            def step(it):
                for i in range(2):
                    f = it * 2 + i
                    load_weights(sp, ph["out"], it, i, w_cols(w_out[0], f * P))
                    wait(sp, projected, ph["out"].tile(it, i) * 2 + (2 * FREE - 2) if not (isinstance(it, int) and it == 0) else 0)
                    sp.dma_start(x_tile[i][:, :, :], x[0].rearrange("(c p) n -> p c n", p=P)[:, :, ds(f * P, P)]).then_inc(x_here[i], 16)

            step(0)
            with sp.Fori(1, KT // 2) as it:
                step(it)
            sp.sem_inc(phase_end, 1)

        def out_pe(pe):
            def step(it):
                for i in range(2):
                    for half in range(2):
                        for k in range(KT):
                            if isinstance(it, int) and i == 0 and half == 0:
                                pe.wait_ge(o_low, k + 1)
                            dense_k(pe, ph["out"], it, i, half, k, KT, OB[i][half], act_in,
                                    (h_squared, it * 4 + (half + 2 * i - 3)), closed=False)
                        if half == 0:
                            pe.wait_ge(x_here[i], it * 16 + 16)
                        for c in range(4):
                            last = nc.tensor.matmul(bank[OB[i][half]][:, c * P:(c + 1) * P], x_tile[i][:, 4 * half + c, :],
                                                    ident[:, :], start=False, stop=c == 3)
                        last.then_inc(projected, 1)

            step(0)
            with pe.Fori(1, KT // 2) as it:
                step(it)

        def out_act(act):
            for k in range(KT):
                nc.scalar.activation(act_in[0][:, k, :], h_t[:, k, :], ACT.Copy).then_inc(o_high, 1)

            def step(it):
                for i in range(2):
                    for half in range(2):
                        act.wait_ge(projected, done(ph["out"], it, i, half))
                        if isinstance(it, int) and i == 0 and half == 0:
                            act.wait_ge(o_low, KT)
                        hs = slice(half * HALF, (half + 1) * HALF)
                        b = bank[OB[i][half]]
                        nc.scalar.activation(h_t[:, ds(it * 2 + i, 1), hs].rearrange("p a t -> p (a t)"), b[:, :], ACT.Copy)
                        wait(act, h_summed, it * 4 + (half + 2 * i - 1))
                        nc.scalar.activation(sq_now[:, hs], b[:, :], ACT.Square).then_inc(h_squared, 1)

            step(0)
            with act.Fori(1, KT // 2) as it:
                step(it)

        def out_vec(dve):
            v = nc.vector
            v.memset(sq_sum[:, :], 0.0)
            for k in range(KT):
                dve.wait_ge(o_high, k + 1)
                v.tensor_tensor(act_in[1][:, k, :], h_t[:, k, :], act_in[0][:, k, :].bitcast(F32),
                                ALU.subtract).then_inc(o_low, 1)

            with dve.Fori(0, KT // 2) as it:
                for i in range(2):
                    for half in range(2):
                        hs = slice(half * HALF, (half + 1) * HALF)
                        dve.wait_ge(h_squared, it * 4 + (half + 2 * i + 1))
                        v.tensor_tensor(sq_sum[:, hs], sq_sum[:, hs], sq_now[:, hs], ALU.add).then_inc(h_summed, 1)
                        dve.drain()

        def norm_pe(pe, count):
            pe.wait_ge(h_summed, count)
            for half in range(2):
                last = nc.tensor.matmul(bank[X0 + half][:, :], ones[:, :], sq_sum[:, half * HALF:(half + 1) * HALF],
                                        start=True, stop=True)
            last.then_inc(n_sum, 1)

        def norm_act(act, number):
            act.wait_ge(n_sum, number)
            for half in range(2):
                nc.scalar.activation(rms[:, half * HALF:(half + 1) * HALF], bank[X0 + half][:, :], ACT.Ln,
                                     scale=1.0 / D, bias=EPS)
            act.drain()
            nc.scalar.activation(rms[:, :], rms[:, :], ACT.Exp, scale=-0.5).then_inc(n_rms, 1)

        def norm_split_act(act):
            for k in range(KT):
                act.wait_ge(n_scaled, k + 1)
                nc.scalar.activation(act_in[0][:, k, :], scaled_h[k % 2][:, :], ACT.Copy).then_inc(n_high, 1)

        def norm_split_vec(dve):
            v = nc.vector
            dve.wait_ge(n_rms, 1)
            for k in range(KT + 1):
                if k < KT:
                    v.scalar_tensor_tensor(scaled_h[k % 2][:, :], h_t[:, k, :], norm_ffn_c[:, k:k + 1], rms[:, :],
                                           ALU.mult, ALU.mult).then_inc(n_scaled, 1)
                if k:
                    dve.wait_ge(n_high, k)
                    v.tensor_tensor(act_in[1][:, k - 1, :], scaled_h[(k - 1) % 2][:, :],
                                    act_in[0][:, k - 1, :].bitcast(F32), ALU.subtract).then_inc(n_low, 1)
                    dve.drain()

        ff = {x_: sem("ff_" + x_) for x_ in ("silu", "mult", "high", "low", "added")}
        FF_BEFORE = [0]
        for n_ in FF_CHUNKS:
            FF_BEFORE.append(FF_BEFORE[-1] + n_)

        def ffn_sp(sp):
            for c, n in enumerate(FF_CHUNKS):
                with sp.Fori(0, n) as j:
                    for i, w in enumerate((w_gate[0], w_up[0])):
                        load_weights(sp, ph[f"up{c}"], j, i, w_cols(w, (j + FF_BEFORE[c]) * P))
                with sp.Fori(0, KT // 2) as it:
                    for i in range(2):
                        rows_ = w_down[0][FF_BEFORE[c] * P:FF_BEFORE[c + 1] * P, :]
                        load_weights(sp, ph[f"down{c}"], it, i, w_cols(rows_, (it * 2 + i) * P, n))

        def ffn_pool(pool):
            for c, n in enumerate(FF_CHUNKS):
                with pool.Fori(0, n) as j:
                    split_weights(pool, ph[f"up{c}"], j, 0)
                    split_weights(pool, ph[f"up{c}"], j, 1)
                with pool.Fori(0, KT // 2) as it:
                    split_weights(pool, ph[f"down{c}"], it, 0, n)
                    split_weights(pool, ph[f"down{c}"], it, 1, n)

        def ffn_pe(pe):
            for c, n in enumerate(FF_CHUNKS):
                b = FF_BEFORE[c]

                def up(j):
                    for half in range(2):
                        for k in range(KT):
                            if c == 0 and isinstance(j, int) and half == 0:
                                pe.wait_ge(n_low, k + 1)
                            free = (ff["silu"], (j + b) * 2 + (half - 1))
                            if isinstance(j, int) and j == 0 and c:
                                wait(pe, ff["added"], 16 * c)
                            dense_k(pe, ph[f"up{c}"], j, 0, half, k, KT, D0 + half, act_in, free)
                    for half in range(2):
                        for k in range(KT):
                            dense_k(pe, ph[f"up{c}"], j, 1, half, k, KT, Y0 + half, act_in,
                                    (ff["mult"], (j + b) * 2 + (half - 1)))

                up(0)
                with pe.Fori(1, n) as j:
                    up(j)

                def down(it):
                    for i in range(2):
                        for half in range(2):
                            for k in range(n):
                                if isinstance(it, int) and i == 0 and half == 0:
                                    pe.wait_ge(ff["low"], (b + k + 1) * 2)
                                m = 16 * c + it * 4
                                free = (ff["added"], it * 4 + (16 * c + half + 2 * i - 3)) if not (isinstance(it, int) and it == 0) \
                                    else (ff["mult"], (b + n) * 2)
                                dense_k(pe, ph[f"down{c}"], it, i, half, k, n, OB[i][half], v_region, free)

                down(0)
                with pe.Fori(1, KT // 2) as it:
                    down(it)

        def ffn_act(act):
            def up(b, c, j):
                for half in range(2):
                    hs = slice(half * HALF, (half + 1) * HALF)
                    m = (j + b) * 2 + half
                    act.wait_ge(projected, done(ph[f"up{c}"], j, 0, half))
                    wait(act, ff["mult"], m - 1)
                    nc.scalar.activation(tmp[0][:, hs], bank[D0 + half][:, :], ACT.Silu).then_inc(ff["silu"], 1)
                if c and isinstance(j, int) and j == 0:
                    act.wait_ge(projected, done(ph[f"down{c - 1}"], KT // 2 - 1, 1, 1))
                for half in range(2):
                    hs = slice(half * HALF, (half + 1) * HALF)
                    m = (j + b) * 2 + half
                    act.wait_ge(ff["mult"], m + 1)
                    nc.scalar.activation(v_region[0][:, ds(j, 1), hs].rearrange("p a t -> p (a t)"), tmp[1][:, hs],
                                         ACT.Copy).then_inc(ff["high"], 1)

            for c, n in enumerate(FF_CHUNKS):
                up(FF_BEFORE[c], c, 0)
                with act.Fori(1, n) as j:
                    up(FF_BEFORE[c], c, j)

        def ffn_vec(dve):
            v = nc.vector

            def up(b, c, j):
                for half in range(2):
                    hs = slice(half * HALF, (half + 1) * HALF)
                    m = (j + b) * 2 + half
                    dve.wait_ge(ff["silu"], m + 1)
                    dve.wait_ge(projected, done(ph[f"up{c}"], j, 1, half))
                    wait(dve, ff["high"], m - 1)
                    v.tensor_tensor(tmp[1][:, hs], tmp[0][:, hs], bank[Y0 + half][:, :], ALU.mult).then_inc(ff["mult"], 1)
                for half in range(2):
                    hs = slice(half * HALF, (half + 1) * HALF)
                    m = (j + b) * 2 + half
                    dve.wait_ge(ff["high"], m + 1)
                    v.tensor_tensor(v_region[1][:, ds(j, 1), hs].rearrange("p a t -> p (a t)"), tmp[1][:, hs],
                                    v_region[0][:, ds(j, 1), hs].rearrange("p a t -> p (a t)").bitcast(F32),
                                    ALU.subtract).then_inc(ff["low"], 1)
                dve.drain()

            def down(c, it):
                for i in range(2):
                    for half in range(2):
                        dve.wait_ge(projected, done(ph[f"down{c}"], it, i, half))
                        hf = h_t[:, ds(it * 2 + i, 1), half * HALF:(half + 1) * HALF].rearrange("p a t -> p (a t)")
                        v.tensor_tensor(hf, hf, bank[OB[i][half]][:, :], ALU.add).then_inc(ff["added"], 1)

            for c, n in enumerate(FF_CHUNKS):
                up(FF_BEFORE[c], c, 0)
                with dve.Fori(1, n) as j:
                    up(FF_BEFORE[c], c, j)
                with dve.Fori(0, KT // 2) as it:
                    down(c, it)

        out_rows = [at(f"out_rows{i}", [P, D], F32, work + 28672 + 4096 * i) for i in range(2)]
        f_sq, f_scaled, f_turned, f_copied, f_stored = sem("f_sq"), sem("f_scaled"), sem("f_turned"), sem("f_copied"), [sem(f"f_stored{i}") for i in range(2)]

        def final_act(act):
            for k in range(KT):
                if k == 0:
                    act.wait_ge(ff["added"], 16 * len(FF_CHUNKS))
                wait(act, h_summed, 4 * KT // 2 + k)
                nc.scalar.activation(sq_now[:, :], h_t[:, k, :], ACT.Square).then_inc(f_sq, 1)
            norm_act(act, 2)
            for c in range(KT):
                act.wait_ge(f_turned, 2 * c + 1)
                if c >= 2:
                    act.wait_ge(f_stored[c % 2], 16 * (c // 2))
                nc.scalar.activation(out_rows[c % 2][:, 0:HALF], bank[D0][:, :], ACT.Copy).then_inc(f_copied, 1)

        f_copied_v = sem("f_copied_v")

        def final_vec(dve):
            v = nc.vector
            dve.drain()
            v.memset(sq_sum[:, :], 0.0)
            dve.drain()
            for k in range(KT):
                dve.wait_ge(f_sq, k + 1)
                v.tensor_tensor(sq_sum[:, :], sq_sum[:, :], sq_now[:, :], ALU.add).then_inc(h_summed, 1)
                dve.drain()
            dve.wait_ge(n_rms, 2)
            for k in range(KT):
                v.scalar_tensor_tensor(h_t[:, k, :], h_t[:, k, :], norm_final_c[:, k:k + 1], rms[:, :],
                                       ALU.mult, ALU.mult).then_inc(f_scaled, 1)
            for c in range(KT):
                dve.wait_ge(f_turned, 2 * c + 2)
                if c >= 2:
                    dve.wait_ge(f_stored[c % 2], 16 * (c // 2))
                v.tensor_copy(out_rows[c % 2][:, HALF:D], bank[D1][:, :]).then_inc(f_copied_v, 1)

        def final_pe(pe):
            norm_pe(pe, 4 * KT // 2 + KT)
            for c in range(KT):
                for half in range(2):
                    if c == 0:
                        pe.wait_ge(f_scaled, 4 * half + 4)
                    else:
                        pe.wait_ge((f_copied, f_copied_v)[half], c)
                    for f in range(4):
                        last = nc.tensor.transpose(bank[D0 + half][:, f * P:(f + 1) * P],
                                                   h_t[:, 4 * half + f, c * P:(c + 1) * P], ident[:, :])
                    last.then_inc(f_turned, 1)

        def final_sp(sp):
            for c in range(KT):
                sp.wait_ge(f_copied, c + 1)
                sp.wait_ge(f_copied_v, c + 1)
                sp.dma_start(out[0, c * P:(c + 1) * P, :], out_rows[c % 2][:, :]).then_inc(f_stored[c % 2], 16)
            for i in range(2):
                sp.wait_ge(f_stored[i], 16 * (KT // 2))

        block = ctx.enter_context(nc.Block())

        @block.sync
        def _(sp):
            setup_sp(sp)
            setup_store_sp(sp)
            sp.sem_inc(phase_end, 1)
            attention_sp(sp)
            sp.sem_inc(phase_end, 1)
            gates_sp(sp, gates_a)
            delta_sp(sp)
            gates_sp(sp, gates_b)
            out_sp(sp)
            ffn_sp(sp)
            final_sp(sp)

        @block.gpsimd
        def _(pool):
            pool.sem_inc(weights_split, FREE)
            setup_pool(pool)
            with pool.Fori(0, NSLOT) as s:
                for i in range(9):
                    split_weights(pool, ph["attn"], s, i)
            gates_pool(pool, gates_a)
            with pool.Fori(0, NHB) as h:
                for i in range(4):
                    split_weights(pool, ph["delta"], h, i)
            gates_pool(pool, gates_b)
            with pool.Fori(0, KT // 2) as it:
                for i in range(2):
                    split_weights(pool, ph["out"], it, i)
            ffn_pool(pool)

        @block.tensor
        def _(pe):
            setup_pe(pe)
            setup_turn_pe(pe)
            barrier(pe, 1)
            attention(pe, dense_att_pe, att_pe, nothing)
            barrier(pe, 2)
            gates_pe(pe, gates_a)
            barrier(pe, 3)
            delta(pe, dense_delta_pe, nothing, nothing, delta_pe)
            barrier(pe, 4)
            gates_pe(pe, gates_b)
            barrier(pe, 5)
            out_pe(pe)
            norm_pe(pe, 4 * KT // 2)
            ffn_pe(pe)
            final_pe(pe)

        @block.scalar
        def _(act):
            setup_act(act)
            barrier(act, 1)
            attention(act, dense_att_act, att_act, mix_act_engine)
            barrier(act, 2)
            gates_act(act, gates_a)
            barrier(act, 3)
            load_rows(act, 0)
            delta(act, dense_delta_act, nothing, silu_delta_act, delta_act)
            barrier(act, 4)
            gates_act(act, gates_b)
            barrier(act, 5)
            out_act(act)
            norm_act(act, 1)
            norm_split_act(act)
            ffn_act(act)
            final_act(act)

        @block.vector
        def _(dve):
            setup_vec(dve)
            dve.wait_ge(consts, 3)
            barrier(dve, 1)
            attention(dve, nothing, att_vec, mix_vec_engine)
            barrier(dve, 2)
            gates_vec(dve, gates_a)
            barrier(dve, 3)
            dve.wait_ge(conv_loaded, 64)
            for i in range(2):
                nc.vector.memset(conv_in[i][:, 0:3], 0.0)
            dve.drain()
            delta(dve, nothing, conv_vec, nothing, delta_vec)
            barrier(dve, 4)
            gates_vec(dve, gates_b)
            barrier(dve, 5)
            out_vec(dve)
            norm_split_vec(dve)
            ffn_vec(dve)
            final_vec(dve)


INS = ["x", "norm_mix", "w_in", "conv_w", "a_log", "dt_bias", "dn_norm", "w_proj_attn", "w_proj_delta",
       "w_out", "norm_ffn", "w_gate", "w_up", "w_down", "norm_final"]


def kernel(**inputs):
    import concourse.bacc as bacc
    from concourse.bass_utils import run_bass_kernel_spmd

    nc = bacc.Bacc("TRN2", target_bir_lowering=False, num_devices=1)
    arrays, args = {}, []
    for name in INS:
        a = np.ascontiguousarray(inputs[name])
        arrays[f"in_{name}"] = a
        args.append(nc.dram_tensor(f"in_{name}", a.shape, mybir.dt.from_np(a.dtype), kind="ExternalInput").ap())
    out = nc.dram_tensor("out", (1, S, D), F32, kind="ExternalOutput").ap()
    build(nc, *args, out)
    r = run_bass_kernel_spmd(nc, [arrays], core_ids=[0])
    return r.results[0]["out"]
```

```python
import math
from contextlib import ExitStack

import numpy as np

import concourse.bass as bass
from concourse import mybir

F32 = mybir.dt.float32
F32R = mybir.dt.float32r
I32 = mybir.dt.int32
U8 = mybir.dt.uint8
ALU = mybir.AluOpType
ACT = mybir.ActivationFunctionType
AXX = mybir.AxisListType.X
ds = bass.ds

P = 128
S = 1024
D = 1024
KT = D // P
HALF = 512
NSLOT = 4
DILATION = (1, 4, 16)
NHA = 12
NHB = 8
NCH = S // P
DFF = ((8 * D // 3 + 255) // 256) * 256
FF_CHUNKS = (8, 8, DFF // P - 16)
EPS = 1e-6
NEG = -1e30
D_ATTN = NHA * P
COL_QA, COL_KA, COL_VA = 0, D_ATTN, 2 * D_ATTN
COL_QD = 3 * D_ATTN
COL_KD, COL_VD, COL_Z = COL_QD + NHB * P, COL_QD + 2 * NHB * P, COL_QD + 3 * NHB * P
COL_BETA = COL_QD + 4 * NHB * P
COL_GATE = COL_BETA + 2 * NHB
FREE = 3
PASSES = ((0, 0), (0, 1), (1, 0))


def wait(eng, sem, value):
    if isinstance(value, int) and value <= 0:
        return
    eng.wait_ge(sem, value)


def build(nc, x, norm_mix, w_in, conv_w, a_log, dt_bias, dn_norm, w_proj_attn, w_proj_delta,
          w_out, norm_ffn, w_gate, w_up, w_down, norm_final, out):
    ctx = ExitStack()
    with ctx:
        place = [nc.sbuf_base + (-nc.sbuf_base) % 64]

        def at(name, shape, dt, offset):
            return nc.alloc_sbuf_tensor_at(name, shape, dt, offset=offset)

        passed = {}

        def wait_alone(eng, s_, value):
            if isinstance(value, int) and value <= 0:
                return
            eng.wait_ge(s_, value)
            if not isinstance(value, int):
                if eng not in passed:
                    passed[eng] = sem(f"passed{len(passed)}")
                eng.sem_inc(passed[eng], 1)

        def size_of(shape, dt):
            n = (1 if dt == U8 else 4) * int(np.prod(shape[1:]))
            return n + (-n) % 32

        def keep(name, shape, dt=F32):
            t = at(name, shape, dt, place[0])
            place[0] += size_of(shape, dt)
            return t

        def sem(name):
            return ctx.enter_context(nc.semaphore(name))

        ident = keep("ident", [P, P])
        ones = keep("ones", [P, P])
        band = keep("band", [P, 2, 256])
        band_pair = keep("band_pair", [P, P])
        neg_upper = keep("neg_upper", [P, P])
        strict_up = keep("strict_up", [P, P])
        merge_mask = keep("merge_mask", [P, 7, P], U8)
        slopes = keep("slopes", [P, NHA])
        norm_mix_c = keep("norm_mix_c", [P, KT])
        norm_ffn_c = keep("norm_ffn_c", [P, KT])
        norm_final_c = keep("norm_final_c", [P, KT])
        dn_norm_c = keep("dn_norm_c", [P, 1])
        conv_c = keep("conv_c", [P, 4, 3 * NHB])
        rate = keep("rate", [40, 4])
        per_token = keep("per_token", [P, NCH, 4, 32])

        raw, wpart = [], []
        for slot in range(2):
            raw.append(keep(f"raw{slot}", [P, KT, P]))
            wpart.append([keep(f"w_hi{slot}", [P, KT, P], F32R), keep(f"w_lo{slot}", [P, KT, P], F32R)])
        slot2 = place[0]
        raw.append(keep("raw2", [P, KT, P]))
        wpart.append([keep("w_hi2", [P, KT, P], F32R), keep("w_lo2", [P, KT, P], F32R)])
        tmp = [at(f"tmp{i}", [P, S], F32, slot2 + 4096 * i) for i in range(3)]

        act_in = [keep("u_hi", [P, KT, S], F32R), keep("u_lo", [P, KT, S], F32R)]
        work = place[0]
        v_region = [at("v_hi", [P, KT, S], F32R, work), at("v_lo", [P, KT, S], F32R, work + 32768)]
        NB = NSLOT + NHB
        branch = [at("b_hi", [P, NB, S], F32R, work), at("b_lo", [P, NB, S], F32R, work + 49152)]
        x_rows = at("x_rows", [P, KT, D], F32, work)
        h_t = at("h_t", [P, KT, S], F32, work + 65536)
        assert work + 98304 <= nc.sbuf_usable_end, (work, nc.sbuf_usable_end)

        bank = [ctx.enter_context(nc.psum_tensor(f"bank{i}", [P, HALF], F32)) for i in range(8)]
        D0, D1, X0, X1, Y0, Y1, Z0, Z1 = range(8)

        scr_stat = nc.dram_tensor("scr_stat", [3, 2 * S], F32).ap()
        scr_rows = nc.dram_tensor("scr_rows", [3, NHB, S], F32).ap()
        scr_branch = nc.dram_tensor("scr_branch", [(NSLOT + NHB) * P, S], F32).ap()
        scr_gate = nc.dram_tensor("scr_gate", [2 * D, S], F32).ap()

        raw_loaded = [sem(f"raw_loaded{i}") for i in range(3)]
        weights_split = sem("weights_split")
        projected = sem("projected")
        phase_end = sem("phase_end")
        consts = sem("consts")
        const_step = sem("const_step")
        params = sem("params")
        conv_loaded = sem("conv_loaded")

        class Phase:
            def __init__(self, base, per, period, used):
                self.base, self.per, self.period, self.used = base, per, period, used

            def tile(self, it, i):
                return self.per * it + (self.base + i)

            def use(self, it, i):
                return (self.per // self.period) * it + (self.used + i // self.period + 1)

        order = [("attn", 9, NSLOT, 3), ("delta", 4, NHB, 2), ("gates", 2, KT, 2), ("merge", 2, KT, 2), ("out", 2, KT // 2, 2)]
        for c, n in enumerate(FF_CHUNKS):
            order += [(f"up{c}", 2, n, 2), (f"down{c}", 2, KT // 2, 2)]
        ph, base, used = {}, 0, 0
        for name, per, iters, period in order:
            ph[name] = Phase(base, per, period, used)
            base += per * iters
            used += per * iters // period

        def load_weights(sp, phase, it, i, src):
            n = phase.tile(it, i)
            wait_alone(sp, weights_split, n + (FREE - phase.period + 1))
            slot = i % phase.period
            sp.dma_start(raw[slot][:, 0:src.shape[1], :], src).then_inc(raw_loaded[slot], 16)

        def split_weights(pool, phase, it, i, kt=KT):
            n, slot = phase.tile(it, i), i % phase.period
            hi, lo = wpart[slot]
            pool.wait_ge(raw_loaded[slot], phase.use(it, i) * 16)
            wait_alone(pool, projected, n * 2 + 2 * (FREE - phase.period + 1))
            nc.gpsimd.tensor_copy(hi[:, 0:kt, :], raw[slot][:, 0:kt, :])
            pool.drain()
            nc.gpsimd.tensor_tensor(lo[:, 0:kt, :], raw[slot][:, 0:kt, :], hi[:, 0:kt, :].bitcast(F32),
                                    ALU.subtract).then_inc(weights_split, 1)

        def dense_k(pe, phase, it, i, half, k, kt, dst, rhs, free=None, closed=True):
            n, slot = phase.tile(it, i), i % phase.period
            if k == 0:
                if half == 0:
                    pe.wait_ge(weights_split, n + (FREE + 1))
                if free is not None:
                    wait(pe, *free)
            for wp, ap in PASSES:
                last = nc.tensor.matmul(bank[dst][:, :], wpart[slot][wp][:, k, :],
                                        rhs[ap][:, k, half * HALF:(half + 1) * HALF],
                                        start=k == 0 and (wp, ap) == PASSES[0],
                                        stop=closed and k == kt - 1 and (wp, ap) == PASSES[-1])
            if k == kt - 1 and closed:
                last.then_inc(projected, 1)

        def done(phase, it, i, half):
            return phase.tile(it, i) * 2 + (2 * FREE + half + 1)

        def barrier(eng, number):
            eng.drain().then_inc(phase_end, 1)
            eng.wait_ge(phase_end, 3 * number)

        def w_cols(w, col, kt=KT):
            return w.rearrange("(k p) n -> p k n", p=P)[:, 0:kt, ds(col, P)]

        def flat(t):
            return t[:, :, :].rearrange("p a b -> p (a b)")

        w_in2, conv2 = w_in[0], conv_w[0]
        cst = {}

        late = work + 57344
        rows = at("rows", [P, S], F32, late)
        row_t = [at(f"row_t{i}", [40, S], F32, late + 4096 + 4096 * i) for i in range(5)]
        reset = at("reset", [8, S], F32, late + 24576)
        w_ba = at("w_ba", [P, KT, P], F32, late - 12288)
        w_ba_part = [at("w_ba_hi", [P, KT, P], F32R, late - 8192), at("w_ba_lo", [P, KT, P], F32R, late - 4096)]
        blocks = at("blocks", [P, 8, P], F32, work + 92160)
        lvl_tmp = at("lvl_tmp", [P, P], F32, work + 91136)
        iota_i = at("iota_i", [P, P], I32, work + 91648)
        u_tmp = at("u_tmp", [P, 2, HALF], F32, work + 32768)
        xn = at("xn", [P, 2, D], F32, work + 36864)
        sq_scr = at("sq_scr", [P, D], F32, work + 86016)
        rstd = at("rstd", [P, KT], F32, work + 90112)
        ssum = at("ssum", [P, KT], F32, work + 90144)

        x_sq, x_rstd = sem("x_sq"), sem("x_rstd")
        x_scaled = sem("x_scaled")
        x_turned = sem("x_turned")
        x_weighted, x_high, x_low = sem("x_weighted"), sem("x_high"), sem("x_low")
        ba_split, ba_done, ba_act, ba_vec, ba_turned, rows_stored = (
            sem("ba_split"), sem("ba_done"), sem("ba_act"), sem("ba_vec"), sem("ba_turned"), sem("rows_stored"))
        ba_loaded, rate_loaded = sem("ba_loaded"), sem("rate_loaded")
        x_load = [sem(f"x_load{i}") for i in range(KT)]

        def setup_sp(sp):
            sp.dma_start(x_rows[:, 0, :], x[0, 0:P, :]).then_inc(x_load[0], 16)
            sp.wait_ge(consts, 1)
            for j in range(2):
                sp.dma_start(w_ba[:, :, 32 * j:32 * j + 8],
                             w_in2.rearrange("(k p) n -> p k n", p=P)[:, :, COL_BETA + 8 * j:COL_BETA + 8 * j + 8],
                             allow_slow_non_contiguous=True).then_inc(ba_loaded, 16)
            for t, src in ((norm_mix_c, norm_mix[0]), (norm_ffn_c, norm_ffn[0]), (norm_final_c, norm_final)):
                sp.dma_start(t[:, :], src.rearrange("(f p) -> p f", p=P),
                             allow_slow_non_contiguous=True).then_inc(params, 16)
            sp.dma_start(dn_norm_c[:, :], dn_norm[0].rearrange("(p a) -> p a", a=1),
                         allow_slow_non_contiguous=True).then_inc(params, 16)
            for c in range(1, KT):
                sp.dma_start(x_rows[:, c, :], x[0, c * P:(c + 1) * P, :]).then_inc(x_load[c], 16)
            sp.dma_start(rate[32:40, 0:1], a_log[0].rearrange("(p a) -> p a", a=1),
                         allow_slow_non_contiguous=True).then_inc(rate_loaded, 16)
            sp.dma_start(rate[32:40, 2:3], dt_bias[0].rearrange("(p a) -> p a", a=1),
                         allow_slow_non_contiguous=True).then_inc(rate_loaded, 16)
            for j in range(4):
                sp.dma_start(conv_c[:, j, :], conv2[j].rearrange("(t p) -> p t", p=P),
                             allow_slow_non_contiguous=True).then_inc(conv_loaded, 16)

        def pool_then(pool):
            step = []

            def then(ins):
                step.append(1)
                ins.then_inc(const_step, 1)
                pool.wait_ge(const_step, len(step))
            return then

        def setup_pool(pool, then):
            g = nc.gpsimd
            then(g.memset(flat(w_ba), 0.0))
            g.memset(reset[:, :], 1.0).then_inc(consts, 1)
            then(g.memset(ones[:, :], 1.0))
            then(g.memset(ident[:, :], 0.0))
            then(g.affine_select(out=ident[:, :], in_=ident[:, :], compare_op=ALU.not_equal, fill=1.0, base=0,
                                 pattern=[[-1, P]], channel_multiplier=1))
            g.memset(neg_upper[:, :], 0.0).then_inc(consts, 1)
            then(g.iota(iota_i[:, :], pattern=[[1, P]], base=0, channel_multiplier=-1))
            then(g.tensor_copy(band[:, 1, P:256], iota_i[:, :]))
            then(g.affine_select(out=band[:, 1, P:256], in_=band[:, 1, P:256], compare_op=ALU.is_ge, fill=NEG,
                                 base=0, pattern=[[-1, P]], channel_multiplier=1))
            then(g.iota(iota_i[:, :], pattern=[[1, P]], base=-P, channel_multiplier=-1))
            then(g.tensor_copy(band[:, 1, 0:P], iota_i[:, :]))
            then(g.affine_select(out=band[:, 1, 0:P], in_=band[:, 1, 0:P], compare_op=ALU.is_ge, fill=NEG,
                                 base=0, pattern=[[1, P]], channel_multiplier=-1))
            then(g.memset(band[:, 0, 0:P], NEG))
            then(g.tensor_copy(band[:, 0, P:256], band[:, 1, P:256]))
            then(g.tensor_copy(band_pair[:, :], band[:, 1, P:256]))
            pair = band_pair[:, :].rearrange("p (b i) -> p b i", b=2)
            then(g.affine_select(out=pair, in_=pair, compare_op=ALU.is_ge, fill=NEG, base=63,
                                 pattern=[[64, 2], [0, 64]], channel_multiplier=-1))
            for h in range(NHA):
                g.memset(slopes[:, h:h + 1], float(2.0 ** (-8.0 * (h + 1) / NHA)) * DILATION[h // NSLOT])
            pool.drain().then_inc(consts, 1)
            for c in range(KT):
                for q in range(2):
                    pool.wait_ge(x_high, 2 * c + q + 1)
                    g.tensor_tensor(act_in[1][:, 4 * q:4 * q + 4, c * P:(c + 1) * P],
                                    u_tmp[:, q, :].rearrange("p (f t) -> p f t", t=P),
                                    act_in[0][:, 4 * q:4 * q + 4, c * P:(c + 1) * P].bitcast(F32),
                                    ALU.subtract).then_inc(x_low, 1)

        def mask_pool(pool, then):
            g = nc.gpsimd
            then(g.affine_select(out=neg_upper[:, :], in_=neg_upper[:, :], compare_op=ALU.is_ge, fill=NEG, base=0,
                                 pattern=[[1, P]], channel_multiplier=-1))
            then(g.affine_select(out=strict_up[:, :], in_=ones[:, :], compare_op=ALU.is_ge, fill=0.0, base=-1,
                                 pattern=[[1, P]], channel_multiplier=-1))
            for l in range(8):
                b = 1 << l
                v = blocks[:, l, :].rearrange("p (n b) -> p n b", b=b)
                then(g.memset(blocks[:, l, :], 1.0))
                then(g.affine_select(out=v, in_=v, compare_op=ALU.is_ge, fill=0.0, base=0,
                                     pattern=[[-b, P // b], [0, b]], channel_multiplier=1))
                then(g.affine_select(out=v, in_=v, compare_op=ALU.is_ge, fill=0.0, base=b - 1,
                                     pattern=[[b, P // b], [0, b]], channel_multiplier=-1))
            for l in range(7):
                then(g.tensor_tensor(lvl_tmp[:, :], blocks[:, l + 1, :], blocks[:, l, :], ALU.subtract))
                up = l == 0
                then(g.affine_select(out=lvl_tmp[:, :], in_=lvl_tmp[:, :], compare_op=ALU.is_ge, fill=0.0, base=0,
                                     pattern=[[1 if up else -1, P]], channel_multiplier=-1 if up else 1))
                then(g.tensor_copy(merge_mask[:, l, :], lvl_tmp[:, :]))
            pool.drain().then_inc(consts, 1)

        def setup_act(act):
            def squares(c):
                act.wait_ge(x_load[c], 16)
                wait(act, x_sq, c)
                nc.scalar.activation(sq_scr[:, :], x_rows[:, c, :], ACT.Square,
                                     accum_out=ssum[:, c:c + 1]).then_inc(x_sq, 1)

            def roots(group):
                cs = slice(4 * group, 4 * group + 4)
                act.wait_ge(x_sq, 4 * group + 4)
                nc.scalar.activation(rstd[:, cs], ssum[:, cs], ACT.Ln, scale=1.0 / D, bias=EPS)
                act.drain()
                nc.scalar.activation(rstd[:, cs], rstd[:, cs], ACT.Exp, scale=-0.5).then_inc(x_rstd, 1)

            for c in range(4):
                squares(c)
            roots(0)
            for c in range(KT):
                for q in range(2):
                    act.wait_ge(x_weighted, 2 * c + q + 1)
                    nc.scalar.activation(act_in[0][:, 4 * q:4 * q + 4, c * P:(c + 1) * P],
                                         u_tmp[:, q, :].rearrange("p (f t) -> p f t", t=P),
                                         ACT.Copy).then_inc(x_high, 1)
                if c < 3:
                    squares(4 + c)
                if c == 2:
                    squares(7)
                    roots(1)

        def setup_vec(dve):
            v = nc.vector
            dve.wait_ge(params, 16 * 4)
            for c in range(KT):
                dve.wait_ge(x_rstd, c // 4 + 1)
                if c >= 2:
                    dve.wait_ge(x_turned, 2 * (c - 1))
                v.tensor_scalar(xn[:, c % 2, :], x_rows[:, c, :], rstd[:, c:c + 1], None,
                                ALU.mult).then_inc(x_scaled, 1)
                for q in range(2):
                    dve.wait_ge(x_turned, 2 * c + q + 1)
                    if c:
                        dve.wait_ge(x_low, 2 * (c - 1) + q + 1)
                    v.tensor_tensor(u_tmp[:, q, :].rearrange("p (f t) -> p f t", t=P),
                                    bank[X0 + q][:, :].rearrange("p (f t) -> p f t", t=P),
                                    norm_mix_c[:, 4 * q:4 * q + 4].unsqueeze(2).broadcast_to([P, 4, P]),
                                    ALU.mult).then_inc(x_weighted, 1)
                if c == 1:
                    dve.wait_ge(ba_loaded, 32)
                    v.tensor_copy(flat(w_ba_part[0]), flat(w_ba))
                    dve.drain()
                    v.tensor_tensor(flat(w_ba_part[1]), flat(w_ba), flat(w_ba_part[0]).bitcast(F32),
                                    ALU.subtract).then_inc(ba_split, 1)

        def setup_pe(pe):
            pe.sem_inc(projected, 2 * FREE)
            pe.wait_ge(consts, 2)

            def beta_decay(q, k):
                for wp, ap in PASSES:
                    last = nc.tensor.matmul(bank[Z0 + q][:, :], w_ba_part[wp][:, k, :],
                                            act_in[ap][:, k, q * HALF:(q + 1) * HALF],
                                            start=k == 0 and (wp, ap) == PASSES[0],
                                            stop=k == KT - 1 and (wp, ap) == PASSES[-1])
                if k == KT - 1:
                    last.then_inc(ba_done, 1)

            for c in range(KT):
                pe.wait_ge(x_scaled, c + 1)
                for q in range(2):
                    if c:
                        pe.wait_ge(x_weighted, 2 * (c - 1) + q + 1)
                    for f in range(4):
                        last = nc.tensor.transpose(bank[X0 + q][:, f * P:(f + 1) * P],
                                                   xn[:, c % 2, (4 * q + f) * P:(4 * q + f + 1) * P], ident[:, :])
                    last.then_inc(x_turned, 1)
                if c >= KT // 2:
                    if c == KT // 2:
                        pe.wait_ge(ba_split, 1)
                        pe.wait_ge(x_low, KT)
                    for k in (2 * c - KT, 2 * c - KT + 1):
                        beta_decay(0, k)
            pe.wait_ge(x_low, 2 * KT)
            for k in range(KT):
                beta_decay(1, k)

        b8, a8 = slice(0, 8), slice(32, 40)

        def decay_act(act, j):
            f = nc.scalar.activation
            if j == 2:
                act.wait_ge(rate_loaded, 32)
                f(rate[a8, 1:2], rate[a8, 0:1], ACT.Exp).then_inc(ba_act, 1)
                act.wait_ge(ba_done, 2)
                for q in range(2):
                    f(row_t[0][:, q * HALF:(q + 1) * HALF], bank[Z0 + q][0:40, :], ACT.Copy).then_inc(ba_act, 1)
            elif j == 10:
                act.wait_ge(ba_vec, 1)
                f(row_t[1][b8, :], row_t[0][b8, :], ACT.Exp, scale=-1.0)
                f(row_t[1][a8, :], row_t[2][a8, :], ACT.Exp)
                act.drain()
                f(row_t[1][a8, :], row_t[1][a8, :], ACT.Ln, bias=1.0).then_inc(ba_act, 1)
            elif j == 38:
                act.wait_ge(ba_vec, 3)
                f(row_t[3][b8, :], rows[b8, :], ACT.Exp)
                f(rows[96:104, :], row_t[2][b8, :], ACT.Exp).then_inc(ba_act, 1)
            elif j == 48:
                act.wait_ge(ba_vec, 7)
                for i, src in enumerate((rows[b8, :], row_t[3][b8, :], row_t[4][b8, :])):
                    act.dma_start(scr_rows[i], src).then_inc(rows_stored, 16)
            if 48 <= j < 48 + NCH // 2:
                for c in (2 * (j - 48), 2 * (j - 48) + 1):
                    act.wait_ge(ba_turned, c + 1)
                    f(per_token[:, c, :, 0:8], bank[X0 + c % 2][:, 0:P].rearrange("p (k e) -> p k e", e=32)[:, :, 0:8],
                      ACT.Copy).then_inc(ba_act, 1)

        def decay_pe(pe, j):
            if 48 <= j < 48 + NCH // 2:
                if j == 48:
                    pe.wait_ge(ba_vec, 7)
                for c in (2 * (j - 48), 2 * (j - 48) + 1):
                    if c >= 2:
                        pe.wait_ge(ba_act, 5 + c - 1)
                    nc.tensor.transpose(bank[X0 + c % 2][:, 0:P], rows[:, c * P:(c + 1) * P],
                                        ident[:, :]).then_inc(ba_turned, 1)
            elif j == 48 + NCH // 2:
                pe.wait_ge(ba_act, 5 + NCH)

        def decay_vec(dve, j):
            if j:
                return
            v = nc.vector
            dve.wait_ge(ba_act, 3)
            dve.wait_ge(rate_loaded, 32)
            dve.wait_ge(consts, 1)
            v.tensor_scalar(row_t[0][a8, :], row_t[0][a8, :], rate[a8, 2:3], None, ALU.add)
            v.memset(rows[:, :], 0.0)
            v.memset(reset[:, 0:S:P], 0.0)
            dve.drain()
            v.tensor_scalar(row_t[3][a8, :], row_t[0][a8, :], -1.0, None, ALU.mult)
            dve.drain()
            v.tensor_tensor(row_t[2][a8, :], row_t[0][a8, :], row_t[3][a8, :], ALU.min).then_inc(ba_vec, 1)
            dve.wait_ge(ba_act, 4)
            v.tensor_scalar(row_t[1][b8, :], row_t[1][b8, :], 1.0, None, ALU.add)
            v.scalar_tensor_tensor(row_t[1][a8, :], row_t[0][a8, :], 0.0, row_t[1][a8, :], ALU.max, ALU.add)
            dve.drain()
            v.reciprocal(rows[a8, :], row_t[1][b8, :])
            v.tensor_scalar(row_t[2][b8, :], row_t[1][a8, :], rate[a8, 1:2], -1.0, ALU.mult,
                            ALU.mult).then_inc(ba_vec, 1)
            dve.drain()
            v.tensor_tensor_scan(rows[b8, :], reset[:, :], row_t[2][b8, :], 0.0, ALU.mult, ALU.add)
            v.tensor_scalar(row_t[4][b8, :], rows[a8, :], -1.0, None, ALU.mult)
            dve.drain()
            gc3 = rows[b8, :].rearrange("p (c t) -> p c t", t=P)
            v.tensor_tensor(row_t[2][b8, :].rearrange("p (c t) -> p c t", t=P),
                            gc3[:, :, P - 1:P].broadcast_to([8, NCH, P]), gc3, ALU.subtract).then_inc(ba_vec, 1)
            dve.wait_ge(ba_act, 5)
            v.tensor_copy(row_t[1][b8, :], rows[a8, :])
            dve.drain()
            v.tensor_tensor(rows[64:72, :], row_t[3][b8, :], row_t[1][b8, :], ALU.mult).then_inc(ba_vec, 4)

        a0 = work
        qk_t = []
        for g in range(3):
            qk_t.append((at(f"qa{g}", [P, S], F32, a0), at(f"ka{g}", [P, S], F32, a0 + 4096)))
            a0 += 8192
        va_t = at("va_t", [P, S], F32, a0)
        va = at("va", [P, KT, P], F32, a0 + 4096)
        a0 += 8192
        score, prob, prob_t = [], [], []
        for b in range(2):
            score.append(at(f"score{b}", [P, HALF], F32, a0))
            prob.append(at(f"prob{b}", [P, HALF], F32, a0 + 2048))
            prob_t.append(at(f"prob_t{b}", [P, HALF], F32, a0 + 4096))
            a0 += 6144
        o_t = [at(f"o_t{g}", [P, S], F32, a0 + 4096 * g) for g in range(3)]
        a0 += 12288
        stat_b = [at(f"stat_b{g}", [P, 2 * S], F32, a0 + 8192 * g) for g in range(3)]
        a0 += 24576
        joint = at("joint", [P, S], F32, a0)
        stat = at("stat", [P, 16], F32, a0 + 4096)
        neg_max = at("neg_max", [P, 8], F32, a0 + 4160)
        stat_t = at("stat_t", [16, P], F32, a0 + 4192)
        assert a0 + 4800 <= work + 98304

        dense_read = sem("dense_read")
        v_turned, v_copied = sem("v_turned"), sem("v_copied")
        scored, scaled, maxed, exped = sem("scored"), sem("scaled"), sem("maxed"), sem("exped")
        p_turned, p_copied = sem("p_turned"), sem("p_copied")
        o_ready, o_taken = sem("o_ready"), sem("o_taken")
        st_turned, st_copied, st_stored, st_loaded = sem("st_turned"), sem("st_copied"), sem("st_stored"), [sem(f"st_loaded{g}") for g in range(3)]
        mix_vec, mix_act, mixed_sem, y_stored = sem("mix_vec"), sem("mix_act"), sem("mixed_a"), sem("y_stored")

        PAIRS = (4, 4, 2)
        NP_SLOT = sum(PAIRS)
        FIRST_PAIR = {2: 0, 0: 0, 1: 4}

        def pair_no(s, g, p):
            return NP_SLOT * s + ((0, 4, 8)[g] + p)

        def att_steps(g):
            if g == 2:
                return ["v0", "v1", "s0", "s1", "t0", "t1", "o0", "o1", "st"]
            return ["v0", "v1", "s0", "s1", "t0", "s2", "t1", "o0", "s3", "t2", "o1", "t3", "o2", "o3", "st"]

        def block_keys(g, b):
            if g == 0:
                return (b - 1 if b else None), b
            if g == 1:
                return (b - 4 if b >= 4 else None), b
            return None, b

        def att_pe(pe, s, g, step):
            q, k = qk_t[g]
            kind, p = step[0], step[1:]
            if kind == "v":
                h = int(p)
                wait(pe, dense_read, 18 * s + (6 * g + 6))
                for i in range(4):
                    last = nc.tensor.transpose(bank[Y0 + h][:, i * P:(i + 1) * P],
                                               va_t[:, (4 * h + i) * P:(4 * h + i + 1) * P], ident[:, :])
                last.then_inc(v_turned, 1)
            elif step == "st":
                wait(pe, exped, pair_no(s, g, PAIRS[g] - 1) + 1)
                nc.tensor.transpose(bank[X0][0:16, 0:P], stat[:, :], ident[:, :]).then_inc(st_turned, 1)
            elif kind == "s":
                p = int(p)
                n = pair_no(s, g, p)
                if p >= 2:
                    wait(pe, scaled, n - 1)
                elif p == 0:
                    wait(pe, st_copied, 3 * s + g)
                for i in range(4 if g == 2 else 2):
                    b = (4 if g == 2 else 2) * p + i
                    lhs = q[:, b * P:(b + 1) * P]
                    if g == 2:
                        last = nc.tensor.matmul(bank[X0 + p % 2][:, i * P:(i + 1) * P], lhs, k[:, b * P:(b + 1) * P],
                                                start=True, stop=True)
                    else:
                        before, own = block_keys(g, b)
                        blocks_k = k[:, :].rearrange("p (b i) -> p b i", i=P)
                        if before is None:
                            rhs = blocks_k[:, own:own + 1, :].broadcast_to([P, 2, P])
                        else:
                            rhs = blocks_k[:, before:own + 1:own - before, :]
                        last = nc.tensor.matmul(bank[X0 + p % 2][:, i * 256:(i + 1) * 256].rearrange("p (a j) -> p a j", a=2),
                                                lhs, rhs, start=True, stop=True)
                last.then_inc(scored, 1)
            elif kind == "t":
                p = int(p)
                n = pair_no(s, g, p)
                wait(pe, exped, n + 1)
                wait(pe, p_copied, n - 1)
                if p < 2:
                    wait(pe, v_copied, 6 * s + (2 * g + 2))
                for i in range(4):
                    last = nc.tensor.transpose(bank[Y0 + p % 2][:, i * P:(i + 1) * P],
                                               prob[p % 2][:, i * P:(i + 1) * P], ident[:, :])
                last.then_inc(p_turned, 1)
            else:
                p = int(p)
                n = pair_no(s, g, p)
                wait(pe, p_copied, n + 1)
                ob = Z0 + (p if g == 2 else p // 2)
                if g == 2:
                    wait(pe, o_taken, 6 * s + 2 * g + (p - 1))
                elif p % 2 == 0:
                    wait(pe, o_taken, 6 * s + (2 * g + p // 2 - 1))
                for i in range(4 if g == 2 else 2):
                    b = (4 if g == 2 else 2) * p + i
                    o = bank[ob][:, (b % 4) * P:(b % 4 + 1) * P]
                    before, own = block_keys(g, b)
                    pt = prob_t[p % 2]
                    if g == 2:
                        last = nc.tensor.matmul(o, va[:, own, :], pt[:, i * P:(i + 1) * P], start=True, stop=True)
                    else:
                        if before is not None:
                            nc.tensor.matmul(o, va[:, before, :], pt[:, 2 * i * P:(2 * i + 1) * P], start=True, stop=False)
                        last = nc.tensor.matmul(o, va[:, own, :], pt[:, (2 * i + 1) * P:(2 * i + 2) * P],
                                                start=before is None, stop=True)
                last.then_inc(o_ready, 1)

        def att_act(act, s, g, step):
            kind, p = step[0], step[1:]
            if kind == "v":
                h = int(p)
                act.wait_ge(v_turned, 6 * s + (2 * g + h + 1))
                if h == 0:
                    wait(act, o_ready, pair_no(s, g, 0))
                nc.scalar.activation(va[:, 4 * h:4 * h + 4, :],
                                     bank[Y0 + h][:, :].rearrange("p (b d) -> p b d", d=P), ACT.Copy).then_inc(v_copied, 1)
            elif step == "st":
                act.wait_ge(st_copied, 3 * s + (g + 1))
                act.dma_start(scr_stat[g].rearrange("(a b) -> a b", b=P), stat_t[:, :]).then_inc(st_stored, 16)
            elif kind == "s":
                p = int(p)
                n = pair_no(s, g, p)
                act.wait_ge(maxed, n + 1)
                wait(act, p_turned, n - 1)
                m = 4 if g == 2 else 2
                w = HALF // m
                for i in range(m):
                    b = m * p + i
                    last = nc.scalar.activation(prob[p % 2][:, i * w:(i + 1) * w], score[p % 2][:, i * w:(i + 1) * w],
                                                ACT.Exp, bias=neg_max[:, b:b + 1], accum_out=stat[:, 8 + b:9 + b])
                last.then_inc(exped, 1)
            elif kind == "t":
                p = int(p)
                n = pair_no(s, g, p)
                act.wait_ge(p_turned, n + 1)
                wait(act, o_ready, n - 1)
                nc.scalar.activation(prob_t[p % 2][:, :], bank[Y0 + p % 2][:, :], ACT.Copy).then_inc(p_copied, 1)
            else:
                p = int(p)
                if g != 2 and p % 2 == 0:
                    return
                h = p if g == 2 else p // 2
                act.wait_ge(o_ready, pair_no(s, g, p) + 1)
                if h == 0:
                    wait(act, mixed_sem, s)
                src, o = bank[Z0 + h], o_t[g]
                if g == 0:
                    dst, src = o[:, h * HALF:(h + 1) * HALF], src[:, :]
                elif g == 1:
                    dst = o[:, h * HALF:(h + 1) * HALF].rearrange("p (i r) -> p r i", r=4)
                    src = src[:, :].rearrange("p (r i) -> p r i", r=4)
                else:
                    dst = o[:, :].rearrange("p (i r) -> p r i", r=16)[:, 8 * h:8 * h + 8, :]
                    src = src[:, :].rearrange("p (r i) -> p r i", r=8)
                nc.scalar.activation(dst, src, ACT.Copy).then_inc(o_taken, 1)

        def att_vec(dve, s, g, step):
            kind, p = step[0], step[1:]
            v = nc.vector
            if step == "st":
                dve.wait_ge(st_turned, 3 * s + (g + 1))
                wait(dve, st_stored, 16 * (3 * s + g))
                v.tensor_copy(stat_t[:, :], bank[X0][0:16, 0:P]).then_inc(st_copied, 1)
            elif kind == "s":
                p = int(p)
                n = pair_no(s, g, p)
                dve.wait_ge(scored, n + 1)
                wait(dve, exped, n - 1)
                if p == 0:
                    wait(dve, st_turned, 3 * s + g)
                slope = slopes[:, ds(s + 4 * g, 1)]
                if g == 2:
                    dist = band_pair[:, :].unsqueeze(1).broadcast_to([P, 4, P])
                    m, w = 4, P
                else:
                    first = block_keys(g, 2 * p)[0] is None
                    both = block_keys(g, 2 * p + 1)[0] is None
                    m, w = 2, 256
                    if first and both:
                        dist = band[:, 0:1, :].broadcast_to([P, 2, 256])
                    elif first:
                        dist = band[:, :, :]
                    else:
                        dist = band[:, 1:2, :].broadcast_to([P, 2, 256])
                sc = score[p % 2][:, :].rearrange("p (a j) -> p a j", a=m)
                v.scalar_tensor_tensor(sc, dist, slope, bank[X0 + p % 2][:, :].rearrange("p (a j) -> p a j", a=m),
                                       ALU.mult, ALU.add).then_inc(scaled, 1)
                dve.drain()
                v.reduce_max(stat[:, m * p:m * p + m], sc, AXX)
                dve.drain()
                v.tensor_scalar(neg_max[:, m * p:m * p + m], stat[:, m * p:m * p + m], -1.0, None,
                                ALU.mult).then_inc(maxed, 1)

        def token_view(g, ap):
            if g == 0:
                return ap
            if g == 1:
                return ap.rearrange("p (n r i) -> p n i r", n=2, r=4)
            return ap.rearrange("p (r i) -> p i r", r=16)

        def like(g, ap):
            if g == 0:
                return ap
            if g == 1:
                return ap.rearrange("p (n i r) -> p n i r", n=2, r=4)
            return ap.rearrange("p (i r) -> p i r", r=16)

        def mix_vec_engine(dve, s, piece):
            v = nc.vector
            mx = [stat_b[g][:, 0:S] for g in range(3)]
            den = [stat_b[g][:, S:2 * S] for g in range(3)]
            if piece == "max":
                for g in range(2):
                    dve.wait_ge(st_loaded[g], 16 * s + 16)
                wait(dve, y_stored, 16 * s)
                v.tensor_tensor(like(1, joint[:, :]), like(1, mx[0]), token_view(1, mx[1]), ALU.max)
                dve.drain()
                dve.wait_ge(st_loaded[2], 16 * s + 16)
                v.tensor_tensor(like(2, joint[:, :]), like(2, joint[:, :]), token_view(2, mx[2]), ALU.max)
                dve.drain()
            elif piece[:3] == "sub":
                g = int(piece[3])
                v.tensor_tensor(token_view(g, mx[g]), token_view(g, mx[g]), like(g, joint[:, :]),
                                ALU.subtract).then_inc(mix_vec, 1)
            elif piece[:3] == "mul":
                g = int(piece[3])
                dve.wait_ge(o_taken, 6 * s + 6)
                dve.wait_ge(mix_act, 3 * s + (g + 1))
                v.tensor_tensor(den[g], den[g], mx[g], ALU.mult)
                v.tensor_tensor(like(g, o_t[g][:, :]), like(g, o_t[g][:, :]), token_view(g, mx[g]), ALU.mult)
                dve.drain()
            elif piece[:3] == "add":
                g = int(piece[3])
                first = den[0] if g == 1 else joint[:, :]
                v.tensor_tensor(like(g, joint[:, :]), like(g, first), token_view(g, den[g]), ALU.add)
                v.tensor_tensor(o_t[0][:, :], o_t[0][:, :], o_t[g][:, :], ALU.add)
                dve.drain()
            elif piece[:3] == "rec":
                q = slice(256 * int(piece[3]), 256 * int(piece[3]) + 256)
                v.reciprocal(joint[:, q], joint[:, q])
                dve.drain()
            elif piece == "end":
                v.tensor_tensor(joint[:, :], o_t[0][:, :], joint[:, :], ALU.mult).then_inc(mixed_sem, 1)

        def mix_act_engine(act, s, piece):
            if piece == "load":
                for g in range(3):
                    if isinstance(s, int) or g == 0:
                        act.wait_ge(rows_stored, 48)
                    act.wait_ge(st_stored, 16 * (3 * s + 3))
                    act.dma_start(stat_b[g][:, :], scr_stat[g].partition_broadcast(P)).then_inc(st_loaded[g], 16)
            elif piece[:3] == "sub":
                g = int(piece[3])
                act.wait_ge(mix_vec, 3 * s + (g + 1))
                nc.scalar.activation(stat_b[g][:, 0:S], stat_b[g][:, 0:S], ACT.Exp).then_inc(mix_act, 1)
            elif piece == "end":
                act.wait_ge(mixed_sem, s + 1)
                act.dma_start(scr_branch[ds(s * P, P), :], joint[:, :]).then_inc(y_stored, 16)

        MIX = {0: {32: ["load"], 38: ["max"], 41: ["sub0", "sub1"], 44: ["sub2"], 47: ["mul0"]},
               1: {1: ["mul1"], 4: ["mul2"], 6: ["add1"], 9: ["add2"], 12: ["rec0"], 14: ["rec1"], 19: ["rec2"],
                   21: ["rec3"], 23: ["end"]}}

        def mix_pieces(eng, mix, s, g, j):
            for piece in MIX.get(g, {}).get(j, ()):
                mix(eng, s, piece)

        def dense_att_pe(pe, s, g, j):
            i, half, k = j // 16, j // 8 % 2, j % 8
            m = 9 * s + (3 * g + i)
            dense_k(pe, ph["attn"], s, 3 * g + i, half, k, KT, D0 + half, act_in,
                    (dense_read, m * 2 + (half - 1)))

        def dense_att_act(act, s, g, j):
            if j % 8 != 7:
                return
            i, half = j // 16, j // 8 % 2
            act.wait_ge(projected, done(ph["attn"], s, 3 * g + i, half))
            t = (*qk_t[g], va_t)[i]
            src = bank[D0 + half]
            if i == 2 and half == 0:
                wait(act, v_turned, 6 * s + 2 * g)
            if g == 0:
                dst, src = t[:, half * HALF:(half + 1) * HALF], src[:, :]
            elif g == 1:
                dst = t[:, half * HALF:(half + 1) * HALF].rearrange("p (r i) -> p r i", r=4)
                src = src[:, :].rearrange("p (i r) -> p r i", r=4)
            else:
                dst = t[:, :].rearrange("p (r i) -> p r i", r=16)[:, :, 32 * half:32 * half + 32]
                src = src[:, :].rearrange("p (i r) -> p r i", r=16)
            nc.scalar.activation(dst, src, ACT.Copy, scale=float(P) ** -0.5 if i == 0 else 1.0).then_inc(dense_read, 1)

        AT = {15: (4, 5, 7, 9, 14, 16, 18, 20, 22, 25, 27, 31, 33, 36, 39), 9: (4, 5, 7, 9, 14, 17, 19, 22, 26)}

        def segment(eng, s, g, dense, side, side_s, mix=None, extra=None):
            before = (g + 2) % 3
            steps = att_steps(before) if side is not None else []
            for j in range(48):
                if dense is not None:
                    dense(eng, s, g, j)
                if extra is not None:
                    extra(eng, 48 * g + j)
                if steps and j in AT[len(steps)]:
                    side(eng, side_s, before, steps[AT[len(steps)].index(j)])
                if mix is not None:
                    mix_pieces(eng, mix, s - 1, g, j)

        def nothing(*_):
            pass

        def attention(eng, dense, side, mix, decay_):
            segment(eng, 0, 0, dense, None, 0, extra=decay_)
            segment(eng, 0, 1, dense, side, 0, extra=decay_)
            segment(eng, 0, 2, dense, side, 0)
            with eng.Fori(1, NSLOT) as s:
                segment(eng, s, 0, dense, side, s - 1, mix)
                segment(eng, s, 1, dense, side, s, mix)
                segment(eng, s, 2, dense, side, s)

        MIX_END = {28: ["load"], 33: ["max"], 35: ["sub0", "sub1"], 37: ["sub2"], 39: ["mul0"], 42: ["mul1"],
                   45: ["mul2"], 49: ["add1"], 51: ["add2"], 53: ["rec0"], 55: ["rec1"], 57: ["rec2"], 59: ["rec3"],
                   63: ["end"]}

        def attention_end(eng, side, mix, j):
            if j in AT[9]:
                side(eng, NSLOT - 1, 2, att_steps(2)[AT[9].index(j)])
            for piece in MIX_END.get(j, ()):
                mix(eng, NSLOT - 1, piece)

        def attention_sp(sp):
            with sp.Fori(0, NSLOT) as s:
                for i in range(9):
                    first = (COL_QA, COL_KA, COL_VA)[i % 3] + NSLOT * P * (i // 3)
                    load_weights(sp, ph["attn"], s, i, w_cols(w_in2, s * P + first))

        OB = ((D0, D1), (Y0, Y1))
        g_stored = [sem(f"g_stored{i}") for i in range(2)]
        g_sig, b_loaded, b_high, b_low = (
            sem("g_sig"), sem("b_loaded"), sem("b_high"), sem("b_low"))
        m_gate, m_prod, m_sum, m_high, m_low = sem("m_gate"), sem("m_prod"), sem("m_sum"), sem("m_high"), sem("m_low")
        PEELED = 2

        def gates_sp(sp):
            with sp.Fori(0, KT) as f:
                for i in range(2):
                    load_weights(sp, ph["gates"], f, i, w_cols(w_in2, f * P + (COL_GATE + i * D)))

        def gates_pool(pool):
            with pool.Fori(0, KT) as f:
                for i in range(2):
                    split_weights(pool, ph["gates"], f, i)

        def gate_step_pe(pe, f, i, half, k):
            free = (g_sig, f * 4 + (2 * i + half - 1))
            if isinstance(f, int) and f == 0 and i == 0:
                free = (dl["read"], 8 * NHB - 1 + half)
            dense_k(pe, ph["gates"], f, i, half, k, KT, D0 + half, act_in, free)

        def gate_take_act(act, f, i, half):
            act.wait_ge(projected, done(ph["gates"], f, i, half))
            if half == 0:
                wait(act, g_stored[i], f * 16)
            nc.scalar.activation(tmp[i][:, half * HALF:(half + 1) * HALF], bank[D0 + half][:, :],
                                 ACT.Sigmoid).then_inc(g_sig, 1)
            if half == 1:
                act.wait_ge(g_sig, f * 4 + (2 * i + 2))
                act.dma_start(scr_gate[ds(f * P + i * D, P), :], tmp[i][:, :]).then_inc(g_stored[i], 16)

        def gates_peeled(eng, dense, j):
            dense(eng, j // 32, j // 16 % 2, j // 8 % 2, j % 8)

        def gate_step_act(act, f, i, half, k):
            if k == KT - 1:
                gate_take_act(act, f, i, half)

        def gates_pe(pe):
            with pe.Fori(PEELED, KT) as f:
                for i in range(2):
                    for half in range(2):
                        for k in range(KT):
                            gate_step_pe(pe, f, i, half, k)

        def gates_act(act):
            act.wait_ge(y_stored, 16 * NSLOT)
            act.wait_ge(dl["stored"], 16 * NHB)
            with act.Fori(PEELED, KT) as f:
                for i in range(2):
                    t = f * 2 + (i - 2 * PEELED)
                    act.wait_ge(b_low, f * 2 + (i - 2 * PEELED))
                    act.dma_start(tmp[2][:, :], scr_branch[ds(f * (2 * P) + (i - 2 * PEELED) * P, P), :]).then_inc(b_loaded, 16)
                    gate_take_act(act, f, i, 0)
                    act.wait_ge(b_loaded, f * 32 + (16 * (i - 2 * PEELED) + 16))
                    nc.scalar.activation(branch[0][:, ds(t, 1), :].rearrange("p a t -> p (a t)"), tmp[2][:, :],
                                         ACT.Copy).then_inc(b_high, 1)
                    gate_take_act(act, f, i, 1)

        def gates_vec(dve):
            with dve.Fori(PEELED, KT) as f:
                for i in range(2):
                    t = f * 2 + (i - 2 * PEELED)
                    dve.wait_ge(b_high, f * 2 + (i - 2 * PEELED + 1))
                    nc.vector.tensor_tensor(branch[1][:, ds(t, 1), :].rearrange("p a t -> p (a t)"), tmp[2][:, :],
                                            branch[0][:, ds(t, 1), :].rearrange("p a t -> p (a t)").bitcast(F32),
                                            ALU.subtract).then_inc(b_low, 1)

        def merge_sp(sp):
            with sp.Fori(0, KT) as f:
                load_weights(sp, ph["merge"], f, 0, w_cols(w_proj_attn[0], f * P, NSLOT))
                load_weights(sp, ph["merge"], f, 1, w_cols(w_proj_delta[0], f * P, NHB))

        def merge_pool(pool):
            with pool.Fori(0, KT) as f:
                split_weights(pool, ph["merge"], f, 0, NSLOT)
                split_weights(pool, ph["merge"], f, 1, NHB)

        def merge_pe(pe):
            attn = [b[:, 0:NSLOT, :] for b in branch]
            delta_ = [b[:, NSLOT:NB, :] for b in branch]

            def step(f):
                for i, (kt, rhs) in enumerate(((NSLOT, attn), (NHB, delta_))):
                    for half in range(2):
                        free = (m_prod, f * 4 + (2 * i + half - 3))
                        if isinstance(f, int):
                            free = (g_sig, 4 * KT)
                        for k in range(kt):
                            dense_k(pe, ph["merge"], f, i, half, k, kt, OB[i][half], rhs, free)

            pe.wait_ge(b_low, NB)
            step(0)
            with pe.Fori(1, KT) as f:
                step(f)

        def merge_act(act):
            for i in range(2):
                act.wait_ge(g_stored[i], 16 * KT)

            def load(f):
                for i in range(2):
                    act.dma_start(tmp[i][:, :], scr_gate[ds(f * P + i * D, P), :]).then_inc(m_gate, 16)

            def step(f, more):
                act.wait_ge(m_sum, f + 1)
                if more:
                    load(f + 1)
                nc.scalar.activation(act_in[0][:, ds(f, 1), :].rearrange("p a t -> p (a t)"), tmp[2][:, :],
                                     ACT.Copy).then_inc(m_high, 1)

            load(0)
            with act.Fori(0, KT - 1) as f:
                step(f, True)
            step(KT - 1, False)

        def merge_vec(dve):
            v = nc.vector

            def step(f):
                dve.wait_ge(m_gate, f * 32 + 32)
                for i in range(2):
                    for half in range(2):
                        c = slice(half * HALF, (half + 1) * HALF)
                        dve.wait_ge(projected, done(ph["merge"], f, i, half))
                        v.tensor_tensor(tmp[i][:, c], tmp[i][:, c], bank[OB[i][half]][:, :], ALU.mult).then_inc(m_prod, 1)
                dve.drain()
                v.tensor_tensor(tmp[2][:, :], tmp[0][:, :], tmp[1][:, :], ALU.add).then_inc(m_sum, 1)
                dve.wait_ge(m_high, f + 1)
                v.tensor_tensor(act_in[1][:, ds(f, 1), :].rearrange("p a t -> p (a t)"), tmp[2][:, :],
                                act_in[0][:, ds(f, 1), :].rearrange("p a t -> p (a t)").bitcast(F32),
                                ALU.subtract).then_inc(m_low, 1)
                dve.drain()

            step(0)
            with dve.Fori(1, KT) as f:
                step(f)

        d0 = [work + 16384]

        def dt_(name, shape):
            t = at(name, shape, F32, d0[0])
            d0[0] += size_of(shape, F32)
            return t

        conv_in = [at(f"conv_in{i}", [P, 3 + S + 5], F32, slot2 + 4128 * i) for i in range(2)]
        conv_out = at("conv_out", [P, S], F32, work)
        qkv = [at(f"qkv{i}", [P, S], F32, work + 4096 + 4096 * i) for i in range(3)]
        z_next = at("z_next", [P, S], F32, work + 92160)
        z_now = dt_("z_now", [P, S])
        sq = [dt_(f"sq{i}", [P, S]) for i in range(2)]
        qn, kn = dt_("qn", [P, S]), dt_("kn", [P, S])
        row = [dt_(f"row{i}", [P, S]) for i in range(3)]
        decay, neg_a = row[0], row[2]
        inv, inv_t, half_way = dt_("inv", [P, S]), dt_("inv_t", [P, S]), dt_("half_way", [P, S])
        beta_v, beta_k, k_dec = dt_("beta_v", [P, S]), dt_("beta_k", [P, S]), dt_("k_dec", [P, S])
        col = dt_("col", [P, NCH, 4])
        decay_all = dt_("decay_all", [P, NCH])
        state, u_now = dt_("state", [P, P]), dt_("u_now", [P, P])
        assert d0[0] <= work + 92160, d0[0] - work
        u_bar, w_t = inv, half_way
        o_raw, o_sq = beta_v, beta_k

        dl = {x_: sem("dl_" + x_) for x_ in (
            "read", "conv", "silu", "sq", "ss", "ln", "normed", "vt", "bv", "kt", "kdec", "kk", "qk", "rows",
            "diff", "dec", "a", "pt", "t0t", "t0", "t0c", "y", "yc", "dt", "dtm", "tt", "ttc", "ub", "ubc", "wt", "wtc",
            "qdec", "ws", "u", "o", "s", "sup", "z", "os", "osq", "oss", "oln", "out", "stored", "zero")}

        def compact(t, c, level):
            return t[:, c * 64:(c + 1) * 64].rearrange("p (n b) -> p n b", b=1 << level)

        def c4(t, half):
            return t[:, half * HALF:(half + 1) * HALF].rearrange("p (c t) -> p c t", t=P)

        def chunk(t, c):
            return t[:, c * P:(c + 1) * P]

        STEPS_AT = {0: ["sq"], 7: ["ss"], 10: ["vt0"], 11: ["vt1"], 15: ["kt0"], 16: ["kt1", "kk0"], 17: ["kk1"],
                    18: ["qk0"], 19: ["qk1"], 21: ["t00"], 22: ["t01"], 42: ["ub0", "ub1", "wt0", "wt1"], 63: ["on", "end"]}
        for level in range(1, 7):
            for n_, x_ in enumerate("ydt"):
                STEPS_AT[24 + 3 * (level - 1) + n_] = [f"{x_}{level}0", f"{x_}{level}1"]
        for c_ in range(NCH):
            STEPS_AT[44 + 2 * c_] = [f"a{c_}"]
            STEPS_AT[45 + 2 * c_] = [f"b{c_}"]
        TAPS_AT = {22: (0, 0), 23: (0, 1), 25: (0, 2), 28: (0, 3), 34: (1, 0), 37: (1, 1), 40: (1, 2), 43: (1, 3),
                   48: (2, 0), 50: (2, 1), 52: (2, 2), 54: (2, 3)}
        SILU_AT = {30: 0, 46: 1, 58: 2}

        def left(t, level):
            return t.rearrange("p c (n a b) -> p c n a b", a=2, b=1 << level)[:, :, :, 0, :]

        def delta_pe(pe, h, step):
            mm, tr = nc.tensor.matmul, nc.tensor.transpose
            two = h * 2
            if step == "ss":
                wait(pe, dl["sup"], h * NCH)
                wait(pe, dl["osq"], two)
                for i in range(2):
                    pe.wait_ge(dl["sq"], two + (i + 1))
                    for half in range(2):
                        last = mm(bank[(X0, Y0)[i] + half][:, :], ones[:, :], sq[i][:, half * HALF:(half + 1) * HALF],
                                  start=True, stop=True)
                    last.then_inc(dl["ss"], 1)
            elif step[:2] == "vt":
                half = int(step[2])
                pe.wait_ge(dl["silu"], h * 3 + 3)
                wait(pe, dl["oln"], two)
                for c in range(4 * half, 4 * half + 4):
                    last = tr(bank[Z0 + half][:, (c % 4) * P:(c % 4 + 1) * P], chunk(qkv[2], c), ident[:, :])
                last.then_inc(dl["vt"], 1)
            elif step[:2] == "kt":
                half = int(step[2])
                pe.wait_ge(dl["normed"], two + 2)
                for c in range(4 * half, 4 * half + 4):
                    last = tr(bank[X0 + half][:, (c % 4) * P:(c % 4 + 1) * P], chunk(kn, c), ident[:, :])
                last.then_inc(dl["kt"], 1)
            elif step[:2] == "kk":
                half = int(step[2])
                for c in range(4 * half, 4 * half + 4):
                    last = mm(bank[Y0 + half][:, (c % 4) * P:(c % 4 + 1) * P], chunk(kn, c), chunk(kn, c), start=True, stop=True)
                last.then_inc(dl["kk"], 1)
            elif step[:2] == "qk":
                half = int(step[2])
                pe.wait_ge(dl["bv"], two + (half + 1))
                for c in range(4 * half, 4 * half + 4):
                    last = mm(bank[Z0 + half][:, (c % 4) * P:(c % 4 + 1) * P], chunk(kn, c), chunk(qn, c), start=True, stop=True)
                last.then_inc(dl["qk"], 1)
            elif step[:2] == "t0":
                half = int(step[2])
                pe.wait_ge(dl["t0t"], two + (half + 1))
                pe.wait_ge(dl["kdec"], two + (half + 1))
                for c in range(4 * half, 4 * half + 4):
                    last = tr(bank[X0 + half][:, (c % 4) * P:(c % 4 + 1) * P], chunk(inv_t, c), ident[:, :])
                last.then_inc(dl["t0"], 1)
            elif step[0] in "ydt" and step[1] in "123456":
                level, half = int(step[1]), int(step[2])
                n = h * 12 + (2 * (level - 1) + half)
                if step[0] == "y":
                    if level == 1:
                        pe.wait_ge(dl["t0c"], two + (half + 1))
                        pe.wait_ge(dl["a"], two + 2)
                    for c in range(4 * half, 4 * half + 4):
                        last = mm(compact(bank[Y0 + half], c % 4, level), chunk(neg_a, c),
                                  left(inv[:, :].rearrange("p (c t) -> p c t", t=P), level)[:, c], start=True, stop=True)
                    last.then_inc(dl["y"], 1)
                elif step[0] == "d":
                    pe.wait_ge(dl["yc"], n + 1)
                    if level > 1:
                        pe.wait_ge(dl["ttc"], n - 1)
                    else:
                        pe.wait_ge(dl["pt"], two + (half + 1))
                    for c in range(4 * half, 4 * half + 4):
                        last = mm(bank[Z0 + half][:, (c % 4) * 64:(c % 4 + 1) * 64], chunk(inv_t, c),
                                  half_way[:, c * 64:(c + 1) * 64], start=True, stop=True)
                    last.then_inc(dl["dt"], 1)
                else:
                    pe.wait_ge(dl["dtm"], n + 1)
                    for c in range(4 * half, 4 * half + 4):
                        last = tr(bank[X0 + half][:, (c % 4) * P:(c % 4 + 1) * P], chunk(inv, c), ident[:, :])
                    last.then_inc(dl["tt"], 1)
            elif step[:2] == "ub":
                half = int(step[2])
                pe.wait_ge(dl["ttc"], h * 12 + (11 + half))
                for c in range(4 * half, 4 * half + 4):
                    last = mm(bank[Y0 + half][:, (c % 4) * P:(c % 4 + 1) * P], chunk(inv_t, c), chunk(beta_v, c),
                              start=True, stop=True)
                last.then_inc(dl["ub"], 1)
            elif step[:2] == "wt":
                half = int(step[2])
                for c in range(4 * half, 4 * half + 4):
                    last = mm(bank[Z0 + half][:, (c % 4) * P:(c % 4 + 1) * P], chunk(beta_k, c), chunk(inv_t, c),
                              start=True, stop=True)
                last.then_inc(dl["wt"], 1)
            elif step[0] == "a":
                c = int(step[1])
                n = h * NCH + c
                if c == 0:
                    pe.wait_ge(dl["ubc"], two + 2)
                    pe.wait_ge(dl["wtc"], two + 2)
                    pe.wait_ge(dl["qdec"], h + 1)
                    pe.wait_ge(dl["zero"], h + 1)
                else:
                    pe.wait_ge(dl["sup"], n)
                mm(bank[X0][:, 0:P], chunk(w_t, c), state[:, :], start=True, stop=True).then_inc(dl["ws"], 1)
                mm(bank[Y0 + c // 4][:, (c % 4) * P:(c % 4 + 1) * P], state[:, :], chunk(row[1], c), start=True, stop=False)
            elif step[0] == "b":
                c = int(step[1])
                pe.wait_ge(dl["u"], h * NCH + (c + 1))
                mm(bank[X1][:, 0:P], chunk(k_dec, c), u_now[:, :], start=True, stop=True).then_inc(dl["s"], 1)
                mm(bank[Y0 + c // 4][:, (c % 4) * P:(c % 4 + 1) * P], u_now[:, :], chunk(decay, c),
                   start=False, stop=True).then_inc(dl["o"], 1)
            elif step == "on":
                for half in range(2):
                    pe.wait_ge(dl["osq"], two + (half + 1))
                    mm(bank[Z0 + half][:, :], ones[:, :], o_sq[:, half * HALF:(half + 1) * HALF],
                       start=True, stop=True).then_inc(dl["oss"], 1)

        def delta_act(act, h, step):
            f = nc.scalar.activation
            two = h * 2
            if step == "sq":
                for i in range(2):
                    act.wait_ge(dl["silu"], h * 3 + (i + 1))
                    wait(act, dl["normed"], two)
                    f(sq[i][:, :], qkv[i][:, :], ACT.Square).then_inc(dl["sq"], 1)
                wait(act, dl["stored"], h * 16)
                act.wait_ge(dl["read"], h * 8 + 8)
                f(z_now[:, :], z_next[:, :], ACT.Copy).then_inc(dl["z"], 1)
            elif step == "ss":
                for i in range(2):
                    act.wait_ge(dl["ss"], two + (i + 1))
                    for half in range(2):
                        f(sq[i][:, half * HALF:(half + 1) * HALF], bank[(X0, Y0)[i] + half][:, :], ACT.Ln, bias=EPS)
                    act.drain()
                    f(sq[i][:, :], sq[i][:, :], ACT.Exp, scale=-0.5).then_inc(dl["ln"], 1)
                act.wait_ge(dl["diff"], h + 1)
                f(decay[:, :], decay[:, :], ACT.Exp).then_inc(dl["dec"], 1)
            elif step[:2] == "t0":
                half = int(step[2])
                act.wait_ge(dl["t0"], two + (half + 1))
                f(c4(inv, half), bank[X0 + half][:, :].rearrange("p (c t) -> p c t", t=P), ACT.Copy).then_inc(dl["t0c"], 1)
            elif step[0] in "yt" and step[1] in "123456":
                level, half = int(step[1]), int(step[2])
                n = h * 12 + (2 * (level - 1) + half)
                if step[0] == "y":
                    act.wait_ge(dl["y"], n + 1)
                    f(half_way[:, half * 256:half * 256 + 256], bank[Y0 + half][:, 0:256], ACT.Copy).then_inc(dl["yc"], 1)
                else:
                    act.wait_ge(dl["tt"], n + 1)
                    f(inv_t[:, half * HALF:(half + 1) * HALF], bank[X0 + half][:, :], ACT.Copy).then_inc(dl["ttc"], 1)
            elif step[:2] == "ub":
                half = int(step[2])
                act.wait_ge(dl["ub"], two + (half + 1))
                f(u_bar[:, half * HALF:(half + 1) * HALF], bank[Y0 + half][:, :], ACT.Copy).then_inc(dl["ubc"], 1)
            elif step in ("b3", "b7"):
                half = int(step[1]) // 4
                act.wait_ge(dl["o"], h * NCH + (4 * half + 4))
                f(o_raw[:, half * HALF:(half + 1) * HALF], bank[Y0 + half][:, :], ACT.Copy)
                f(o_sq[:, half * HALF:(half + 1) * HALF], bank[Y0 + half][:, :], ACT.Square).then_inc(dl["osq"], 1)
            elif step == "on":
                if not isinstance(h, int):
                    load_rows(act, h + 1)
                for half in range(2):
                    act.wait_ge(dl["oss"], two + (half + 1))
                    f(o_sq[:, half * HALF:(half + 1) * HALF], bank[Z0 + half][:, :], ACT.Ln, scale=1.0 / P, bias=EPS)
                    act.drain()
                    f(o_sq[:, half * HALF:(half + 1) * HALF], o_sq[:, half * HALF:(half + 1) * HALF], ACT.Exp,
                      scale=-0.5).then_inc(dl["oln"], 1)
            elif step == "end":
                act.wait_ge(dl["out"], h + 1)
                act.dma_start(scr_branch[ds(h * P + NSLOT * P, P), :], z_now[:, :]).then_inc(dl["stored"], 16)

        def delta_vec(dve, h, step):
            v = nc.vector
            two = h * 2

            def b4(kind, half):
                return col[:, 4 * half:4 * half + 4, kind:kind + 1].broadcast_to([P, 4, P])

            if step == "sq":
                v.tensor_copy(col[:, :, :], per_token[:, :, :, ds(h, 1)].rearrange("p c k a -> p c (k a)"))
                dve.wait_ge(dl["rows"], h * 48 + 48)
                v.tensor_copy(decay_all[:, :], row[1][:, P - 1:S:P])
                dve.drain()
                c8 = decay[:, :].rearrange("p (c t) -> p c t", t=P)
                v.tensor_tensor(c8, c8, col[:, :, 0:1].broadcast_to([P, NCH, P]), ALU.subtract)
                dve.drain()
                v.scalar_tensor_tensor(c8, c8, 0.0, neg_upper[:, :].unsqueeze(1).broadcast_to([P, NCH, P]),
                                       ALU.min, ALU.add).then_inc(dl["diff"], 1)
                a8 = neg_a[:, :].rearrange("p (c t) -> p c t", t=P)
                v.tensor_tensor(a8, a8, strict_up[:, :].unsqueeze(1).broadcast_to([P, NCH, P]), ALU.mult)
                wait(dve, dl["s"], h * NCH)
                v.memset(state[:, :], 0.0).then_inc(dl["zero"], 1)
                v.tensor_copy(inv_t[:, :].rearrange("p (c t) -> p c t", t=P),
                              ident[:, :].unsqueeze(1).broadcast_to([P, NCH, P]))
                dve.drain()
            elif step == "ss":
                dve.wait_ge(dl["ln"], two + 1)
                v.scalar_tensor_tensor(qn[:, :], qkv[0][:, :], float(P) ** -0.5, sq[0][:, :], ALU.mult,
                                       ALU.mult).then_inc(dl["normed"], 1)
                dve.wait_ge(dl["ln"], two + 2)
                v.tensor_tensor(kn[:, :], qkv[1][:, :], sq[1][:, :], ALU.mult).then_inc(dl["normed"], 1)
                dve.wait_ge(dl["dec"], h + 1)
                v.tensor_tensor(neg_a[:, :], neg_a[:, :], decay[:, :], ALU.mult)
                dve.drain()
            elif step[:2] == "vt":
                half = int(step[2])
                dve.wait_ge(dl["vt"], two + (half + 1))
                if half == 0:
                    wait(dve, dl["out"], h)
                v.tensor_tensor(c4(beta_v, half), bank[Z0 + half][:, :].rearrange("p (c t) -> p c t", t=P),
                                b4(1, half), ALU.mult).then_inc(dl["bv"], 1)
            elif step[:2] == "kt":
                half = int(step[2])
                dve.wait_ge(dl["kt"], two + (half + 1))
                src = bank[X0 + half][:, :].rearrange("p (c t) -> p c t", t=P)
                v.tensor_tensor(c4(beta_k, half), src, b4(2, half), ALU.mult)
                v.tensor_tensor(c4(k_dec, half), src, b4(3, half), ALU.mult).then_inc(dl["kdec"], 1)
            elif step[:2] == "kk":
                half = int(step[2])
                hs = slice(half * HALF, (half + 1) * HALF)
                dve.wait_ge(dl["kk"], two + (half + 1))
                v.tensor_tensor(neg_a[:, hs], bank[Y0 + half][:, :], neg_a[:, hs], ALU.mult).then_inc(dl["a"], 1)
                dve.drain()
                v.copy_predicated(c4(inv_t, half), merge_mask[:, 0:1, :].broadcast_to([P, 4, P]),
                                  c4(neg_a, half)).then_inc(dl["t0t"], 1)
            elif step[:2] == "qk":
                half = int(step[2])
                hs = slice(half * HALF, (half + 1) * HALF)
                dve.wait_ge(dl["qk"], two + (half + 1))
                v.tensor_tensor(decay[:, hs], bank[Z0 + half][:, :], decay[:, hs], ALU.mult).then_inc(dl["pt"], 1)
                if half == 1:
                    v.tensor_tensor(row[1][:, :], row[1][:, :], qn[:, :], ALU.mult).then_inc(dl["qdec"], 1)
            elif step[0] == "d" and step[1] in "123456":
                level, half = int(step[1]), int(step[2])
                n = h * 12 + (2 * (level - 1) + half)
                wait_alone(dve, dl["dt"], n + 1)
                v.copy_predicated(left(c4(inv, half), level),
                                  left(merge_mask[:, level:level + 1, :].broadcast_to([P, 4, P]), level),
                                  bank[Z0 + half][:, 0:256].rearrange("p (c n b) -> p c n b", c=4,
                                                                      b=1 << level)).then_inc(dl["dtm"], 1)
            elif step[:2] == "wt":
                half = int(step[2])
                dve.wait_ge(dl["wt"], two + (half + 1))
                v.tensor_copy(w_t[:, half * HALF:(half + 1) * HALF], bank[Z0 + half][:, :]).then_inc(dl["wtc"], 1)
            elif step[0] == "a":
                c = int(step[1])
                dve.wait_ge(dl["ws"], h * NCH + (c + 1))
                if c == 0:
                    dve.wait_ge(dl["ubc"], two + 2)
                v.tensor_tensor(u_now[:, :], chunk(u_bar, c), bank[X0][:, 0:P], ALU.subtract).then_inc(dl["u"], 1)
            elif step[0] == "b":
                c = int(step[1])
                dve.wait_ge(dl["s"], h * NCH + (c + 1))
                v.scalar_tensor_tensor(state[:, :], state[:, :], decay_all[:, c:c + 1], bank[X1][:, 0:P],
                                       ALU.mult, ALU.add).then_inc(dl["sup"], 1)
            elif step == "on":
                for half in range(2):
                    hs = slice(half * HALF, (half + 1) * HALF)
                    dve.wait_ge(dl["oln"], two + (half + 1))
                    v.scalar_tensor_tensor(o_raw[:, hs], o_raw[:, hs], dn_norm_c[:, 0:1], o_sq[:, hs], ALU.mult, ALU.mult)
                dve.drain()
                dve.wait_ge(dl["z"], h + 1)
                v.tensor_tensor(z_now[:, :], o_raw[:, :], z_now[:, :], ALU.mult).then_inc(dl["out"], 1)

        def dense_delta_pe(pe, h, j):
            i, half, k = j // 16, j // 8 % 2, j % 8
            m = 4 * h + i
            free = (dl["read"], m * 2 + (half - 1))
            if isinstance(h, int) and i == 0:
                free = (dense_read, 2 * 9 * NSLOT - 1 + half)
            dense_k(pe, ph["delta"], h, i, half, k, KT, D0 + half, act_in, free)

        def dense_delta_act(act, h, j):
            if j % 8 != 7:
                return
            i, half = j // 16, j // 8 % 2
            f = nc.scalar.activation
            act.wait_ge(projected, done(ph["delta"], h, i, half))
            if i == 3:
                if half == 0:
                    wait(act, dl["z"], h)
                    if isinstance(h, int):
                        act.wait_ge(consts, 4)
                f(z_next[:, half * HALF:(half + 1) * HALF], bank[D0 + half][:, :], ACT.Silu).then_inc(dl["read"], 1)
                return
            if half == 0:
                wait(act, dl["conv"], h * 3 + (i - 1))
            f(conv_in[i % 2][:, 3 + half * HALF:3 + (half + 1) * HALF], bank[D0 + half][:, :],
              ACT.Copy).then_inc(dl["read"], 1)

        def silu_delta_act(act, h, i):
            act.wait_ge(dl["conv"], h * 3 + (i + 1))
            if i < 2:
                wait(act, dl["normed"], h * 2 - 2 + (i + 1) if isinstance(h, int) else h * 2 + (i - 1))
            else:
                wait(act, dl["vt"], h * 2)
            nc.scalar.activation(qkv[i][:, :], conv_out[:, :], ACT.Silu).then_inc(dl["silu"], 1)

        def conv_vec(dve, h, i, j):
            v = nc.vector
            if j == 0:
                dve.wait_ge(dl["read"], h * 8 + (2 * i + 2))
                wait(dve, dl["silu"], h * 3 + i)
            else:
                dve.drain()
            tap = conv_c[:, j, ds(h + i * NHB, 1)]
            if j == 0:
                v.tensor_scalar(conv_out[:, :], conv_in[i % 2][:, 0:S], tap, None, ALU.mult)
            else:
                last = v.scalar_tensor_tensor(conv_out[:, :], conv_in[i % 2][:, j:j + S], tap, conv_out[:, :],
                                              ALU.mult, ALU.add)
            if j == 3:
                last.then_inc(dl["conv"], 1)

        def delta_iteration(eng, h, dense, conv, silu, side, mix=None):
            for j in range(64):
                dense(eng, h, j)
                if mix is not None:
                    attention_end(eng, side, mix, j)
                else:
                    for s_ in STEPS_AT.get(j, ()):
                        side(eng, h - 1, s_)
                if j in TAPS_AT:
                    conv(eng, h, *TAPS_AT[j])
                if j in SILU_AT:
                    silu(eng, h, SILU_AT[j])

        def delta_heads(eng, dense, conv, silu, side):
            with eng.Fori(1, NHB) as h:
                delta_iteration(eng, h, dense, conv, silu, side)

        def delta_end(eng, gate, side):
            for j in range(64):
                gates_peeled(eng, gate, j)
                for s_ in STEPS_AT.get(j, ()):
                    side(eng, NHB - 1, s_)

        def load_rows(act, h):
            wait(act, dl["o"], h * NCH)
            if isinstance(h, int):
                act.wait_ge(rows_stored, 48)
            for j in range(3):
                src = scr_rows[j][ds(h, 1), :] if not isinstance(h, int) else scr_rows[j][h:h + 1, :]
                act.dma_start(row[j][:, :], src.rearrange("a t -> (a t)").partition_broadcast(P)).then_inc(dl["rows"], 16)

        def delta_sp(sp):
            with sp.Fori(0, NHB) as h:
                for i, c in enumerate((COL_QD, COL_KD, COL_VD, COL_Z)):
                    load_weights(sp, ph["delta"], h, i, w_cols(w_in2, h * P + c))

        x_tile = [at(f"x_tile{i}", [P, KT, P], F32, work + 4096 * i) for i in range(2)]
        sq_sum = at("sq_sum", [P, S], F32, work + 8192)
        sq_now = at("sq_now", [P, S], F32, work + 12288)
        rms = at("rms", [P, S], F32, work + 16384)
        scaled_h = [at(f"scaled_h{i}", [P, S], F32, work + 20480 + 4096 * i) for i in range(2)]
        x_here = [sem(f"x_here{i}") for i in range(2)]
        h_squared, h_summed = sem("h_squared"), sem("h_summed")
        n_sum, n_rms, n_scaled, n_high, n_low = sem("n_sum"), sem("n_rms"), sem("n_scaled"), sem("n_high"), sem("n_low")
        def out_sp(sp):
            def x_columns(it, i):
                sp.dma_start(x_tile[i][:, :, :],
                             x[0].rearrange("(c p) n -> p c n", p=P)[:, :, ds((it * 2 + i) * P, P)]).then_inc(x_here[i], 16)

            for i in range(2):
                load_weights(sp, ph["out"], 0, i, w_cols(w_out[0], i * P))
            sp.wait_ge(projected, done(ph["merge"], KT - 1, 1, 1))
            for i in range(2):
                x_columns(0, i)
            with sp.Fori(1, KT // 2) as it:
                for i in range(2):
                    load_weights(sp, ph["out"], it, i, w_cols(w_out[0], (it * 2 + i) * P))
                    sp.wait_ge(projected, done(ph["out"], it - 1, i, 1))
                    x_columns(it, i)

        def out_pe(pe):
            def step(it):
                for i in range(2):
                    for half in range(2):
                        for k in range(KT):
                            free = (h_squared, it * 4 + (half + 2 * i - 3))
                            if isinstance(it, int):
                                free = (m_prod, 4 * KT - 3 + 2 * i + half)
                                if i == 0 and half == 0:
                                    pe.wait_ge(m_low, k + 1)
                            dense_k(pe, ph["out"], it, i, half, k, KT, OB[i][half], act_in, free, closed=False)
                        if half == 0:
                            pe.wait_ge(x_here[i], it * 16 + 16)
                        for c in range(4):
                            last = nc.tensor.matmul(bank[OB[i][half]][:, c * P:(c + 1) * P], x_tile[i][:, 4 * half + c, :],
                                                    ident[:, :], start=False, stop=c == 3)
                        last.then_inc(projected, 1)

            step(0)
            with pe.Fori(1, KT // 2) as it:
                step(it)

        def out_act(act):
            def step(it):
                for i in range(2):
                    for half in range(2):
                        act.wait_ge(projected, done(ph["out"], it, i, half))
                        hs = slice(half * HALF, (half + 1) * HALF)
                        b = bank[OB[i][half]]
                        nc.scalar.activation(h_t[:, ds(it * 2 + i, 1), hs].rearrange("p a t -> p (a t)"), b[:, :], ACT.Copy)
                        wait(act, h_summed, it * 4 + (half + 2 * i - 1))
                        nc.scalar.activation(sq_now[:, hs], b[:, :], ACT.Square).then_inc(h_squared, 1)

            step(0)
            with act.Fori(1, KT // 2) as it:
                step(it)

        def out_vec(dve):
            v = nc.vector
            v.memset(sq_sum[:, :], 0.0)
            dve.drain()
            with dve.Fori(0, KT // 2) as it:
                for i in range(2):
                    for half in range(2):
                        hs = slice(half * HALF, (half + 1) * HALF)
                        dve.wait_ge(h_squared, it * 4 + (half + 2 * i + 1))
                        v.tensor_tensor(sq_sum[:, hs], sq_sum[:, hs], sq_now[:, hs], ALU.add).then_inc(h_summed, 1)
                        dve.drain()

        def norm_pe(pe, count):
            pe.wait_ge(h_summed, count)
            for half in range(2):
                last = nc.tensor.matmul(bank[X0 + half][:, :], ones[:, :], sq_sum[:, half * HALF:(half + 1) * HALF],
                                        start=True, stop=True)
            last.then_inc(n_sum, 1)

        def norm_act(act, number):
            act.wait_ge(n_sum, number)
            for half in range(2):
                nc.scalar.activation(rms[:, half * HALF:(half + 1) * HALF], bank[X0 + half][:, :], ACT.Ln,
                                     scale=1.0 / D, bias=EPS)
            act.drain()
            nc.scalar.activation(rms[:, :], rms[:, :], ACT.Exp, scale=-0.5).then_inc(n_rms, 1)

        def norm_split_act(act):
            for k in range(KT):
                act.wait_ge(n_scaled, k + 1)
                nc.scalar.activation(act_in[0][:, k, :], scaled_h[k % 2][:, :], ACT.Copy).then_inc(n_high, 1)

        def norm_split_vec(dve):
            v = nc.vector
            dve.wait_ge(n_rms, 1)
            for k in range(KT + 1):
                if k < KT:
                    v.scalar_tensor_tensor(scaled_h[k % 2][:, :], h_t[:, k, :], norm_ffn_c[:, k:k + 1], rms[:, :],
                                           ALU.mult, ALU.mult).then_inc(n_scaled, 1)
                if k:
                    dve.wait_ge(n_high, k)
                    v.tensor_tensor(act_in[1][:, k - 1, :], scaled_h[(k - 1) % 2][:, :],
                                    act_in[0][:, k - 1, :].bitcast(F32), ALU.subtract).then_inc(n_low, 1)
                    dve.drain()

        ff = {x_: sem("ff_" + x_) for x_ in ("silu", "mult", "high", "low", "added")}
        FF_BEFORE = [0]
        for n_ in FF_CHUNKS:
            FF_BEFORE.append(FF_BEFORE[-1] + n_)

        def ffn_sp(sp):
            for c, n in enumerate(FF_CHUNKS):
                with sp.Fori(0, n) as j:
                    for i, w in enumerate((w_gate[0], w_up[0])):
                        load_weights(sp, ph[f"up{c}"], j, i, w_cols(w, (j + FF_BEFORE[c]) * P))
                with sp.Fori(0, KT // 2) as it:
                    for i in range(2):
                        rows_ = w_down[0][FF_BEFORE[c] * P:FF_BEFORE[c + 1] * P, :]
                        load_weights(sp, ph[f"down{c}"], it, i, w_cols(rows_, (it * 2 + i) * P, n))

        def ffn_pool(pool):
            for c, n in enumerate(FF_CHUNKS):
                with pool.Fori(0, n) as j:
                    split_weights(pool, ph[f"up{c}"], j, 0)
                    split_weights(pool, ph[f"up{c}"], j, 1)
                with pool.Fori(0, KT // 2) as it:
                    split_weights(pool, ph[f"down{c}"], it, 0, n)
                    split_weights(pool, ph[f"down{c}"], it, 1, n)

        def ffn_pe(pe):
            for c, n in enumerate(FF_CHUNKS):
                b = FF_BEFORE[c]

                def up(j):
                    for half in range(2):
                        for k in range(KT):
                            if c == 0 and isinstance(j, int) and half == 0:
                                pe.wait_ge(n_low, k + 1)
                            free = (ff["silu"], (j + b) * 2 + (half - 1))
                            if isinstance(j, int) and j == 0 and c:
                                wait(pe, ff["added"], 16 * c)
                            dense_k(pe, ph[f"up{c}"], j, 0, half, k, KT, D0 + half, act_in, free)
                    for half in range(2):
                        for k in range(KT):
                            dense_k(pe, ph[f"up{c}"], j, 1, half, k, KT, Y0 + half, act_in,
                                    (ff["mult"], (j + b) * 2 + (half - 1)))

                up(0)
                with pe.Fori(1, n) as j:
                    up(j)

                def down(it):
                    for i in range(2):
                        for half in range(2):
                            for k in range(n):
                                if isinstance(it, int) and i == 0 and half == 0:
                                    pe.wait_ge(ff["low"], (b + k + 1) * 2)
                                m = 16 * c + it * 4
                                free = (ff["added"], it * 4 + (16 * c + half + 2 * i - 3)) if not (isinstance(it, int) and it == 0) \
                                    else (ff["mult"], (b + n) * 2)
                                dense_k(pe, ph[f"down{c}"], it, i, half, k, n, OB[i][half], v_region, free)

                down(0)
                with pe.Fori(1, KT // 2) as it:
                    down(it)

        def ffn_act(act):
            def up(b, c, j):
                for half in range(2):
                    hs = slice(half * HALF, (half + 1) * HALF)
                    m = (j + b) * 2 + half
                    act.wait_ge(projected, done(ph[f"up{c}"], j, 0, half))
                    wait(act, ff["mult"], m - 1)
                    nc.scalar.activation(tmp[0][:, hs], bank[D0 + half][:, :], ACT.Silu).then_inc(ff["silu"], 1)
                if c and isinstance(j, int) and j == 0:
                    act.wait_ge(projected, done(ph[f"down{c - 1}"], KT // 2 - 1, 1, 1))
                for half in range(2):
                    hs = slice(half * HALF, (half + 1) * HALF)
                    m = (j + b) * 2 + half
                    act.wait_ge(ff["mult"], m + 1)
                    nc.scalar.activation(v_region[0][:, ds(j, 1), hs].rearrange("p a t -> p (a t)"), tmp[1][:, hs],
                                         ACT.Copy).then_inc(ff["high"], 1)

            for c, n in enumerate(FF_CHUNKS):
                up(FF_BEFORE[c], c, 0)
                with act.Fori(1, n) as j:
                    up(FF_BEFORE[c], c, j)

        def ffn_vec(dve):
            v = nc.vector

            def up(b, c, j):
                for half in range(2):
                    hs = slice(half * HALF, (half + 1) * HALF)
                    m = (j + b) * 2 + half
                    dve.wait_ge(ff["silu"], m + 1)
                    dve.wait_ge(projected, done(ph[f"up{c}"], j, 1, half))
                    wait(dve, ff["high"], m - 1)
                    v.tensor_tensor(tmp[1][:, hs], tmp[0][:, hs], bank[Y0 + half][:, :], ALU.mult).then_inc(ff["mult"], 1)
                for half in range(2):
                    hs = slice(half * HALF, (half + 1) * HALF)
                    m = (j + b) * 2 + half
                    dve.wait_ge(ff["high"], m + 1)
                    v.tensor_tensor(v_region[1][:, ds(j, 1), hs].rearrange("p a t -> p (a t)"), tmp[1][:, hs],
                                    v_region[0][:, ds(j, 1), hs].rearrange("p a t -> p (a t)").bitcast(F32),
                                    ALU.subtract).then_inc(ff["low"], 1)
                dve.drain()

            def down(c, it):
                for i in range(2):
                    for half in range(2):
                        dve.wait_ge(projected, done(ph[f"down{c}"], it, i, half))
                        hf = h_t[:, ds(it * 2 + i, 1), half * HALF:(half + 1) * HALF].rearrange("p a t -> p (a t)")
                        v.tensor_tensor(hf, hf, bank[OB[i][half]][:, :], ALU.add).then_inc(ff["added"], 1)

            for c, n in enumerate(FF_CHUNKS):
                up(FF_BEFORE[c], c, 0)
                with dve.Fori(1, n) as j:
                    up(FF_BEFORE[c], c, j)
                with dve.Fori(0, KT // 2) as it:
                    down(c, it)

        out_rows = [at(f"out_rows{i}", [P, D], F32, work + 28672 + 4096 * i) for i in range(2)]
        f_sq, f_scaled, f_turned, f_copied, f_stored = sem("f_sq"), sem("f_scaled"), sem("f_turned"), sem("f_copied"), [sem(f"f_stored{i}") for i in range(2)]

        def final_act(act):
            for k in range(KT):
                if k == 0:
                    act.wait_ge(ff["added"], 16 * len(FF_CHUNKS))
                wait(act, h_summed, 4 * KT // 2 + k)
                nc.scalar.activation(sq_now[:, :], h_t[:, k, :], ACT.Square).then_inc(f_sq, 1)
            norm_act(act, 2)
            for c in range(KT):
                act.wait_ge(f_turned, 2 * c + 1)
                if c >= 2:
                    act.wait_ge(f_stored[c % 2], 16 * (c // 2))
                nc.scalar.activation(out_rows[c % 2][:, 0:HALF], bank[D0][:, :], ACT.Copy).then_inc(f_copied, 1)

        f_copied_v = sem("f_copied_v")

        def final_vec(dve):
            v = nc.vector
            dve.drain()
            v.memset(sq_sum[:, :], 0.0)
            dve.drain()
            for k in range(KT):
                dve.wait_ge(f_sq, k + 1)
                v.tensor_tensor(sq_sum[:, :], sq_sum[:, :], sq_now[:, :], ALU.add).then_inc(h_summed, 1)
                dve.drain()
            dve.wait_ge(n_rms, 2)
            for k in range(KT):
                v.scalar_tensor_tensor(h_t[:, k, :], h_t[:, k, :], norm_final_c[:, k:k + 1], rms[:, :],
                                       ALU.mult, ALU.mult).then_inc(f_scaled, 1)
            for c in range(KT):
                dve.wait_ge(f_turned, 2 * c + 2)
                if c >= 2:
                    dve.wait_ge(f_stored[c % 2], 16 * (c // 2))
                v.tensor_copy(out_rows[c % 2][:, HALF:D], bank[D1][:, :]).then_inc(f_copied_v, 1)

        def final_pe(pe):
            norm_pe(pe, 4 * KT // 2 + KT)
            for c in range(KT):
                for half in range(2):
                    if c == 0:
                        pe.wait_ge(f_scaled, 4 * half + 4)
                    else:
                        pe.wait_ge((f_copied, f_copied_v)[half], c)
                    for f in range(4):
                        last = nc.tensor.transpose(bank[D0 + half][:, f * P:(f + 1) * P],
                                                   h_t[:, 4 * half + f, c * P:(c + 1) * P], ident[:, :])
                    last.then_inc(f_turned, 1)

        def final_sp(sp):
            for c in range(KT):
                sp.wait_ge(f_copied, c + 1)
                sp.wait_ge(f_copied_v, c + 1)
                sp.dma_start(out[0, c * P:(c + 1) * P, :], out_rows[c % 2][:, :]).then_inc(f_stored[c % 2], 16)
            for i in range(2):
                sp.wait_ge(f_stored[i], 16 * (KT // 2))

        block = ctx.enter_context(nc.Block())

        @block.sync
        def _(sp):
            setup_sp(sp)
            attention_sp(sp)
            delta_sp(sp)
            gates_sp(sp)
            merge_sp(sp)
            out_sp(sp)
            ffn_sp(sp)
            final_sp(sp)

        @block.gpsimd
        def _(pool):
            pool.sem_inc(weights_split, FREE)
            then = pool_then(pool)
            setup_pool(pool, then)
            for i in range(9):
                split_weights(pool, ph["attn"], 0, i)
            mask_pool(pool, then)
            with pool.Fori(1, NSLOT) as s:
                for i in range(9):
                    split_weights(pool, ph["attn"], s, i)
            with pool.Fori(0, NHB) as h:
                for i in range(4):
                    split_weights(pool, ph["delta"], h, i)
            gates_pool(pool)
            merge_pool(pool)
            with pool.Fori(0, KT // 2) as it:
                for i in range(2):
                    split_weights(pool, ph["out"], it, i)
            ffn_pool(pool)

        @block.tensor
        def _(pe):
            setup_pe(pe)
            attention(pe, dense_att_pe, att_pe, nothing, decay_pe)
            delta_iteration(pe, 0, dense_delta_pe, nothing, nothing, att_pe, nothing)
            barrier(pe, 1)
            delta_heads(pe, dense_delta_pe, nothing, nothing, delta_pe)
            delta_end(pe, gate_step_pe, delta_pe)
            barrier(pe, 2)
            gates_pe(pe)
            merge_pe(pe)
            out_pe(pe)
            norm_pe(pe, 4 * KT // 2)
            ffn_pe(pe)
            final_pe(pe)

        @block.scalar
        def _(act):
            setup_act(act)
            attention(act, dense_att_act, att_act, mix_act_engine, decay_act)
            delta_iteration(act, 0, dense_delta_act, nothing, silu_delta_act, att_act, mix_act_engine)
            barrier(act, 1)
            load_rows(act, 0)
            delta_heads(act, dense_delta_act, nothing, silu_delta_act, delta_act)
            delta_end(act, gate_step_act, delta_act)
            barrier(act, 2)
            gates_act(act)
            merge_act(act)
            out_act(act)
            norm_act(act, 1)
            norm_split_act(act)
            ffn_act(act)
            final_act(act)

        @block.vector
        def _(dve):
            setup_vec(dve)
            dve.wait_ge(consts, 3)
            attention(dve, nothing, att_vec, mix_vec_engine, decay_vec)
            dve.wait_ge(projected, done(ph["attn"], NSLOT - 1, 8, 1))
            for i in range(2):
                nc.vector.memset(conv_in[i][:, 0:3], 0.0)
            dve.wait_ge(conv_loaded, 64)
            delta_iteration(dve, 0, nothing, conv_vec, nothing, att_vec, mix_vec_engine)
            dve.wait_ge(consts, 4)
            barrier(dve, 1)
            delta_heads(dve, nothing, conv_vec, nothing, delta_vec)
            delta_end(dve, nothing, delta_vec)
            barrier(dve, 2)
            gates_vec(dve)
            merge_vec(dve)
            out_vec(dve)
            norm_split_vec(dve)
            ffn_vec(dve)
            final_vec(dve)


INS = ["x", "norm_mix", "w_in", "conv_w", "a_log", "dt_bias", "dn_norm", "w_proj_attn", "w_proj_delta",
       "w_out", "norm_ffn", "w_gate", "w_up", "w_down", "norm_final"]


def kernel(**inputs):
    import concourse.bacc as bacc
    from concourse.bass_utils import run_bass_kernel_spmd

    nc = bacc.Bacc("TRN2", target_bir_lowering=False, num_devices=1)
    arrays, args = {}, []
    for name in INS:
        a = np.ascontiguousarray(inputs[name])
        arrays[f"in_{name}"] = a
        args.append(nc.dram_tensor(f"in_{name}", a.shape, mybir.dt.from_np(a.dtype), kind="ExternalInput").ap())
    out = nc.dram_tensor("out", (1, S, D), F32, kind="ExternalOutput").ap()
    build(nc, *args, out)
    r = run_bass_kernel_spmd(nc, [arrays], core_ids=[0])
    return r.results[0]["out"]
```

```python
import math
from contextlib import ExitStack

import numpy as np

import concourse.bass as bass
from concourse import mybir

F32 = mybir.dt.float32
F32R = mybir.dt.float32r
I32 = mybir.dt.int32
U8 = mybir.dt.uint8
ALU = mybir.AluOpType
ACT = mybir.ActivationFunctionType
AXX = mybir.AxisListType.X
ds = bass.ds

P = 128
S = 1024
D = 1024
KT = D // P
HALF = 512
NSLOT = 4
DILATION = (1, 4, 16)
NHA = 12
NHB = 8
NCH = S // P
DFF = ((8 * D // 3 + 255) // 256) * 256
FF_CHUNKS = (8, 8, DFF // P - 16)
EPS = 1e-6
NEG = -1e30
D_ATTN = NHA * P
COL_QA, COL_KA, COL_VA = 0, D_ATTN, 2 * D_ATTN
COL_QD = 3 * D_ATTN
COL_KD, COL_VD, COL_Z = COL_QD + NHB * P, COL_QD + 2 * NHB * P, COL_QD + 3 * NHB * P
COL_BETA = COL_QD + 4 * NHB * P
COL_GATE = COL_BETA + 2 * NHB
FREE = 3
PASSES = ((0, 0), (0, 1), (1, 0))


def wait(eng, sem, value):
    if isinstance(value, int) and value <= 0:
        return
    eng.wait_ge(sem, value)


def build(nc, x, norm_mix, w_in, conv_w, a_log, dt_bias, dn_norm, w_proj_attn, w_proj_delta,
          w_out, norm_ffn, w_gate, w_up, w_down, norm_final, out):
    ctx = ExitStack()
    with ctx:
        place = [nc.sbuf_base + (-nc.sbuf_base) % 64]

        def at(name, shape, dt, offset):
            return nc.alloc_sbuf_tensor_at(name, shape, dt, offset=offset)

        passed = {}

        def wait_alone(eng, s_, value):
            if isinstance(value, int) and value <= 0:
                return
            eng.wait_ge(s_, value)
            if not isinstance(value, int):
                if eng not in passed:
                    passed[eng] = sem(f"passed{len(passed)}")
                eng.sem_inc(passed[eng], 1)

        def size_of(shape, dt):
            n = (1 if dt == U8 else 4) * int(np.prod(shape[1:]))
            return n + (-n) % 32

        def keep(name, shape, dt=F32):
            t = at(name, shape, dt, place[0])
            place[0] += size_of(shape, dt)
            return t

        def sem(name):
            return ctx.enter_context(nc.semaphore(name))

        ident = keep("ident", [P, P])
        ones = keep("ones", [P, P])
        band = keep("band", [P, 2, 256])
        band_pair = keep("band_pair", [P, P])
        neg_upper = keep("neg_upper", [P, P])
        strict_up = keep("strict_up", [P, P])
        merge_mask = keep("merge_mask", [P, 7, P], U8)
        slopes = keep("slopes", [P, NHA])
        norm_mix_c = keep("norm_mix_c", [P, KT])
        norm_ffn_c = keep("norm_ffn_c", [P, KT])
        norm_final_c = keep("norm_final_c", [P, KT])
        dn_norm_c = keep("dn_norm_c", [P, 1])
        conv_c = keep("conv_c", [P, 4, 3 * NHB])
        rate = keep("rate", [40, 4])
        per_token = keep("per_token", [P, NCH, 4, 32])

        raw, wpart = [], []
        for slot in range(2):
            raw.append(keep(f"raw{slot}", [P, KT, P]))
            wpart.append([keep(f"w_hi{slot}", [P, KT, P], F32R), keep(f"w_lo{slot}", [P, KT, P], F32R)])
        slot2 = place[0]
        raw.append(keep("raw2", [P, KT, P]))
        wpart.append([keep("w_hi2", [P, KT, P], F32R), keep("w_lo2", [P, KT, P], F32R)])
        tmp = [at(f"tmp{i}", [P, S], F32, slot2 + 4096 * i) for i in range(3)]

        act_in = [keep("u_hi", [P, KT, S], F32R), keep("u_lo", [P, KT, S], F32R)]
        work = place[0]
        v_region = [at("v_hi", [P, KT, S], F32R, work), at("v_lo", [P, KT, S], F32R, work + 32768)]
        NB = NSLOT + NHB
        branch = [at("b_hi", [P, NB, S], F32R, work), at("b_lo", [P, NB, S], F32R, work + 49152)]
        x_rows = at("x_rows", [P, KT, D], F32, work)
        h_t = at("h_t", [P, KT, S], F32, work + 65536)
        assert work + 98304 <= nc.sbuf_usable_end, (work, nc.sbuf_usable_end)

        bank = [ctx.enter_context(nc.psum_tensor(f"bank{i}", [P, HALF], F32)) for i in range(8)]
        D0, D1, X0, X1, Y0, Y1, Z0, Z1 = range(8)

        scr_stat = nc.dram_tensor("scr_stat", [3, 2 * S], F32).ap()
        scr_rows = nc.dram_tensor("scr_rows", [3, NHB, S], F32).ap()
        scr_branch = nc.dram_tensor("scr_branch", [(NSLOT + NHB) * P, S], F32).ap()
        scr_gate = nc.dram_tensor("scr_gate", [2 * D, S], F32).ap()

        raw_loaded = [sem(f"raw_loaded{i}") for i in range(3)]
        weights_split = sem("weights_split")
        projected = sem("projected")
        consts = sem("consts")
        const_step = sem("const_step")
        params = sem("params")
        conv_loaded = sem("conv_loaded")

        class Phase:
            def __init__(self, base, per, period, used):
                self.base, self.per, self.period, self.used = base, per, period, used

            def tile(self, it, i):
                return self.per * it + (self.base + i)

            def use(self, it, i):
                return (self.per // self.period) * it + (self.used + i // self.period + 1)

        order = [("attn", 9, NSLOT, 3), ("delta", 4, NHB, 2), ("gates", 2, KT, 2), ("merge", 2, KT, 2), ("out", 2, KT // 2, 2)]
        for c, n in enumerate(FF_CHUNKS):
            order += [(f"up{c}", 2, n, 2), (f"down{c}", 2, KT // 2, 2)]
        ph, base, used = {}, 0, 0
        for name, per, iters, period in order:
            ph[name] = Phase(base, per, period, used)
            base += per * iters
            used += per * iters // period

        def load_weights(sp, phase, it, i, src):
            n = phase.tile(it, i)
            wait_alone(sp, weights_split, n + (FREE - phase.period + 1))
            slot = i % phase.period
            sp.dma_start(raw[slot][:, 0:src.shape[1], :], src).then_inc(raw_loaded[slot], 16)

        def split_weights(pool, phase, it, i, kt=KT):
            n, slot = phase.tile(it, i), i % phase.period
            hi, lo = wpart[slot]
            pool.wait_ge(raw_loaded[slot], phase.use(it, i) * 16)
            wait_alone(pool, projected, n * 2 + 2 * (FREE - phase.period + 1))
            nc.gpsimd.tensor_copy(hi[:, 0:kt, :], raw[slot][:, 0:kt, :])
            pool.drain()
            nc.gpsimd.tensor_tensor(lo[:, 0:kt, :], raw[slot][:, 0:kt, :], hi[:, 0:kt, :].bitcast(F32),
                                    ALU.subtract).then_inc(weights_split, 1)

        def dense_k(pe, phase, it, i, half, k, kt, dst, rhs, free=None, closed=True):
            n, slot = phase.tile(it, i), i % phase.period
            if k == 0:
                if half == 0:
                    pe.wait_ge(weights_split, n + (FREE + 1))
                if free is not None:
                    wait(pe, *free)
            for wp, ap in PASSES:
                last = nc.tensor.matmul(bank[dst][:, :], wpart[slot][wp][:, k, :],
                                        rhs[ap][:, k, half * HALF:(half + 1) * HALF],
                                        start=k == 0 and (wp, ap) == PASSES[0],
                                        stop=closed and k == kt - 1 and (wp, ap) == PASSES[-1])
            if k == kt - 1 and closed:
                last.then_inc(projected, 1)

        def done(phase, it, i, half):
            return phase.tile(it, i) * 2 + (2 * FREE + half + 1)

        def w_cols(w, col, kt=KT):
            return w.rearrange("(k p) n -> p k n", p=P)[:, 0:kt, ds(col, P)]

        def flat(t):
            return t[:, :, :].rearrange("p a b -> p (a b)")

        w_in2, conv2 = w_in[0], conv_w[0]

        late = work + 57344
        rows = at("rows", [P, S], F32, late)
        row_t = [at(f"row_t{i}", [40, S], F32, late + 4096 + 4096 * i) for i in range(5)]
        reset = at("reset", [8, S], F32, late + 24576)
        w_ba = at("w_ba", [P, KT, P], F32, late - 12288)
        w_ba_part = [at("w_ba_hi", [P, KT, P], F32R, late - 8192), at("w_ba_lo", [P, KT, P], F32R, late - 4096)]
        blocks = at("blocks", [P, 8, P], F32, work + 92160)
        lvl_tmp = at("lvl_tmp", [P, P], F32, work + 91136)
        iota_i = at("iota_i", [P, P], I32, work + 91648)
        u_tmp = at("u_tmp", [P, 2, HALF], F32, work + 32768)
        xn = at("xn", [P, 2, D], F32, work + 36864)
        sq_scr = at("sq_scr", [P, D], F32, work + 86016)
        rstd = at("rstd", [P, KT], F32, work + 90112)
        ssum = at("ssum", [P, KT], F32, work + 90144)

        XB = ((X0, X1), (Y0, Y1))
        x_sq, x_rstd = sem("x_sq"), sem("x_rstd")
        x_scaled = sem("x_scaled")
        x_turned = sem("x_turned")
        x_weighted, x_high, x_low = sem("x_weighted"), sem("x_high"), sem("x_low")
        ba_split, ba_done, ba_act, ba_vec, ba_turned, rows_stored = (
            sem("ba_split"), sem("ba_done"), sem("ba_act"), sem("ba_vec"), sem("ba_turned"), sem("rows_stored"))
        ba_loaded, rate_loaded = sem("ba_loaded"), sem("rate_loaded")
        x_load = [sem(f"x_load{i}") for i in range(KT)]

        def setup_sp(sp):
            for c in range(2):
                sp.dma_start(x_rows[:, c, :], x[0, c * P:(c + 1) * P, :]).then_inc(x_load[c], 16)
            sp.wait_ge(consts, 1)
            for j in range(2):
                sp.dma_start(w_ba[:, :, 32 * j:32 * j + 8],
                             w_in2.rearrange("(k p) n -> p k n", p=P)[:, :, COL_BETA + 8 * j:COL_BETA + 8 * j + 8],
                             allow_slow_non_contiguous=True).then_inc(ba_loaded, 16)
            for c in range(2, 4):
                sp.dma_start(x_rows[:, c, :], x[0, c * P:(c + 1) * P, :]).then_inc(x_load[c], 16)
            for t, src in ((norm_mix_c, norm_mix[0]), (norm_ffn_c, norm_ffn[0]), (norm_final_c, norm_final)):
                sp.dma_start(t[:, :], src.rearrange("(f p) -> p f", p=P),
                             allow_slow_non_contiguous=True).then_inc(params, 16)
            sp.dma_start(dn_norm_c[:, :], dn_norm[0].rearrange("(p a) -> p a", a=1),
                         allow_slow_non_contiguous=True).then_inc(params, 16)
            for c in range(4, KT):
                sp.dma_start(x_rows[:, c, :], x[0, c * P:(c + 1) * P, :]).then_inc(x_load[c], 16)
            sp.dma_start(rate[32:40, 0:1], a_log[0].rearrange("(p a) -> p a", a=1),
                         allow_slow_non_contiguous=True).then_inc(rate_loaded, 16)
            sp.dma_start(rate[32:40, 2:3], dt_bias[0].rearrange("(p a) -> p a", a=1),
                         allow_slow_non_contiguous=True).then_inc(rate_loaded, 16)
            for j in range(4):
                sp.dma_start(conv_c[:, j, :], conv2[j].rearrange("(t p) -> p t", p=P),
                             allow_slow_non_contiguous=True).then_inc(conv_loaded, 16)

        def pool_then(pool):
            step = []

            def then(ins):
                step.append(1)
                ins.then_inc(const_step, 1)
                pool.wait_ge(const_step, len(step))
            return then

        def setup_pool(pool, then):
            g = nc.gpsimd
            then(g.memset(flat(w_ba), 0.0))
            g.memset(reset[:, :], 1.0).then_inc(consts, 1)
            then(g.memset(ones[:, :], 1.0))
            then(g.memset(ident[:, :], 0.0))
            then(g.affine_select(out=ident[:, :], in_=ident[:, :], compare_op=ALU.not_equal, fill=1.0, base=0,
                                 pattern=[[-1, P]], channel_multiplier=1))
            g.memset(neg_upper[:, :], 0.0).then_inc(consts, 1)
            then(g.iota(iota_i[:, :], pattern=[[1, P]], base=0, channel_multiplier=-1))
            then(g.tensor_copy(band[:, 1, P:256], iota_i[:, :]))
            then(g.affine_select(out=band[:, 1, P:256], in_=band[:, 1, P:256], compare_op=ALU.is_ge, fill=NEG,
                                 base=0, pattern=[[-1, P]], channel_multiplier=1))
            then(g.iota(iota_i[:, :], pattern=[[1, P]], base=-P, channel_multiplier=-1))
            then(g.tensor_copy(band[:, 1, 0:P], iota_i[:, :]))
            then(g.affine_select(out=band[:, 1, 0:P], in_=band[:, 1, 0:P], compare_op=ALU.is_ge, fill=NEG,
                                 base=0, pattern=[[1, P]], channel_multiplier=-1))
            then(g.memset(band[:, 0, 0:P], NEG))
            then(g.tensor_copy(band[:, 0, P:256], band[:, 1, P:256]))
            then(g.tensor_copy(band_pair[:, :], band[:, 1, P:256]))
            pair = band_pair[:, :].rearrange("p (b i) -> p b i", b=2)
            then(g.affine_select(out=pair, in_=pair, compare_op=ALU.is_ge, fill=NEG, base=63,
                                 pattern=[[64, 2], [0, 64]], channel_multiplier=-1))
            for h in range(NHA):
                g.memset(slopes[:, h:h + 1], float(2.0 ** (-8.0 * (h + 1) / NHA)) * DILATION[h // NSLOT])
            pool.drain().then_inc(consts, 1)
            for c in range(KT):
                for q in range(2):
                    pool.wait_ge(x_high, 2 * c + q + 1)
                    g.tensor_tensor(act_in[1][:, 4 * q:4 * q + 4, c * P:(c + 1) * P],
                                    u_tmp[:, q, :].rearrange("p (f t) -> p f t", t=P),
                                    act_in[0][:, 4 * q:4 * q + 4, c * P:(c + 1) * P].bitcast(F32),
                                    ALU.subtract).then_inc(x_low, 1)

        def mask_pool(pool, then):
            g = nc.gpsimd
            then(g.affine_select(out=neg_upper[:, :], in_=neg_upper[:, :], compare_op=ALU.is_ge, fill=NEG, base=0,
                                 pattern=[[1, P]], channel_multiplier=-1))
            then(g.affine_select(out=strict_up[:, :], in_=ones[:, :], compare_op=ALU.is_ge, fill=0.0, base=-1,
                                 pattern=[[1, P]], channel_multiplier=-1))
            for l in range(8):
                b = 1 << l
                v = blocks[:, l, :].rearrange("p (n b) -> p n b", b=b)
                then(g.memset(blocks[:, l, :], 1.0))
                then(g.affine_select(out=v, in_=v, compare_op=ALU.is_ge, fill=0.0, base=0,
                                     pattern=[[-b, P // b], [0, b]], channel_multiplier=1))
                then(g.affine_select(out=v, in_=v, compare_op=ALU.is_ge, fill=0.0, base=b - 1,
                                     pattern=[[b, P // b], [0, b]], channel_multiplier=-1))
            for l in range(7):
                then(g.tensor_tensor(lvl_tmp[:, :], blocks[:, l + 1, :], blocks[:, l, :], ALU.subtract))
                up = l == 0
                then(g.affine_select(out=lvl_tmp[:, :], in_=lvl_tmp[:, :], compare_op=ALU.is_ge, fill=0.0, base=0,
                                     pattern=[[1 if up else -1, P]], channel_multiplier=-1 if up else 1))
                then(g.tensor_copy(merge_mask[:, l, :], lvl_tmp[:, :]))
            pool.drain().then_inc(consts, 1)

        def setup_act(act):
            nc.scalar.preload_act_table_set("natural_log")

            def squares(c):
                act.wait_ge(x_load[c], 16)
                wait(act, x_sq, c)
                nc.scalar.activation(sq_scr[:, :], x_rows[:, c, :], ACT.Square,
                                     accum_out=ssum[:, c:c + 1]).then_inc(x_sq, 1)

            def roots(group):
                cs = slice(4 * group, 4 * group + 4)
                act.wait_ge(x_sq, 4 * group + 4)
                nc.scalar.activation(rstd[:, cs], ssum[:, cs], ACT.Ln, scale=1.0 / D, bias=EPS)
                act.drain()
                nc.scalar.activation(rstd[:, cs], rstd[:, cs], ACT.Exp, scale=-0.5).then_inc(x_rstd, 1)

            for c in range(4):
                squares(c)
            roots(0)
            for c in (4, 5):
                squares(c)
            for c in range(KT):
                for q in range(2):
                    act.wait_ge(x_weighted, 2 * c + q + 1)
                    nc.scalar.activation(act_in[0][:, 4 * q:4 * q + 4, c * P:(c + 1) * P],
                                         u_tmp[:, q, :].rearrange("p (f t) -> p f t", t=P),
                                         ACT.Copy).then_inc(x_high, 1)
                if c < 2:
                    squares(6 + c)
                if c == 1:
                    roots(1)

        def setup_vec(dve):
            v = nc.vector
            dve.wait_ge(params, 16 * 4)

            def scale(c):
                dve.wait_ge(x_rstd, c // 4 + 1)
                if c >= 2:
                    dve.wait_ge(x_turned, 2 * (c - 1))
                v.tensor_scalar(xn[:, c % 2, :], x_rows[:, c, :], rstd[:, c:c + 1], None,
                                ALU.mult).then_inc(x_scaled, 1)

            dve.wait_ge(ba_loaded, 32)
            v.tensor_copy(flat(w_ba_part[0]), flat(w_ba))
            dve.drain()
            v.tensor_tensor(flat(w_ba_part[1]), flat(w_ba), flat(w_ba_part[0]).bitcast(F32),
                            ALU.subtract).then_inc(ba_split, 1)
            scale(0)
            for c in range(KT):
                if c + 1 < KT:
                    scale(c + 1)
                for q in range(2):
                    dve.wait_ge(x_turned, 2 * c + q + 1)
                    if c:
                        dve.wait_ge(x_low, 2 * (c - 1) + q + 1)
                    v.tensor_tensor(u_tmp[:, q, :].rearrange("p (f t) -> p f t", t=P),
                                    bank[XB[c % 2][q]][:, :].rearrange("p (f t) -> p f t", t=P),
                                    norm_mix_c[:, 4 * q:4 * q + 4].unsqueeze(2).broadcast_to([P, 4, P]),
                                    ALU.mult).then_inc(x_weighted, 1)

        def setup_pe(pe):
            pe.sem_inc(projected, 2 * FREE)
            pe.wait_ge(consts, 2)

            def beta_decay(q, k):
                for wp, ap in PASSES:
                    last = nc.tensor.matmul(bank[Z0 + q][:, :], w_ba_part[wp][:, k, :],
                                            act_in[ap][:, k, q * HALF:(q + 1) * HALF],
                                            start=k == 0 and (wp, ap) == PASSES[0],
                                            stop=k == KT - 1 and (wp, ap) == PASSES[-1])
                if k == KT - 1:
                    last.then_inc(ba_done, 1)

            for c in range(KT):
                pe.wait_ge(x_scaled, c + 1)
                for q in range(2):
                    if c >= 2:
                        pe.wait_ge(x_weighted, 2 * (c - 2) + q + 1)
                    for f in range(4):
                        last = nc.tensor.transpose(bank[XB[c % 2][q]][:, f * P:(f + 1) * P],
                                                   xn[:, c % 2, (4 * q + f) * P:(4 * q + f + 1) * P], ident[:, :])
                    last.then_inc(x_turned, 1)
                if c >= KT // 2:
                    if c == KT // 2:
                        pe.wait_ge(ba_split, 1)
                        pe.wait_ge(x_low, KT)
                    for k in (2 * c - KT, 2 * c - KT + 1):
                        beta_decay(0, k)
            pe.wait_ge(x_low, 2 * KT)
            for k in range(KT):
                beta_decay(1, k)

        b8, a8 = slice(0, 8), slice(32, 40)

        def decay_act(act, j):
            f = nc.scalar.activation
            if j == 2:
                act.wait_ge(rate_loaded, 32)
                f(rate[a8, 1:2], rate[a8, 0:1], ACT.Exp).then_inc(ba_act, 1)
                act.wait_ge(ba_done, 2)
                for q in range(2):
                    f(row_t[0][:, q * HALF:(q + 1) * HALF], bank[Z0 + q][0:40, :], ACT.Copy).then_inc(ba_act, 1)
            elif j == 10:
                act.wait_ge(ba_vec, 1)
                f(row_t[1][b8, :], row_t[0][b8, :], ACT.Exp, scale=-1.0)
                f(row_t[1][a8, :], row_t[2][a8, :], ACT.Exp)
                act.drain()
                f(row_t[1][a8, :], row_t[1][a8, :], ACT.Ln, bias=1.0).then_inc(ba_act, 1)
            elif j == 38:
                act.wait_ge(ba_vec, 3)
                f(row_t[3][b8, :], rows[b8, :], ACT.Exp)
                f(rows[96:104, :], row_t[2][b8, :], ACT.Exp).then_inc(ba_act, 1)
            elif j == 48:
                act.wait_ge(ba_vec, 7)
                for i, src in enumerate((rows[b8, :], row_t[3][b8, :], row_t[4][b8, :])):
                    act.dma_start(scr_rows[i], src).then_inc(rows_stored, 16)
            if 48 <= j < 48 + NCH // 2:
                for c in (2 * (j - 48), 2 * (j - 48) + 1):
                    act.wait_ge(ba_turned, c + 1)
                    f(per_token[:, c, :, 0:8], bank[X0 + c % 2][:, 0:P].rearrange("p (k e) -> p k e", e=32)[:, :, 0:8],
                      ACT.Copy).then_inc(ba_act, 1)

        def decay_pe(pe, j):
            if 48 <= j < 48 + NCH // 2:
                if j == 48:
                    pe.wait_ge(ba_vec, 7)
                for c in (2 * (j - 48), 2 * (j - 48) + 1):
                    if c >= 2:
                        pe.wait_ge(ba_act, 5 + c - 1)
                    nc.tensor.transpose(bank[X0 + c % 2][:, 0:P], rows[:, c * P:(c + 1) * P],
                                        ident[:, :]).then_inc(ba_turned, 1)
            elif j == 48 + NCH // 2:
                pe.wait_ge(ba_act, 5 + NCH)

        def decay_vec(dve, j):
            if j:
                return
            v = nc.vector
            dve.wait_ge(ba_act, 3)
            dve.wait_ge(rate_loaded, 32)
            dve.wait_ge(consts, 1)
            v.tensor_scalar(row_t[0][a8, :], row_t[0][a8, :], rate[a8, 2:3], None, ALU.add)
            v.memset(rows[:, :], 0.0)
            v.memset(reset[:, 0:S:P], 0.0)
            dve.drain()
            v.tensor_scalar(row_t[3][a8, :], row_t[0][a8, :], -1.0, None, ALU.mult)
            dve.drain()
            v.tensor_tensor(row_t[2][a8, :], row_t[0][a8, :], row_t[3][a8, :], ALU.min).then_inc(ba_vec, 1)
            dve.wait_ge(ba_act, 4)
            v.tensor_scalar(row_t[1][b8, :], row_t[1][b8, :], 1.0, None, ALU.add)
            v.scalar_tensor_tensor(row_t[1][a8, :], row_t[0][a8, :], 0.0, row_t[1][a8, :], ALU.max, ALU.add)
            dve.drain()
            v.reciprocal(rows[a8, :], row_t[1][b8, :])
            v.tensor_scalar(row_t[2][b8, :], row_t[1][a8, :], rate[a8, 1:2], -1.0, ALU.mult,
                            ALU.mult).then_inc(ba_vec, 1)
            dve.drain()
            v.tensor_tensor_scan(rows[b8, :], reset[:, :], row_t[2][b8, :], 0.0, ALU.mult, ALU.add)
            v.tensor_scalar(row_t[4][b8, :], rows[a8, :], -1.0, None, ALU.mult)
            dve.drain()
            gc3 = rows[b8, :].rearrange("p (c t) -> p c t", t=P)
            v.tensor_tensor(row_t[2][b8, :].rearrange("p (c t) -> p c t", t=P),
                            gc3[:, :, P - 1:P].broadcast_to([8, NCH, P]), gc3, ALU.subtract).then_inc(ba_vec, 1)
            dve.wait_ge(ba_act, 5)
            v.tensor_copy(row_t[1][b8, :], rows[a8, :])
            dve.drain()
            v.tensor_tensor(rows[64:72, :], row_t[3][b8, :], row_t[1][b8, :], ALU.mult).then_inc(ba_vec, 4)

        a0 = work
        qk_t = []
        for g in range(3):
            qk_t.append((at(f"qa{g}", [P, S], F32, a0), at(f"ka{g}", [P, S], F32, a0 + 4096)))
            a0 += 8192
        va_t = at("va_t", [P, S], F32, a0)
        va = at("va", [P, KT, P], F32, a0 + 4096)
        a0 += 8192
        score, prob, prob_t = [], [], []
        for b in range(2):
            score.append(at(f"score{b}", [P, HALF], F32, a0))
            prob.append(at(f"prob{b}", [P, HALF], F32, a0 + 2048))
            prob_t.append(at(f"prob_t{b}", [P, HALF], F32, a0 + 4096))
            a0 += 6144
        o_t = [at(f"o_t{g}", [P, S], F32, a0 + 4096 * g) for g in range(3)]
        a0 += 12288
        stat_b = [at(f"stat_b{g}", [P, 2 * S], F32, a0 + 8192 * g) for g in range(3)]
        a0 += 24576
        joint = at("joint", [P, S], F32, a0)
        stat = at("stat", [P, 16], F32, a0 + 4096)
        neg_max = at("neg_max", [P, 8], F32, a0 + 4160)
        stat_t = at("stat_t", [16, P], F32, a0 + 4192)
        assert a0 + 4800 <= work + 98304

        dense_read = sem("dense_read")
        v_turned, v_copied = sem("v_turned"), sem("v_copied")
        scored, scaled, maxed, exped = sem("scored"), sem("scaled"), sem("maxed"), sem("exped")
        p_turned, p_copied = sem("p_turned"), sem("p_copied")
        o_ready, o_taken = sem("o_ready"), sem("o_taken")
        st_turned, st_copied, st_stored, st_loaded = sem("st_turned"), sem("st_copied"), sem("st_stored"), [sem(f"st_loaded{g}") for g in range(3)]
        summed = sem("summed")
        mix_vec, mix_act, mixed_sem, y_stored = sem("mix_vec"), sem("mix_act"), sem("mixed_a"), sem("y_stored")

        PAIRS = (4, 4, 2)
        NP_SLOT = sum(PAIRS)

        def pair_no(s, g, p):
            return NP_SLOT * s + ((0, 4, 8)[g] + p)

        def att_steps(g):
            if g == 2:
                return ["v0", "v1", "s0", "s1", "t0", "t1", "o0", "o1", "st"]
            return ["v0", "v1", "s0", "s1", "t0", "s2", "t1", "o0", "s3", "t2", "o1", "t3", "o2", "o3", "st"]

        def block_keys(g, b):
            if g == 0:
                return (b - 1 if b else None), b
            if g == 1:
                return (b - 4 if b >= 4 else None), b
            return None, b

        def att_pe(pe, s, g, step):
            q, k = qk_t[g]
            kind, p = step[0], step[1:]
            if kind == "v":
                h = int(p)
                wait(pe, dense_read, 18 * s + (6 * g + 6))
                for i in range(4):
                    last = nc.tensor.transpose(bank[Y0 + h][:, i * P:(i + 1) * P],
                                               va_t[:, (4 * h + i) * P:(4 * h + i + 1) * P], ident[:, :])
                last.then_inc(v_turned, 1)
            elif step == "st":
                wait(pe, exped, pair_no(s, g, PAIRS[g] - 1) + 1)
                nc.tensor.transpose(bank[X0][0:16, 0:P], stat[:, :], ident[:, :]).then_inc(st_turned, 1)
            elif kind == "s":
                p = int(p)
                n = pair_no(s, g, p)
                if p >= 2:
                    wait(pe, scaled, n - 1)
                elif p == 0:
                    wait(pe, st_copied, 3 * s + g)
                for i in range(4 if g == 2 else 2):
                    b = (4 if g == 2 else 2) * p + i
                    lhs = q[:, b * P:(b + 1) * P]
                    if g == 2:
                        last = nc.tensor.matmul(bank[X0 + p % 2][:, i * P:(i + 1) * P], lhs, k[:, b * P:(b + 1) * P],
                                                start=True, stop=True)
                    else:
                        before, own = block_keys(g, b)
                        blocks_k = k[:, :].rearrange("p (b i) -> p b i", i=P)
                        if before is None:
                            rhs = blocks_k[:, own:own + 1, :].broadcast_to([P, 2, P])
                        else:
                            rhs = blocks_k[:, before:own + 1:own - before, :]
                        last = nc.tensor.matmul(bank[X0 + p % 2][:, i * 256:(i + 1) * 256].rearrange("p (a j) -> p a j", a=2),
                                                lhs, rhs, start=True, stop=True)
                last.then_inc(scored, 1)
            elif kind == "t":
                p = int(p)
                n = pair_no(s, g, p)
                wait(pe, exped, n + 1)
                wait(pe, p_copied, n - 1)
                if p < 2:
                    wait(pe, v_copied, 6 * s + (2 * g + 2))
                for i in range(4):
                    last = nc.tensor.transpose(bank[Y0 + p % 2][:, i * P:(i + 1) * P],
                                               prob[p % 2][:, i * P:(i + 1) * P], ident[:, :])
                last.then_inc(p_turned, 1)
            else:
                p = int(p)
                n = pair_no(s, g, p)
                wait(pe, p_copied, n + 1)
                ob = Z0 + (p if g == 2 else p // 2)
                if g == 2:
                    wait(pe, o_taken, 6 * s + 2 * g + (p - 1))
                elif p % 2 == 0:
                    wait(pe, o_taken, 6 * s + (2 * g + p // 2 - 1))
                for i in range(4 if g == 2 else 2):
                    b = (4 if g == 2 else 2) * p + i
                    o = bank[ob][:, (b % 4) * P:(b % 4 + 1) * P]
                    before, own = block_keys(g, b)
                    pt = prob_t[p % 2]
                    if g == 2:
                        last = nc.tensor.matmul(o, va[:, own, :], pt[:, i * P:(i + 1) * P], start=True, stop=True)
                    else:
                        if before is not None:
                            nc.tensor.matmul(o, va[:, before, :], pt[:, 2 * i * P:(2 * i + 1) * P], start=True, stop=False)
                        last = nc.tensor.matmul(o, va[:, own, :], pt[:, (2 * i + 1) * P:(2 * i + 2) * P],
                                                start=before is None, stop=True)
                last.then_inc(o_ready, 1)

        def att_act(act, s, g, step):
            kind, p = step[0], step[1:]
            if kind == "v":
                h = int(p)
                act.wait_ge(v_turned, 6 * s + (2 * g + h + 1))
                if h == 0:
                    wait(act, o_ready, pair_no(s, g, 0))
                nc.scalar.activation(va[:, 4 * h:4 * h + 4, :],
                                     bank[Y0 + h][:, :].rearrange("p (b d) -> p b d", d=P), ACT.Copy).then_inc(v_copied, 1)
            elif step == "st":
                act.wait_ge(st_copied, 3 * s + (g + 1))
                act.dma_start(scr_stat[g].rearrange("(a b) -> a b", b=P), stat_t[:, :]).then_inc(st_stored, 16)
            elif kind == "s":
                p = int(p)
                n = pair_no(s, g, p)
                act.wait_ge(maxed, n + 1)
                wait(act, p_turned, n - 1)
                m = 4 if g == 2 else 2
                w = HALF // m
                for i in range(m):
                    b = m * p + i
                    last = nc.scalar.activation(prob[p % 2][:, i * w:(i + 1) * w], score[p % 2][:, i * w:(i + 1) * w],
                                                ACT.Exp, bias=neg_max[:, b:b + 1], accum_out=stat[:, 8 + b:9 + b])
                last.then_inc(exped, 1)
            elif kind == "t":
                p = int(p)
                n = pair_no(s, g, p)
                act.wait_ge(p_turned, n + 1)
                wait(act, o_ready, n - 1)
                nc.scalar.activation(prob_t[p % 2][:, :], bank[Y0 + p % 2][:, :], ACT.Copy).then_inc(p_copied, 1)
            else:
                p = int(p)
                if g != 2 and p % 2 == 0:
                    return
                h = p if g == 2 else p // 2
                act.wait_ge(o_ready, pair_no(s, g, p) + 1)
                if h == 0:
                    wait(act, mixed_sem if g == 2 else summed, s)
                src, o = bank[Z0 + h], o_t[g]
                if g == 0:
                    dst, src = o[:, h * HALF:(h + 1) * HALF], src[:, :]
                elif g == 1:
                    dst = o[:, h * HALF:(h + 1) * HALF].rearrange("p (i r) -> p r i", r=4)
                    src = src[:, :].rearrange("p (r i) -> p r i", r=4)
                else:
                    dst = o[:, :].rearrange("p (i r) -> p r i", r=16)[:, 8 * h:8 * h + 8, :]
                    src = src[:, :].rearrange("p (r i) -> p r i", r=8)
                nc.scalar.activation(dst, src, ACT.Copy).then_inc(o_taken, 1)

        def att_vec(dve, s, g, step):
            kind, p = step[0], step[1:]
            v = nc.vector
            if step == "st":
                dve.wait_ge(st_turned, 3 * s + (g + 1))
                wait(dve, st_stored, 16 * (3 * s + g))
                v.tensor_copy(stat_t[:, :], bank[X0][0:16, 0:P]).then_inc(st_copied, 1)
            elif kind == "s":
                p = int(p)
                n = pair_no(s, g, p)
                dve.wait_ge(scored, n + 1)
                wait(dve, exped, n - 1)
                if p == 0:
                    wait(dve, st_turned, 3 * s + g)
                slope = slopes[:, ds(s + 4 * g, 1)]
                if g == 2:
                    dist = band_pair[:, :].unsqueeze(1).broadcast_to([P, 4, P])
                    m, w = 4, P
                else:
                    first = block_keys(g, 2 * p)[0] is None
                    both = block_keys(g, 2 * p + 1)[0] is None
                    m, w = 2, 256
                    if first and both:
                        dist = band[:, 0:1, :].broadcast_to([P, 2, 256])
                    elif first:
                        dist = band[:, :, :]
                    else:
                        dist = band[:, 1:2, :].broadcast_to([P, 2, 256])
                sc = score[p % 2][:, :].rearrange("p (a j) -> p a j", a=m)
                v.scalar_tensor_tensor(sc, dist, slope, bank[X0 + p % 2][:, :].rearrange("p (a j) -> p a j", a=m),
                                       ALU.mult, ALU.add).then_inc(scaled, 1)
                dve.drain()
                v.reduce_max(stat[:, m * p:m * p + m], sc, AXX)
                dve.drain()
                v.tensor_scalar(neg_max[:, m * p:m * p + m], stat[:, m * p:m * p + m], -1.0, None,
                                ALU.mult).then_inc(maxed, 1)

        def token_view(g, ap):
            if g == 0:
                return ap
            if g == 1:
                return ap.rearrange("p (n r i) -> p n i r", n=2, r=4)
            return ap.rearrange("p (r i) -> p i r", r=16)

        def like(g, ap):
            if g == 0:
                return ap
            if g == 1:
                return ap.rearrange("p (n i r) -> p n i r", n=2, r=4)
            return ap.rearrange("p (i r) -> p i r", r=16)

        def mix_vec_engine(dve, s, piece):
            v = nc.vector
            mx = [stat_b[g][:, 0:S] for g in range(3)]
            den = [stat_b[g][:, S:2 * S] for g in range(3)]
            if piece == "max":
                for g in range(2):
                    dve.wait_ge(st_loaded[g], 16 * s + 16)
                wait(dve, y_stored, 16 * s)
                v.tensor_tensor(like(1, joint[:, :]), like(1, mx[0]), token_view(1, mx[1]), ALU.max)
                dve.drain()
                dve.wait_ge(st_loaded[2], 16 * s + 16)
                v.tensor_tensor(like(2, joint[:, :]), like(2, joint[:, :]), token_view(2, mx[2]), ALU.max)
                dve.drain()
            elif piece[:3] == "sub":
                g = int(piece[3])
                v.tensor_tensor(token_view(g, mx[g]), token_view(g, mx[g]), like(g, joint[:, :]),
                                ALU.subtract).then_inc(mix_vec, 1)
            elif piece[:3] == "mul":
                g = int(piece[3])
                dve.wait_ge(o_taken, 6 * s + 6)
                dve.wait_ge(mix_act, 3 * s + (g + 1))
                v.tensor_tensor(den[g], den[g], mx[g], ALU.mult)
                v.tensor_tensor(like(g, o_t[g][:, :]), like(g, o_t[g][:, :]), token_view(g, mx[g]), ALU.mult)
                dve.drain()
            elif piece[:3] == "add":
                g = int(piece[3])
                first = den[0] if g == 1 else joint[:, :]
                v.tensor_tensor(like(g, joint[:, :]), like(g, first), token_view(g, den[g]), ALU.add)
                last = v.tensor_tensor(o_t[2][:, :], o_t[2][:, :], o_t[2 - g][:, :], ALU.add)
                if g == 2:
                    last.then_inc(summed, 1)
                dve.drain()
            elif piece[:3] == "rec":
                q = slice(256 * int(piece[3]), 256 * int(piece[3]) + 256)
                v.reciprocal(joint[:, q], joint[:, q])
                dve.drain()
            elif piece == "end":
                v.tensor_tensor(joint[:, :], o_t[2][:, :], joint[:, :], ALU.mult).then_inc(mixed_sem, 1)

        def mix_act_engine(act, s, piece):
            if piece == "load":
                for g in range(3):
                    if isinstance(s, int) or g == 0:
                        act.wait_ge(rows_stored, 48)
                    act.wait_ge(st_stored, 16 * (3 * s + 3))
                    act.dma_start(stat_b[g][:, :], scr_stat[g].partition_broadcast(P)).then_inc(st_loaded[g], 16)
            elif piece[:3] == "sub":
                g = int(piece[3])
                act.wait_ge(mix_vec, 3 * s + (g + 1))
                nc.scalar.activation(stat_b[g][:, 0:S], stat_b[g][:, 0:S], ACT.Exp).then_inc(mix_act, 1)
            elif piece == "end":
                act.wait_ge(mixed_sem, s + 1)
                act.dma_start(scr_branch[ds(s * P, P), :], joint[:, :]).then_inc(y_stored, 16)

        MIX = {0: {29: ["load"], 40: ["max"]},
               1: {0: ["sub0", "sub1"], 1: ["sub2"], 3: ["mul0"], 8: ["mul1"], 10: ["mul2"], 17: ["add1"], 19: ["add2"],
                   23: ["rec0"], 26: ["rec1"], 30: ["rec2"], 34: ["rec3"], 38: ["end"]}}

        def mix_pieces(eng, mix, s, g, j):
            for piece in MIX.get(g, {}).get(j, ()):
                mix(eng, s, piece)

        def dense_att_pe(pe, s, g, j):
            i, half, k = j // 16, j // 8 % 2, j % 8
            m = 9 * s + (3 * g + i)
            dense_k(pe, ph["attn"], s, 3 * g + i, half, k, KT, D0 + half, act_in,
                    (dense_read, m * 2 + (half - 1)))

        def dense_att_act(act, s, g, j):
            if j % 8 != 7:
                return
            i, half = j // 16, j // 8 % 2
            act.wait_ge(projected, done(ph["attn"], s, 3 * g + i, half))
            t = (*qk_t[g], va_t)[i]
            src = bank[D0 + half]
            if i == 2 and half == 0:
                wait(act, v_turned, 6 * s + 2 * g)
            if g == 0:
                dst, src = t[:, half * HALF:(half + 1) * HALF], src[:, :]
            elif g == 1:
                dst = t[:, half * HALF:(half + 1) * HALF].rearrange("p (r i) -> p r i", r=4)
                src = src[:, :].rearrange("p (i r) -> p r i", r=4)
            else:
                dst = t[:, :].rearrange("p (r i) -> p r i", r=16)[:, :, 32 * half:32 * half + 32]
                src = src[:, :].rearrange("p (i r) -> p r i", r=16)
            nc.scalar.activation(dst, src, ACT.Copy, scale=float(P) ** -0.5 if i == 0 else 1.0).then_inc(dense_read, 1)

        AT = {15: (4, 5, 7, 9, 14, 16, 18, 20, 22, 25, 27, 31, 33, 36, 39), 9: (4, 5, 7, 9, 14, 17, 19, 22, 26)}

        def segment(eng, s, g, dense, side, side_s, mix=None, extra=None):
            before = (g + 2) % 3
            steps = att_steps(before) if side is not None else []
            for j in range(48):
                if dense is not None:
                    dense(eng, s, g, j)
                if extra is not None:
                    extra(eng, 48 * g + j)
                if steps and j in AT[len(steps)]:
                    side(eng, side_s, before, steps[AT[len(steps)].index(j)])
                if mix is not None:
                    mix_pieces(eng, mix, s - 1, g, j)

        def nothing(*_):
            pass

        def attention(eng, dense, side, mix, decay_):
            segment(eng, 0, 0, dense, None, 0, extra=decay_)
            segment(eng, 0, 1, dense, side, 0, extra=decay_)
            segment(eng, 0, 2, dense, side, 0)
            with eng.Fori(1, NSLOT) as s:
                segment(eng, s, 0, dense, side, s - 1, mix)
                segment(eng, s, 1, dense, side, s, mix)
                segment(eng, s, 2, dense, side, s)

        MIX_END = {28: ["load"], 40: ["max"], 56: ["sub0", "sub1"], 57: ["sub2"], 59: ["mul0", "mul1", "mul2"],
                   61: ["add1", "add2"]}
        MIX_LATE = {45: ["rec0"], 48: ["rec1"], 51: ["rec2"], 54: ["rec3"], 57: ["end"]}

        def attention_end(eng, side, mix, j):
            if j in AT[9]:
                side(eng, NSLOT - 1, 2, att_steps(2)[AT[9].index(j)])
            for piece in MIX_END.get(j, ()):
                mix(eng, NSLOT - 1, piece)

        def attention_sp(sp):
            with sp.Fori(0, NSLOT) as s:
                for i in range(9):
                    first = (COL_QA, COL_KA, COL_VA)[i % 3] + NSLOT * P * (i // 3)
                    load_weights(sp, ph["attn"], s, i, w_cols(w_in2, s * P + first))

        OB = ((D0, D1), (Y0, Y1))
        g_stored = [sem(f"g_stored{i}") for i in range(2)]
        g_sig, b_loaded, b_high, b_low = (
            sem("g_sig"), sem("b_loaded"), sem("b_high"), sem("b_low"))
        first_loaded = sem("first_loaded")
        m_gate, m_prod, m_sum, m_high, m_low = sem("m_gate"), sem("m_prod"), sem("m_sum"), sem("m_high"), sem("m_low")
        PEELED = 2

        def gates_sp(sp):
            def step(f):
                for i in range(2):
                    load_weights(sp, ph["gates"], f, i, w_cols(w_in2, f * P + (COL_GATE + i * D)))

            step(0)
            store_delta(sp, NHB - 2)
            step(1)
            step(2)
            store_delta(sp, NHB - 1)
            with sp.Fori(3, KT) as f:
                step(f)

        def gates_pool(pool):
            with pool.Fori(0, KT) as f:
                for i in range(2):
                    split_weights(pool, ph["gates"], f, i)

        def gate_step_pe(pe, f, i, half, k):
            free = (g_sig, f * 4 + (2 * i + half - 1))
            if isinstance(f, int) and f == 0 and i == 0:
                free = (dl["read"], 8 * NHB - 1 + half)
            dense_k(pe, ph["gates"], f, i, half, k, KT, D0 + half, act_in, free)

        def gate_take_act(act, f, i, half):
            act.wait_ge(projected, done(ph["gates"], f, i, half))
            if half == 0:
                wait(act, g_stored[i], f * 16)
            nc.scalar.activation(tmp[i][:, half * HALF:(half + 1) * HALF], bank[D0 + half][:, :],
                                 ACT.Sigmoid).then_inc(g_sig, 1)
            if half == 1:
                act.wait_ge(g_sig, f * 4 + (2 * i + 2))
                act.dma_start(scr_gate[ds(f * P + i * D, P), :], tmp[i][:, :]).then_inc(g_stored[i], 16)

        def gates_peeled(eng, dense, j):
            dense(eng, j // 32, j // 16 % 2, j // 8 % 2, j % 8)

        def gate_step_act(act, f, i, half, k):
            if k == KT - 1:
                gate_take_act(act, f, i, half)

        def gates_pe(pe):
            with pe.Fori(PEELED, KT) as f:
                for i in range(2):
                    for half in range(2):
                        for k in range(KT):
                            gate_step_pe(pe, f, i, half, k)

        def gates_act(act):
            act.wait_ge(y_stored, 16 * (NSLOT - 1))
            with act.Fori(PEELED, KT) as f:
                for i in range(2):
                    t = f * 2 + (i - 2 * PEELED)
                    act.wait_ge(b_low, f * 2 + (i - 2 * PEELED))
                    if i == 1:
                        act.wait_ge(y_stored, 16 * NSLOT)
                        act.wait_ge(dl["stored"], 16 * NHB)
                    act.dma_start(tmp[2][:, :], scr_branch[ds(f * (2 * P) + (i - 2 * PEELED) * P, P), :]).then_inc(b_loaded, 16)
                    gate_take_act(act, f, i, 0)
                    act.wait_ge(b_loaded, f * 32 + (16 * (i - 2 * PEELED) + 16))
                    nc.scalar.activation(branch[0][:, ds(t, 1), :].rearrange("p a t -> p (a t)"), tmp[2][:, :],
                                         ACT.Copy).then_inc(b_high, 1)
                    gate_take_act(act, f, i, 1)

        def gates_vec(dve):
            with dve.Fori(PEELED, KT) as f:
                for i in range(2):
                    t = f * 2 + (i - 2 * PEELED)
                    dve.wait_ge(b_high, f * 2 + (i - 2 * PEELED + 1))
                    nc.vector.tensor_tensor(branch[1][:, ds(t, 1), :].rearrange("p a t -> p (a t)"), tmp[2][:, :],
                                            branch[0][:, ds(t, 1), :].rearrange("p a t -> p (a t)").bitcast(F32),
                                            ALU.subtract).then_inc(b_low, 1)

        FIRST = (NB // 2 - NSLOT)

        def merge_sp(sp):
            with sp.Fori(0, KT) as f:
                load_weights(sp, ph["merge"], f, 0, w_cols(w_proj_attn[0], f * P, NSLOT))
                sp.dma_start(raw[0][:, NSLOT:NB // 2, :], w_cols(w_proj_delta[0], f * P, FIRST)).then_inc(first_loaded, 16)
                load_weights(sp, ph["merge"], f, 1,
                             w_cols(w_proj_delta[0][FIRST * P:NHB * P, :], f * P, NB // 2))

        def merge_pool(pool):
            with pool.Fori(0, KT) as f:
                pool.wait_ge(first_loaded, f * 16 + 16)
                split_weights(pool, ph["merge"], f, 0, NB // 2)
                split_weights(pool, ph["merge"], f, 1, NB // 2)

        def merge_pe(pe):
            def product(f, slot, k, b, half, dst, start, stop):
                for wp, ap in PASSES:
                    last = nc.tensor.matmul(bank[dst][:, :], wpart[slot][wp][:, k, :],
                                            branch[ap][:, b, half * HALF:(half + 1) * HALF],
                                            start=start and (wp, ap) == PASSES[0], stop=stop and (wp, ap) == PASSES[-1])
                return last

            def step(f):
                free = 4 * KT if isinstance(f, int) else None
                n = ph["merge"].tile(f, 0)

                def bank_free(number):
                    if free:
                        if number == 0:
                            pe.wait_ge(g_sig, free)
                    else:
                        pe.wait_ge(m_prod, f * 4 + (number - 3))

                pe.wait_ge(weights_split, n + (FREE + 1))
                bank_free(0)
                for k in range(NSLOT):
                    last = product(f, 0, k, k, 0, OB[0][0], k == 0, k == NSLOT - 1)
                last.then_inc(projected, 1)
                for half in range(2):
                    bank_free(2 + half)
                    for k in range(NSLOT, NB // 2):
                        product(f, 0, k, k, half, OB[1][half], k == NSLOT, False)
                bank_free(1)
                for k in range(NSLOT):
                    last = product(f, 0, k, k, 1, OB[0][1], k == 0, k == NSLOT - 1)
                last.then_inc(projected, 1)
                pe.wait_ge(weights_split, n + (FREE + 2))
                for half in range(2):
                    for k in range(NB // 2):
                        last = product(f, 1, k, NB // 2 + k, half, OB[1][half], False, k == NB // 2 - 1)
                    last.then_inc(projected, 1)

            pe.wait_ge(b_low, NB)
            step(0)
            with pe.Fori(1, KT) as f:
                step(f)

        def merge_act(act):
            for i in range(2):
                act.wait_ge(g_stored[i], 16 * KT)

            def load(f):
                for i in range(2):
                    act.dma_start(tmp[i][:, :], scr_gate[ds(f * P + i * D, P), :]).then_inc(m_gate, 16)

            def step(f, more):
                act.wait_ge(m_sum, f + 1)
                if more:
                    load(f + 1)
                nc.scalar.activation(act_in[0][:, ds(f, 1), :].rearrange("p a t -> p (a t)"), tmp[2][:, :],
                                     ACT.Copy).then_inc(m_high, 1)

            load(0)
            with act.Fori(0, KT - 1) as f:
                step(f, True)
            step(KT - 1, False)

        def merge_vec(dve):
            v = nc.vector

            def step(f):
                dve.wait_ge(m_gate, f * 32 + 32)
                for i in range(2):
                    for half in range(2):
                        c = slice(half * HALF, (half + 1) * HALF)
                        dve.wait_ge(projected, done(ph["merge"], f, i, half))
                        v.tensor_tensor(tmp[i][:, c], tmp[i][:, c], bank[OB[i][half]][:, :], ALU.mult).then_inc(m_prod, 1)
                dve.drain()
                v.tensor_tensor(tmp[2][:, :], tmp[0][:, :], tmp[1][:, :], ALU.add).then_inc(m_sum, 1)
                dve.wait_ge(m_high, f + 1)
                v.tensor_tensor(act_in[1][:, ds(f, 1), :].rearrange("p a t -> p (a t)"), tmp[2][:, :],
                                act_in[0][:, ds(f, 1), :].rearrange("p a t -> p (a t)").bitcast(F32),
                                ALU.subtract).then_inc(m_low, 1)
                dve.drain()

            step(0)
            with dve.Fori(1, KT) as f:
                step(f)

        d0 = [work + 16384]

        def dt_(name, shape):
            t = at(name, shape, F32, d0[0])
            d0[0] += size_of(shape, F32)
            return t

        conv_in = [at(f"conv_in{i}", [P, 3 + S + 5], F32, slot2 + 4128 * i) for i in range(2)]
        conv_out = at("conv_out", [P, S], F32, work)
        qkv = [at(f"qkv{i}", [P, S], F32, work + 4096 + 4096 * i) for i in range(3)]
        z_next = at("z_next", [P, S], F32, work + 92160)
        z_now = dt_("z_now", [P, S])
        qn = dt_("qn", [P, S])
        sq = [dt_(f"sq{i}", [P, S]) for i in range(2)]
        kn = dt_("kn", [P, S])
        row = [dt_("row0", [P, S]), dt_("row1", [P, S]), at("row2", [P, S], F32, work + 87040)]
        decay, neg_a = row[0], row[2]
        inv, inv_t = dt_("inv", [P, S]), dt_("inv_t", [P, S])
        assert d0[0] == work + 53248
        d0[0] += 4096
        half_way = dt_("half_way", [P, S])
        beta_v, beta_k, k_dec = dt_("beta_v", [P, S]), dt_("beta_k", [P, S]), dt_("k_dec", [P, S])
        col = dt_("col", [P, NCH, 4])
        decay_all = dt_("decay_all", [P, NCH])
        state, u_now = dt_("state", [P, P]), dt_("u_now", [P, P])
        assert d0[0] <= work + 81920, d0[0] - work
        u_bar, w_t = inv, half_way
        o_raw, o_sq = beta_v, beta_k

        dl = {x_: sem("dl_" + x_) for x_ in (
            "read", "conv", "silu", "sq", "ss", "ln", "normed", "vt", "bv", "kt", "kdec", "kk", "qk", "rows",
            "diff", "dec", "a", "pt", "t0t", "t0", "t0c", "y", "yc", "dt", "dtm", "tt", "ttc", "ub", "ubc", "wt", "wtc",
            "qdec", "ws", "u", "o", "s", "sup", "z", "os", "osq", "oss", "oln", "oexp", "out", "stored", "zero", "col", "eye")}

        def compact(t, c, level):
            return t[:, c * 64:(c + 1) * 64].rearrange("p (n b) -> p n b", b=1 << level)

        def c4(t, half):
            return t[:, half * HALF:(half + 1) * HALF].rearrange("p (c t) -> p c t", t=P)

        def chunk(t, c):
            return t[:, c * P:(c + 1) * P]

        STEPS_AT = {4: ["ss"], 8: ["vt0"], 9: ["vt1"], 15: ["kt0"], 16: ["kt1", "kk0"], 17: ["kk1"], 18: ["qk0"],
                    19: ["qk1"], 21: ["t00"], 22: ["t01"], 42: ["ub0", "ub1", "wt0", "wt1"], 61: ["os"], 63: ["on"]}
        for level in range(1, 7):
            for n_, x_ in enumerate("ydt"):
                STEPS_AT[24 + 3 * (level - 1) + n_] = [f"{x_}{level}0", f"{x_}{level}1"]
        for c_ in range(NCH):
            STEPS_AT[44 + 2 * c_] = [f"a{c_}"]
            STEPS_AT[45 + 2 * c_] = [f"b{c_}"]
        WHOLE, HALVES = slice(0, S), (slice(0, HALF), slice(HALF, S))
        TAPS_AT = {20: (0, 0, WHOLE), 23: (0, 1, WHOLE), 25: (0, 2, WHOLE), 28: (0, 3, WHOLE),
                   34: (1, 0, WHOLE), 37: (1, 1, WHOLE), 40: (1, 2, WHOLE), 43: (1, 3, WHOLE)}
        for n_ in range(8):
            TAPS_AT[48 + n_] = (2, n_ // 2, HALVES[n_ % 2])
        SILU_AT = {30: 0, 46: 1, 58: 2}
        SQUARE_AT = {47: 0, 49: 1}
        ROWS_AT, PREPARE_AT = 60, 62

        def left(t, level):
            return t.rearrange("p c (n a b) -> p c n a b", a=2, b=1 << level)[:, :, :, 0, :]

        def delta_pe(pe, h, step):
            mm, tr = nc.tensor.matmul, nc.tensor.transpose
            two = h * 2
            if step == "ss":
                wait(pe, dl["sup"], h * NCH)
                wait(pe, dl["osq"], two)
                for i in range(2):
                    pe.wait_ge(dl["sq"], two + (i + 1))
                    for half in range(2):
                        last = mm(bank[(X0, Y0)[i] + half][:, :], ones[:, :], sq[i][:, half * HALF:(half + 1) * HALF],
                                  start=True, stop=True)
                    last.then_inc(dl["ss"], 1)
            elif step[:2] == "vt":
                half = int(step[2])
                pe.wait_ge(dl["silu"], h * 3 + 3)
                wait(pe, dl["oln"], two)
                for c in range(4 * half, 4 * half + 4):
                    last = tr(bank[Z0 + half][:, (c % 4) * P:(c % 4 + 1) * P], chunk(qkv[2], c), ident[:, :])
                last.then_inc(dl["vt"], 1)
            elif step[:2] == "kt":
                half = int(step[2])
                pe.wait_ge(dl["normed"], two + 2)
                for c in range(4 * half, 4 * half + 4):
                    last = tr(bank[X0 + half][:, (c % 4) * P:(c % 4 + 1) * P], chunk(kn, c), ident[:, :])
                last.then_inc(dl["kt"], 1)
            elif step[:2] == "kk":
                half = int(step[2])
                for c in range(4 * half, 4 * half + 4):
                    last = mm(bank[Y0 + half][:, (c % 4) * P:(c % 4 + 1) * P], chunk(kn, c), chunk(kn, c), start=True, stop=True)
                last.then_inc(dl["kk"], 1)
            elif step[:2] == "qk":
                half = int(step[2])
                pe.wait_ge(dl["bv"], two + (half + 1))
                for c in range(4 * half, 4 * half + 4):
                    last = mm(bank[Z0 + half][:, (c % 4) * P:(c % 4 + 1) * P], chunk(kn, c), chunk(qn, c), start=True, stop=True)
                last.then_inc(dl["qk"], 1)
            elif step[:2] == "t0":
                half = int(step[2])
                pe.wait_ge(dl["t0t"], two + (half + 1))
                pe.wait_ge(dl["kdec"], two + (half + 1))
                for c in range(4 * half, 4 * half + 4):
                    last = tr(bank[X0 + half][:, (c % 4) * P:(c % 4 + 1) * P], chunk(inv_t, c), ident[:, :])
                last.then_inc(dl["t0"], 1)
            elif step[0] in "ydt" and step[1] in "123456":
                level, half = int(step[1]), int(step[2])
                n = h * 12 + (2 * (level - 1) + half)
                if step[0] == "y":
                    if level == 1:
                        pe.wait_ge(dl["t0c"], two + (half + 1))
                        pe.wait_ge(dl["a"], two + 2)
                    for c in range(4 * half, 4 * half + 4):
                        last = mm(compact(bank[Y0 + half], c % 4, level), chunk(neg_a, c),
                                  left(inv[:, :].rearrange("p (c t) -> p c t", t=P), level)[:, c], start=True, stop=True)
                    last.then_inc(dl["y"], 1)
                elif step[0] == "d":
                    pe.wait_ge(dl["yc"], n + 1)
                    if level > 1:
                        pe.wait_ge(dl["ttc"], n - 1)
                    else:
                        pe.wait_ge(dl["pt"], two + (half + 1))
                    for c in range(4 * half, 4 * half + 4):
                        last = mm(bank[Z0 + half][:, (c % 4) * 64:(c % 4 + 1) * 64], chunk(inv_t, c),
                                  half_way[:, c * 64:(c + 1) * 64], start=True, stop=True)
                    last.then_inc(dl["dt"], 1)
                else:
                    pe.wait_ge(dl["dtm"], n + 1)
                    for c in range(4 * half, 4 * half + 4):
                        last = tr(bank[X0 + half][:, (c % 4) * P:(c % 4 + 1) * P], chunk(inv, c), ident[:, :])
                    last.then_inc(dl["tt"], 1)
            elif step[:2] == "ub":
                half = int(step[2])
                pe.wait_ge(dl["ttc"], h * 12 + (11 + half))
                for c in range(4 * half, 4 * half + 4):
                    last = mm(bank[Y0 + half][:, (c % 4) * P:(c % 4 + 1) * P], chunk(inv_t, c), chunk(beta_v, c),
                              start=True, stop=True)
                last.then_inc(dl["ub"], 1)
            elif step[:2] == "wt":
                half = int(step[2])
                for c in range(4 * half, 4 * half + 4):
                    last = mm(bank[Z0 + half][:, (c % 4) * P:(c % 4 + 1) * P], chunk(beta_k, c), chunk(inv_t, c),
                              start=True, stop=True)
                last.then_inc(dl["wt"], 1)
            elif step[0] == "a":
                c = int(step[1])
                n = h * NCH + c
                if c == 0:
                    pe.wait_ge(dl["ubc"], two + 2)
                    pe.wait_ge(dl["wtc"], two + 2)
                    pe.wait_ge(dl["qdec"], h + 1)
                    pe.wait_ge(dl["zero"], h + 1)
                else:
                    pe.wait_ge(dl["sup"], n)
                mm(bank[X0][:, 0:P], chunk(w_t, c), state[:, :], start=True, stop=True).then_inc(dl["ws"], 1)
                mm(bank[Y0 + c // 4][:, (c % 4) * P:(c % 4 + 1) * P], state[:, :], chunk(row[1], c), start=True, stop=False)
            elif step[0] == "b":
                c = int(step[1])
                pe.wait_ge(dl["u"], h * NCH + (c + 1))
                mm(bank[X1][:, 0:P], chunk(k_dec, c), u_now[:, :], start=True, stop=True).then_inc(dl["s"], 1)
                mm(bank[Y0 + c // 4][:, (c % 4) * P:(c % 4 + 1) * P], u_now[:, :], chunk(decay, c),
                   start=False, stop=True).then_inc(dl["o"], 1)
            elif step == "os":
                for half in range(2):
                    pe.wait_ge(dl["osq"], two + (half + 1))
                    mm(bank[Z0 + half][:, :], ones[:, :], o_sq[:, half * HALF:(half + 1) * HALF],
                       start=True, stop=True).then_inc(dl["oss"], 1)

        def delta_act(act, h, step):
            f = nc.scalar.activation
            two = h * 2
            if step == "ss":
                for i in range(2):
                    act.wait_ge(dl["ss"], two + (i + 1))
                    for half in range(2):
                        f(sq[i][:, half * HALF:(half + 1) * HALF], bank[(X0, Y0)[i] + half][:, :], ACT.Ln, bias=EPS)
                act.drain()
                for i in range(2):
                    f(sq[i][:, :], sq[i][:, :], ACT.Exp, scale=-0.5).then_inc(dl["ln"], 1)
                act.wait_ge(dl["diff"], h + 1)
                f(decay[:, :], decay[:, :], ACT.Exp).then_inc(dl["dec"], 1)
            elif step[:2] == "vt":
                half = int(step[2])
                act.wait_ge(dl["vt"], two + (half + 1))
                if half == 0:
                    wait(act, dl["out"], h)
                    act.wait_ge(dl["col"], h + 1)
                for c in range(4 * half, 4 * half + 4):
                    last = f(chunk(beta_v, c), bank[Z0 + half][:, (c % 4) * P:(c % 4 + 1) * P], ACT.Copy,
                             scale=col[:, c, 1:2])
                last.then_inc(dl["bv"], 1)
            elif step == "qk1":
                wait(act, dl["stored"], h * 16)
                act.wait_ge(dl["read"], h * 8 + 8)
                f(z_now[:, :], z_next[:, :], ACT.Copy).then_inc(dl["z"], 1)
            elif step == "a2" and not isinstance(h, int):
                act.wait_ge(dl["wt"], two + 2)
                f(inv_t[:, :].rearrange("p (c t) -> p c t", t=P), ident[:, :].unsqueeze(1).broadcast_to([P, NCH, P]),
                  ACT.Copy).then_inc(dl["eye"], 1)
            elif step[:2] == "t0":
                half = int(step[2])
                act.wait_ge(dl["t0"], two + (half + 1))
                f(c4(inv, half), bank[X0 + half][:, :].rearrange("p (c t) -> p c t", t=P), ACT.Copy).then_inc(dl["t0c"], 1)
            elif step[0] in "yt" and step[1] in "123456":
                level, half = int(step[1]), int(step[2])
                n = h * 12 + (2 * (level - 1) + half)
                if step[0] == "y":
                    act.wait_ge(dl["y"], n + 1)
                    f(half_way[:, half * 256:half * 256 + 256], bank[Y0 + half][:, 0:256], ACT.Copy).then_inc(dl["yc"], 1)
                else:
                    act.wait_ge(dl["tt"], n + 1)
                    f(inv_t[:, half * HALF:(half + 1) * HALF], bank[X0 + half][:, :], ACT.Copy).then_inc(dl["ttc"], 1)
            elif step[:2] == "ub":
                half = int(step[2])
                act.wait_ge(dl["ub"], two + (half + 1))
                f(u_bar[:, half * HALF:(half + 1) * HALF], bank[Y0 + half][:, :], ACT.Copy).then_inc(dl["ubc"], 1)
            elif step in ("b3", "b7"):
                half = int(step[1]) // 4
                act.wait_ge(dl["o"], h * NCH + (4 * half + 4))
                f(o_raw[:, half * HALF:(half + 1) * HALF], bank[Y0 + half][:, :], ACT.Copy)
                f(o_sq[:, half * HALF:(half + 1) * HALF], bank[Y0 + half][:, :], ACT.Square).then_inc(dl["osq"], 1)
            elif step == "on":
                for half in range(2):
                    act.wait_ge(dl["oss"], two + (half + 1))
                    f(o_sq[:, half * HALF:(half + 1) * HALF], bank[Z0 + half][:, :], ACT.Ln, scale=1.0 / P,
                      bias=EPS).then_inc(dl["oln"], 1)
                act.drain()
                f(o_sq[:, :], o_sq[:, :], ACT.Exp, scale=-0.5).then_inc(dl["oexp"], 1)

        def delta_vec(dve, h, step):
            v = nc.vector
            two = h * 2

            def b4(kind, half):
                return col[:, 4 * half:4 * half + 4, kind:kind + 1].broadcast_to([P, 4, P])

            if step == "ss":
                dve.wait_ge(dl["ln"], two + 1)
                v.scalar_tensor_tensor(qn[:, :], qkv[0][:, :], float(P) ** -0.5, sq[0][:, :], ALU.mult,
                                       ALU.mult).then_inc(dl["normed"], 1)
                dve.wait_ge(dl["ln"], two + 2)
                v.tensor_tensor(kn[:, :], qkv[1][:, :], sq[1][:, :], ALU.mult).then_inc(dl["normed"], 1)
                dve.wait_ge(dl["dec"], h + 1)
                v.tensor_tensor(neg_a[:, :], neg_a[:, :], decay[:, :], ALU.mult)
                dve.drain()
            elif step[:2] == "kt":
                half = int(step[2])
                dve.wait_ge(dl["kt"], two + (half + 1))
                src = bank[X0 + half][:, :].rearrange("p (c t) -> p c t", t=P)
                v.tensor_tensor(c4(beta_k, half), src, b4(2, half), ALU.mult)
                v.tensor_tensor(c4(k_dec, half), src, b4(3, half), ALU.mult).then_inc(dl["kdec"], 1)
            elif step[:2] == "kk":
                half = int(step[2])
                hs = slice(half * HALF, (half + 1) * HALF)
                dve.wait_ge(dl["kk"], two + (half + 1))
                wait(dve, dl["eye"], h)
                v.tensor_tensor(neg_a[:, hs], bank[Y0 + half][:, :], neg_a[:, hs], ALU.mult).then_inc(dl["a"], 1)
                dve.drain()
                v.copy_predicated(c4(inv_t, half), merge_mask[:, 0:1, :].broadcast_to([P, 4, P]),
                                  c4(neg_a, half)).then_inc(dl["t0t"], 1)
            elif step[:2] == "qk":
                half = int(step[2])
                hs = slice(half * HALF, (half + 1) * HALF)
                dve.wait_ge(dl["qk"], two + (half + 1))
                v.tensor_tensor(decay[:, hs], bank[Z0 + half][:, :], decay[:, hs], ALU.mult).then_inc(dl["pt"], 1)
                if half == 1:
                    v.tensor_tensor(row[1][:, :], row[1][:, :], qn[:, :], ALU.mult).then_inc(dl["qdec"], 1)
            elif step[0] == "d" and step[1] in "123456":
                level, half = int(step[1]), int(step[2])
                n = h * 12 + (2 * (level - 1) + half)
                wait_alone(dve, dl["dt"], n + 1)
                v.copy_predicated(left(c4(inv, half), level),
                                  left(merge_mask[:, level:level + 1, :].broadcast_to([P, 4, P]), level),
                                  bank[Z0 + half][:, 0:256].rearrange("p (c n b) -> p c n b", c=4,
                                                                      b=1 << level)).then_inc(dl["dtm"], 1)
            elif step[:2] == "wt":
                half = int(step[2])
                dve.wait_ge(dl["wt"], two + (half + 1))
                v.tensor_copy(w_t[:, half * HALF:(half + 1) * HALF], bank[Z0 + half][:, :]).then_inc(dl["wtc"], 1)
            elif step[0] == "a":
                c = int(step[1])
                dve.wait_ge(dl["ws"], h * NCH + (c + 1))
                if c == 0:
                    dve.wait_ge(dl["ubc"], two + 2)
                v.tensor_tensor(u_now[:, :], chunk(u_bar, c), bank[X0][:, 0:P], ALU.subtract).then_inc(dl["u"], 1)
            elif step[0] == "b":
                c = int(step[1])
                dve.wait_ge(dl["s"], h * NCH + (c + 1))
                v.scalar_tensor_tensor(state[:, :], state[:, :], decay_all[:, c:c + 1], bank[X1][:, 0:P],
                                       ALU.mult, ALU.add).then_inc(dl["sup"], 1)
            elif step == "on":
                dve.wait_ge(dl["oexp"], h + 1)
                v.scalar_tensor_tensor(o_raw[:, :], o_raw[:, :], dn_norm_c[:, 0:1], o_sq[:, :], ALU.mult, ALU.mult)
                dve.drain()
                dve.wait_ge(dl["z"], h + 1)
                v.tensor_tensor(z_now[:, :], o_raw[:, :], z_now[:, :], ALU.mult).then_inc(dl["out"], 1)

        def dense_delta_pe(pe, h, j):
            i, half, k = j // 16, j // 8 % 2, j % 8
            m = 4 * h + i
            free = (dl["read"], m * 2 + (half - 1))
            if isinstance(h, int) and i == 0:
                free = (dense_read, 2 * 9 * NSLOT - 1 + half)
            dense_k(pe, ph["delta"], h, i, half, k, KT, D0 + half, act_in, free)

        def dense_delta_act(act, h, j):
            if j % 8 != 7:
                return
            i, half = j // 16, j // 8 % 2
            f = nc.scalar.activation
            act.wait_ge(projected, done(ph["delta"], h, i, half))
            if i == 3:
                if half == 0:
                    wait(act, dl["z"], h)
                    if isinstance(h, int):
                        act.wait_ge(consts, 4)
                f(z_next[:, half * HALF:(half + 1) * HALF], bank[D0 + half][:, :], ACT.Silu).then_inc(dl["read"], 1)
                return
            if half == 0:
                wait(act, dl["conv"], h * 3 + (i - 1))
            f(conv_in[i % 2][:, 3 + half * HALF:3 + (half + 1) * HALF], bank[D0 + half][:, :],
              ACT.Copy).then_inc(dl["read"], 1)

        def silu_delta_act(act, h, i):
            act.wait_ge(dl["conv"], h * 3 + (i + 1))
            if i < 2:
                wait(act, dl["normed"], h * 2 - 2 + (i + 1) if isinstance(h, int) else h * 2 + (i - 1))
            else:
                wait(act, dl["vt"], h * 2)
            nc.scalar.activation(qkv[i][:, :], conv_out[:, :], ACT.Silu).then_inc(dl["silu"], 1)

        def square_delta_act(act, h, i):
            act.wait_ge(dl["silu"], h * 3 + (i + 1))
            wait(act, dl["normed"], h * 2)
            nc.scalar.activation(sq[i][:, :], qkv[i][:, :], ACT.Square).then_inc(dl["sq"], 1)

        def prepare_vec(dve, h):
            v = nc.vector
            v.tensor_copy(col[:, :, :], per_token[:, :, :, ds(h, 1)].rearrange("p c k a -> p c (k a)")).then_inc(dl["col"], 1)
            dve.drain()
            dve.wait_ge(dl["rows"], h * 48 + 48)
            v.tensor_copy(decay_all[:, :], row[1][:, P - 1:S:P])
            c8 = decay[:, :].rearrange("p (c t) -> p c t", t=P)
            v.tensor_tensor(c8, c8, col[:, :, 0:1].broadcast_to([P, NCH, P]), ALU.subtract)
            dve.drain()
            v.scalar_tensor_tensor(c8, c8, 0.0, neg_upper[:, :].unsqueeze(1).broadcast_to([P, NCH, P]),
                                   ALU.min, ALU.add).then_inc(dl["diff"], 1)
            a8 = neg_a[:, :].rearrange("p (c t) -> p c t", t=P)
            v.tensor_tensor(a8, a8, strict_up[:, :].unsqueeze(1).broadcast_to([P, NCH, P]), ALU.mult)
            wait(dve, dl["s"], h * NCH)
            v.memset(state[:, :], 0.0).then_inc(dl["zero"], 1)
            if isinstance(h, int):
                v.tensor_copy(inv_t[:, :].rearrange("p (c t) -> p c t", t=P),
                              ident[:, :].unsqueeze(1).broadcast_to([P, NCH, P]))
            dve.drain()

        def conv_vec(dve, h, i, j, part):
            v = nc.vector
            if j == 0:
                if part.start == 0:
                    dve.wait_ge(dl["read"], h * 8 + (2 * i + 2))
                    wait(dve, dl["silu"], h * 3 + i)
            else:
                dve.drain()
            tap = conv_c[:, j, ds(h + i * NHB, 1)]
            shifted = conv_in[i % 2][:, part.start + j:part.stop + j]
            if j == 0:
                v.tensor_scalar(conv_out[:, part], shifted, tap, None, ALU.mult)
            else:
                last = v.scalar_tensor_tensor(conv_out[:, part], shifted, tap, conv_out[:, part], ALU.mult, ALU.add)
            if j == 3 and part.stop == S:
                last.then_inc(dl["conv"], 1)

        def delta_iteration(eng, h, dense, own, side, mix=None):
            conv, silu, square, rows_, prepare = own
            for j in range(64):
                dense(eng, h, j)
                if mix is not None:
                    attention_end(eng, side, mix, j)
                else:
                    for s_ in STEPS_AT.get(j, ()):
                        if s_ != "on":
                            side(eng, h - 1, s_)
                if j in TAPS_AT:
                    conv(eng, h, *TAPS_AT[j])
                if j in SILU_AT:
                    silu(eng, h, SILU_AT[j])
                if j in SQUARE_AT:
                    square(eng, h, SQUARE_AT[j])
                if j == ROWS_AT:
                    rows_(eng, h)
                if j == PREPARE_AT:
                    prepare(eng, h)
            if mix is None:
                side(eng, h - 1, "on")

        def delta_heads(eng, dense, own, side):
            with eng.Fori(1, NHB) as h:
                delta_iteration(eng, h, dense, own, side)

        def delta_end(eng, gate, side, mix):
            for j in range(64):
                gates_peeled(eng, gate, j)
                for s_ in STEPS_AT.get(j, ()):
                    side(eng, NHB - 1, s_)
                for piece in MIX_LATE.get(j, ()):
                    mix(eng, NSLOT - 1, piece)

        def load_rows(act, h):
            wait(act, dl["o"], h * NCH)
            if isinstance(h, int):
                act.wait_ge(rows_stored, 48)
            for j in range(3):
                src = scr_rows[j][ds(h, 1), :] if not isinstance(h, int) else scr_rows[j][h:h + 1, :]
                act.dma_start(row[j][:, :], src.rearrange("a t -> (a t)").partition_broadcast(P)).then_inc(dl["rows"], 16)

        OWN_ACT = (nothing, silu_delta_act, square_delta_act, load_rows, nothing)
        OWN_VEC = (conv_vec, nothing, nothing, nothing, prepare_vec)

        def store_delta(sp, h):
            sp.wait_ge(dl["out"], h + 1)
            sp.dma_start(scr_branch[ds(h * P + NSLOT * P, P), :], z_now[:, :]).then_inc(dl["stored"], 16)

        def delta_sp(sp):
            def step(h):
                for i, c in enumerate((COL_QD, COL_KD, COL_VD, COL_Z)):
                    load_weights(sp, ph["delta"], h, i, w_cols(w_in2, h * P + c))
                    if i == 1 and not isinstance(h, int):
                        store_delta(sp, h - 2)

            step(0)
            step(1)
            with sp.Fori(2, NHB) as h:
                step(h)

        x_tile = [at(f"x_tile{i}", [P, KT, P], F32, work + 4096 * i) for i in range(2)]
        sq_sum = at("sq_sum", [P, S], F32, work + 8192)
        sq_now = at("sq_now", [P, S], F32, work + 12288)
        rms = at("rms", [P, S], F32, work + 16384)
        scaled_h = [at(f"scaled_h{i}", [P, S], F32, work + 20480 + 4096 * i) for i in range(2)]
        x_here = [sem(f"x_here{i}") for i in range(2)]
        h_squared, h_summed = sem("h_squared"), sem("h_summed")
        n_sum, n_rms, n_scaled, n_high, n_low = sem("n_sum"), sem("n_rms"), sem("n_scaled"), sem("n_high"), sem("n_low")
        def out_sp(sp):
            def x_columns(it, i):
                sp.dma_start(x_tile[i][:, :, :],
                             x[0].rearrange("(c p) n -> p c n", p=P)[:, :, ds((it * 2 + i) * P, P)]).then_inc(x_here[i], 16)

            for i in range(2):
                load_weights(sp, ph["out"], 0, i, w_cols(w_out[0], i * P))
            sp.wait_ge(projected, done(ph["merge"], KT - 1, 1, 1))
            for i in range(2):
                x_columns(0, i)
            with sp.Fori(1, KT // 2) as it:
                for i in range(2):
                    load_weights(sp, ph["out"], it, i, w_cols(w_out[0], (it * 2 + i) * P))
                    sp.wait_ge(projected, done(ph["out"], it - 1, i, 1))
                    x_columns(it, i)

        def out_pe(pe):
            def product(it, i, half, k, free):
                dense_k(pe, ph["out"], it, i, half, k, KT, OB[i][half], act_in, free, closed=False)

            def residual(it, i, half):
                if half == 0:
                    pe.wait_ge(x_here[i], it * 16 + 16)
                for c in range(4):
                    last = nc.tensor.matmul(bank[OB[i][half]][:, c * P:(c + 1) * P], x_tile[i][:, 4 * half + c, :],
                                            ident[:, :], start=False, stop=c == 3)
                last.then_inc(projected, 1)

            for i in range(2):
                for half in range(2):
                    for k in range(KT - 1):
                        if i == 0 and half == 0:
                            pe.wait_ge(m_low, k + 1)
                        product(0, i, half, k, (m_prod, 4 * KT - 3 + 2 * i + half))
            pe.wait_ge(m_low, KT)
            for i in range(2):
                for half in range(2):
                    product(0, i, half, KT - 1, None)
                    residual(0, i, half)
            with pe.Fori(1, KT // 2) as it:
                for i in range(2):
                    for half in range(2):
                        for k in range(KT):
                            product(it, i, half, k, (h_squared, it * 4 + (half + 2 * i - 3)))
                        residual(it, i, half)

        def out_act(act):
            def step(it):
                for i in range(2):
                    for half in range(2):
                        act.wait_ge(projected, done(ph["out"], it, i, half))
                        hs = slice(half * HALF, (half + 1) * HALF)
                        b = bank[OB[i][half]]
                        nc.scalar.activation(h_t[:, ds(it * 2 + i, 1), hs].rearrange("p a t -> p (a t)"), b[:, :], ACT.Copy)
                        wait(act, h_summed, it * 4 + (half + 2 * i - 1))
                        nc.scalar.activation(sq_now[:, hs], b[:, :], ACT.Square).then_inc(h_squared, 1)

            step(0)
            with act.Fori(1, KT // 2) as it:
                step(it)

        def out_vec(dve):
            v = nc.vector
            v.memset(sq_sum[:, :], 0.0)
            dve.drain()
            with dve.Fori(0, KT // 2) as it:
                for i in range(2):
                    for half in range(2):
                        hs = slice(half * HALF, (half + 1) * HALF)
                        dve.wait_ge(h_squared, it * 4 + (half + 2 * i + 1))
                        v.tensor_tensor(sq_sum[:, hs], sq_sum[:, hs], sq_now[:, hs], ALU.add).then_inc(h_summed, 1)
                        dve.drain()

        def norm_pe(pe, count):
            pe.wait_ge(h_summed, count)
            for half in range(2):
                last = nc.tensor.matmul(bank[X0 + half][:, :], ones[:, :], sq_sum[:, half * HALF:(half + 1) * HALF],
                                        start=True, stop=True)
            last.then_inc(n_sum, 1)

        def norm_act(act, number):
            act.wait_ge(n_sum, number)
            for half in range(2):
                nc.scalar.activation(rms[:, half * HALF:(half + 1) * HALF], bank[X0 + half][:, :], ACT.Ln,
                                     scale=1.0 / D, bias=EPS)
            act.drain()
            nc.scalar.activation(rms[:, :], rms[:, :], ACT.Exp, scale=-0.5).then_inc(n_rms, 1)

        def norm_split_act(act):
            for k in range(KT):
                act.wait_ge(n_scaled, k + 1)
                nc.scalar.activation(act_in[0][:, k, :], scaled_h[k % 2][:, :], ACT.Copy).then_inc(n_high, 1)

        def norm_split_vec(dve):
            v = nc.vector
            dve.wait_ge(n_rms, 1)
            for k in range(KT + 1):
                if k < KT:
                    v.scalar_tensor_tensor(scaled_h[k % 2][:, :], h_t[:, k, :], norm_ffn_c[:, k:k + 1], rms[:, :],
                                           ALU.mult, ALU.mult).then_inc(n_scaled, 1)
                if k:
                    dve.wait_ge(n_high, k)
                    v.tensor_tensor(act_in[1][:, k - 1, :], scaled_h[(k - 1) % 2][:, :],
                                    act_in[0][:, k - 1, :].bitcast(F32), ALU.subtract).then_inc(n_low, 1)
                    dve.drain()

        ff = {x_: sem("ff_" + x_) for x_ in ("silu", "mult", "high", "low", "added")}
        FF_BEFORE = [0]
        for n_ in FF_CHUNKS:
            FF_BEFORE.append(FF_BEFORE[-1] + n_)

        def ffn_sp(sp):
            for c, n in enumerate(FF_CHUNKS):
                with sp.Fori(0, n) as j:
                    for i, w in enumerate((w_gate[0], w_up[0])):
                        load_weights(sp, ph[f"up{c}"], j, i, w_cols(w, (j + FF_BEFORE[c]) * P))
                with sp.Fori(0, KT // 2) as it:
                    for i in range(2):
                        rows_ = w_down[0][FF_BEFORE[c] * P:FF_BEFORE[c + 1] * P, :]
                        load_weights(sp, ph[f"down{c}"], it, i, w_cols(rows_, (it * 2 + i) * P, n))

        def ffn_pool(pool):
            for c, n in enumerate(FF_CHUNKS):
                with pool.Fori(0, n) as j:
                    split_weights(pool, ph[f"up{c}"], j, 0)
                    split_weights(pool, ph[f"up{c}"], j, 1)
                with pool.Fori(0, KT // 2) as it:
                    split_weights(pool, ph[f"down{c}"], it, 0, n)
                    split_weights(pool, ph[f"down{c}"], it, 1, n)

        def ffn_pe(pe):
            for c, n in enumerate(FF_CHUNKS):
                b = FF_BEFORE[c]

                def up(j):
                    for half in range(2):
                        for k in range(KT):
                            free = (ff["silu"], (j + b) * 2 + (half - 1))
                            if isinstance(j, int) and j == 0:
                                wait(pe, ff["added"], 16 * c)
                            dense_k(pe, ph[f"up{c}"], j, 0, half, k, KT, D0 + half, act_in, free)
                    for half in range(2):
                        for k in range(KT):
                            dense_k(pe, ph[f"up{c}"], j, 1, half, k, KT, Y0 + half, act_in,
                                    (ff["mult"], (j + b) * 2 + (half - 1)))

                if c:
                    up(0)
                else:
                    for k in range(KT - 2):
                        pe.wait_ge(n_low, k + 1)
                        for i in range(2):
                            for half in range(2):
                                dense_k(pe, ph["up0"], 0, i, half, k, KT, OB[i][half], act_in)
                    for i in range(2):
                        for k in range(KT - 2, KT):
                            if i == 0:
                                pe.wait_ge(n_low, k + 1)
                            for half in range(2):
                                dense_k(pe, ph["up0"], 0, i, half, k, KT, OB[i][half], act_in)
                with pe.Fori(1, n) as j:
                    up(j)

                def down(it):
                    for i in range(2):
                        for half in range(2):
                            for k in range(n):
                                if isinstance(it, int) and i == 0 and half == 0:
                                    pe.wait_ge(ff["low"], (b + k + 1) * 2)
                                m = 16 * c + it * 4
                                free = (ff["added"], it * 4 + (16 * c + half + 2 * i - 3)) if not (isinstance(it, int) and it == 0) \
                                    else (ff["mult"], (b + n) * 2)
                                dense_k(pe, ph[f"down{c}"], it, i, half, k, n, OB[i][half], v_region, free)

                down(0)
                with pe.Fori(1, KT // 2) as it:
                    down(it)

        def ffn_act(act):
            def up(b, c, j):
                for half in range(2):
                    hs = slice(half * HALF, (half + 1) * HALF)
                    m = (j + b) * 2 + half
                    act.wait_ge(projected, done(ph[f"up{c}"], j, 0, half))
                    wait(act, ff["mult"], m - 1)
                    nc.scalar.activation(tmp[0][:, hs], bank[D0 + half][:, :], ACT.Silu).then_inc(ff["silu"], 1)
                if c and isinstance(j, int) and j == 0:
                    act.wait_ge(projected, done(ph[f"down{c - 1}"], KT // 2 - 1, 1, 1))
                for half in range(2):
                    hs = slice(half * HALF, (half + 1) * HALF)
                    m = (j + b) * 2 + half
                    act.wait_ge(ff["mult"], m + 1)
                    nc.scalar.activation(v_region[0][:, ds(j, 1), hs].rearrange("p a t -> p (a t)"), tmp[1][:, hs],
                                         ACT.Copy).then_inc(ff["high"], 1)

            for c, n in enumerate(FF_CHUNKS):
                up(FF_BEFORE[c], c, 0)
                with act.Fori(1, n) as j:
                    up(FF_BEFORE[c], c, j)
            final_square_act(act, 0)
            with act.Fori(1, KT // 2) as it:
                final_square_act(act, it)

        def ffn_vec(dve):
            v = nc.vector

            def up(b, c, j):
                for half in range(2):
                    hs = slice(half * HALF, (half + 1) * HALF)
                    m = (j + b) * 2 + half
                    dve.wait_ge(ff["silu"], m + 1)
                    dve.wait_ge(projected, done(ph[f"up{c}"], j, 1, half))
                    wait(dve, ff["high"], m - 1)
                    v.tensor_tensor(tmp[1][:, hs], tmp[0][:, hs], bank[Y0 + half][:, :], ALU.mult).then_inc(ff["mult"], 1)
                for half in range(2):
                    hs = slice(half * HALF, (half + 1) * HALF)
                    m = (j + b) * 2 + half
                    dve.wait_ge(ff["high"], m + 1)
                    v.tensor_tensor(v_region[1][:, ds(j, 1), hs].rearrange("p a t -> p (a t)"), tmp[1][:, hs],
                                    v_region[0][:, ds(j, 1), hs].rearrange("p a t -> p (a t)").bitcast(F32),
                                    ALU.subtract).then_inc(ff["low"], 1)
                dve.drain()

            def down(c, it):
                for i in range(2):
                    for half in range(2):
                        dve.wait_ge(projected, done(ph[f"down{c}"], it, i, half))
                        hf = h_t[:, ds(it * 2 + i, 1), half * HALF:(half + 1) * HALF].rearrange("p a t -> p (a t)")
                        v.tensor_tensor(hf, hf, bank[OB[i][half]][:, :], ALU.add).then_inc(ff["added"], 1)
                        if c == LAST:
                            final_sum_vec(dve, it, i, half)

            for c, n in enumerate(FF_CHUNKS):
                up(FF_BEFORE[c], c, 0)
                with dve.Fori(1, n) as j:
                    up(FF_BEFORE[c], c, j)
                if c == LAST:
                    v.memset(f_sum[:, :], 0.0)
                    dve.drain()
                with dve.Fori(0, KT // 2) as it:
                    down(c, it)

        assert FF_CHUNKS[-1] <= KT - 2
        f_sum = at("f_sum", [P, S], F32, work + 57344)
        f_now = at("f_now", [P, S], F32, work + 61440)
        f_rms = at("f_rms", [P, KT], F32, work + 28672)
        NOUT = 6
        out_rows = [at(f"out_rows{i}", [P, D], F32, work + 32768 + 4096 * i) for i in range(NOUT)]
        f_turned_half = [sem("f_turned0"), sem("f_turned1")]
        f_sq, f_summed, f_ones, f_rstd, f_scaled = (
            sem("f_sq"), sem("f_summed"), sem("f_ones"), sem("f_rstd"), sem("f_scaled"))
        f_scaled_act, f_weighted = sem("f_scaled_act"), sem("f_weighted")
        f_stored = [sem(f"f_stored{i}") for i in range(NOUT)]
        LAST = len(FF_CHUNKS) - 1
        FB = ((D0, D1), (Y0, Y1), (Z0, Z1))

        def final_square_act(act, it):
            for i in range(2):
                for half in range(2):
                    hs = slice(half * HALF, (half + 1) * HALF)
                    act.wait_ge(ff["added"], it * 4 + (16 * LAST + half + 2 * i + 1))
                    wait(act, f_summed, it * 4 + (half + 2 * i - 1))
                    nc.scalar.activation(f_now[:, hs], h_t[:, ds(it * 2 + i, 1), hs].rearrange("p a t -> p (a t)"),
                                         ACT.Square).then_inc(f_sq, 1)

        def final_sum_vec(dve, it, i, half):
            hs = slice(half * HALF, (half + 1) * HALF)
            dve.wait_ge(f_sq, it * 4 + (half + 2 * i + 1))
            nc.vector.tensor_tensor(f_sum[:, hs], f_sum[:, hs], f_now[:, hs], ALU.add).then_inc(f_summed, 1)
            hf = h_t[:, ds(it * 2 + i, 1), hs].rearrange("p a t -> p (a t)")
            nc.vector.tensor_scalar(hf, hf, norm_final_c[:, ds(it * 2 + i, 1)], None, ALU.mult).then_inc(f_weighted, 1)

        def final_pe(pe):
            def turn(c, half):
                if c >= len(FB):
                    pe.wait_ge((f_scaled_act, f_scaled)[half], c - len(FB) + 1)
                for f in range(4):
                    last = nc.tensor.transpose(bank[FB[c % len(FB)][half]][:, f * P:(f + 1) * P],
                                               h_t[:, 4 * half + f, c * P:(c + 1) * P], ident[:, :])
                last.then_inc(f_turned_half[half], 1)

            pe.wait_ge(f_weighted, 2 * KT - 1)
            for c in range(len(FB)):
                turn(c, 0)
            pe.wait_ge(f_summed, 2 * KT)
            for c in range(KT):
                last = nc.tensor.matmul(bank[X0][:, c:c + 1], f_sum[:, c * P:(c + 1) * P], ones[:, 0:1],
                                        start=True, stop=True)
            last.then_inc(f_ones, 1)
            pe.wait_ge(f_weighted, 2 * KT)
            for c in range(len(FB)):
                turn(c, 1)
            for c in range(len(FB), KT):
                for half in range(2):
                    turn(c, half)

        def final_act(act):
            act.wait_ge(f_ones, 1)
            nc.scalar.activation(f_rms[:, :], bank[X0][:, 0:KT], ACT.Ln, scale=1.0 / D, bias=EPS)
            act.drain()
            nc.scalar.activation(f_rms[:, :], f_rms[:, :], ACT.Exp, scale=-0.5).then_inc(f_rstd, 1)
            act.wait_ge(f_rstd, 1)

            for c in range(KT):
                act.wait_ge(f_turned_half[0], c + 1)
                if c >= NOUT:
                    act.wait_ge(f_stored[c - NOUT], 16)
                nc.scalar.activation(out_rows[c % NOUT][:, 0:HALF], bank[FB[c % len(FB)][0]][:, :], ACT.Copy,
                                     scale=f_rms[:, c:c + 1]).then_inc(f_scaled_act, 1)

        def final_vec(dve):
            dve.wait_ge(f_rstd, 1)
            for c in range(KT):
                dve.wait_ge(f_turned_half[1], c + 1)
                if c >= NOUT:
                    dve.wait_ge(f_stored[c - NOUT], 16)
                nc.vector.tensor_scalar(out_rows[c % NOUT][:, HALF:D], bank[FB[c % len(FB)][1]][:, :],
                                        f_rms[:, c:c + 1], None, ALU.mult).then_inc(f_scaled, 1)

        def final_sp(sp):
            for c in range(KT):
                sp.wait_ge(f_scaled, c + 1)
                sp.wait_ge(f_scaled_act, c + 1)
                sp.dma_start(out[0, c * P:(c + 1) * P, :], out_rows[c % NOUT][:, :]).then_inc(f_stored[c % NOUT], 16)
            for i in range(NOUT):
                sp.wait_ge(f_stored[i], 32 if i + NOUT < KT else 16)

        block = ctx.enter_context(nc.Block())

        @block.sync
        def _(sp):
            setup_sp(sp)
            attention_sp(sp)
            delta_sp(sp)
            gates_sp(sp)
            merge_sp(sp)
            out_sp(sp)
            ffn_sp(sp)
            final_sp(sp)

        @block.gpsimd
        def _(pool):
            pool.sem_inc(weights_split, FREE)
            then = pool_then(pool)
            setup_pool(pool, then)
            for i in range(9):
                split_weights(pool, ph["attn"], 0, i)
            mask_pool(pool, then)
            with pool.Fori(1, NSLOT) as s:
                for i in range(9):
                    split_weights(pool, ph["attn"], s, i)
            with pool.Fori(0, NHB) as h:
                for i in range(4):
                    split_weights(pool, ph["delta"], h, i)
            gates_pool(pool)
            merge_pool(pool)
            with pool.Fori(0, KT // 2) as it:
                for i in range(2):
                    split_weights(pool, ph["out"], it, i)
            ffn_pool(pool)

        @block.tensor
        def _(pe):
            setup_pe(pe)
            attention(pe, dense_att_pe, att_pe, nothing, decay_pe)
            delta_iteration(pe, 0, dense_delta_pe, [nothing] * 5, att_pe, nothing)
            pe.wait_ge(st_copied, 3 * NSLOT)
            pe.wait_ge(scaled, NP_SLOT * NSLOT)
            pe.wait_ge(p_copied, NP_SLOT * NSLOT)
            pe.wait_ge(o_taken, 6 * NSLOT)
            delta_heads(pe, dense_delta_pe, [nothing] * 5, delta_pe)
            delta_end(pe, gate_step_pe, delta_pe, nothing)
            gates_pe(pe)
            merge_pe(pe)
            out_pe(pe)
            norm_pe(pe, 4 * KT // 2)
            ffn_pe(pe)
            final_pe(pe)

        @block.scalar
        def _(act):
            setup_act(act)
            attention(act, dense_att_act, att_act, mix_act_engine, decay_act)
            delta_iteration(act, 0, dense_delta_act, OWN_ACT, att_act, mix_act_engine)
            delta_heads(act, dense_delta_act, OWN_ACT, delta_act)
            delta_end(act, gate_step_act, delta_act, nothing)
            mix_act_engine(act, NSLOT - 1, "end")
            gates_act(act)
            merge_act(act)
            out_act(act)
            norm_act(act, 1)
            norm_split_act(act)
            ffn_act(act)
            final_act(act)

        @block.vector
        def _(dve):
            setup_vec(dve)
            dve.wait_ge(consts, 3)
            attention(dve, nothing, att_vec, mix_vec_engine, decay_vec)
            dve.wait_ge(projected, done(ph["attn"], NSLOT - 1, 8, 1))
            for i in range(2):
                nc.vector.memset(conv_in[i][:, 0:3], 0.0)
            dve.wait_ge(conv_loaded, 64)
            dve.wait_ge(consts, 4)
            delta_iteration(dve, 0, nothing, OWN_VEC, att_vec, mix_vec_engine)
            delta_heads(dve, nothing, OWN_VEC, delta_vec)
            delta_end(dve, nothing, delta_vec, mix_vec_engine)
            gates_vec(dve)
            merge_vec(dve)
            out_vec(dve)
            norm_split_vec(dve)
            ffn_vec(dve)
            final_vec(dve)


INS = ["x", "norm_mix", "w_in", "conv_w", "a_log", "dt_bias", "dn_norm", "w_proj_attn", "w_proj_delta",
       "w_out", "norm_ffn", "w_gate", "w_up", "w_down", "norm_final"]


def kernel(**inputs):
    import concourse.bacc as bacc
    from concourse.bass_utils import run_bass_kernel_spmd

    nc = bacc.Bacc("TRN2", target_bir_lowering=False, num_devices=1)
    arrays, args = {}, []
    for name in INS:
        a = np.ascontiguousarray(inputs[name])
        arrays[f"in_{name}"] = a
        args.append(nc.dram_tensor(f"in_{name}", a.shape, mybir.dt.from_np(a.dtype), kind="ExternalInput").ap())
    out = nc.dram_tensor("out", (1, S, D), F32, kind="ExternalOutput").ap()
    build(nc, *args, out)
    r = run_bass_kernel_spmd(nc, [arrays], core_ids=[0])
    return r.results[0]["out"]
```
